# Optimizing a Trainium2 kernel written in Bass

```python
import jax
import jax.numpy as jnp
from jax import lax
import numpy as np
import jax, jax.numpy as jnp

D_MODEL = 1024
BATCH = 1
SEQ = 256
DEPTH = 1

RW_HEAD_DIM = 64
RW_WIDTH = D_MODEL // 2
RW_HEADS = RW_WIDTH // RW_HEAD_DIM
RW_DECAY_RANK = 64
RW_ICLR_RANK = 64
RW_GATE_RANK = 128
RW_GN_EPS = 64e-5
RET_QK_DIM = 64
RET_QK_WIDTH = D_MODEL // 2
RET_HEADS = RET_QK_WIDTH // RET_QK_DIM
RET_V_DIM = 2 * RET_QK_DIM
RET_V_WIDTH = RET_HEADS * RET_V_DIM
RET_CHUNK = 128
ROPE_BASE = 10000.0
RET_GN_EPS = 1e-5
D_FF = 2816
CONV_WIDTH = 3
RMS_EPS = 1e-6

RW_SIZES = (RW_WIDTH, RW_WIDTH, RW_WIDTH, RW_DECAY_RANK, RW_ICLR_RANK, RW_GATE_RANK)
RET_SIZES = (RET_QK_WIDTH, RET_QK_WIDTH, RET_V_WIDTH, RET_V_WIDTH)
RW_COLS = sum(RW_SIZES)
RET_COLS = sum(RET_SIZES)
IN_SIZES = (RW_COLS, RET_COLS, D_MODEL, D_MODEL)
IN_COLS = sum(IN_SIZES)


def _split(z, sizes):
    return jnp.split(z, [int(s) for s in np.cumsum(sizes)[:-1]], axis=-1)

def rms_norm(x, g):
    xf = x.astype(jnp.float32)
    y = xf * lax.rsqrt(jnp.mean(xf * xf, axis=-1, keepdims=True) + RMS_EPS)
    return (y * g.astype(jnp.float32)).astype(x.dtype)

def group_norm_heads(z, eps):
    mu = jnp.mean(z, axis=-1, keepdims=True)
    var = jnp.mean(jnp.square(z - mu), axis=-1, keepdims=True)
    return (z - mu) * lax.rsqrt(var + eps)

def token_shift(p):
    return jnp.pad(p, ((0, 0), (1, 0), (0, 0)))[:, :-1]

def rwkv7_mixer(p, mu, w0, w2, a0, a2, g2, k_k, k_a, r_k, lnx_w, lnx_b):
    B, T, _ = p.shape
    H, N = RW_HEADS, RW_HEAD_DIM
    p = p.astype(jnp.float32)
    p = p + (token_shift(p) - p) * mu.astype(jnp.float32)
    r, k, v, wd, ad, gd = _split(p, RW_SIZES)
    w = -jax.nn.softplus(-(w0 + jnp.tanh(wd) @ w2)) - 0.5
    decay = jnp.exp(-jnp.exp(w))
    a = jax.nn.sigmoid(a0 + ad @ a2)
    g = jax.nn.sigmoid(gd) @ g2
    heads = lambda z: z.reshape(B, T, H, N).astype(jnp.float32)
    kk = heads(k * k_k)
    kk = kk / jnp.maximum(jnp.sqrt(jnp.sum(kk * kk, axis=-1, keepdims=True)), 1e-12)
    k = k * (1.0 + (a - 1.0) * k_a)
    r, k, v, decay, a = heads(r), heads(k), heads(v), heads(decay), heads(a)

    def step(S, inp):
        r_t, k_t, v_t, w_t, kk_t, a_t = inp
        sa = jnp.einsum('bhvk,bhk->bhv', S, -kk_t)
        S = (S * w_t[:, :, None, :]
             + sa[..., None] * (kk_t * a_t)[:, :, None, :]
             + v_t[..., None] * k_t[:, :, None, :])
        y = jnp.einsum('bhvk,bhk->bhv', S, r_t)
        return S, y

    xs = tuple(jnp.moveaxis(z, 1, 0) for z in (r, k, v, decay, kk, a))
    S0 = jnp.zeros((B, H, N, N), jnp.float32)
    _, y = lax.scan(step, S0, xs)
    y = jnp.moveaxis(y, 0, 1)
    y = group_norm_heads(y, RW_GN_EPS) * lnx_w.reshape(H, N) + lnx_b.reshape(H, N)
    bonus = jnp.sum(r * k * r_k.reshape(H, N), axis=-1, keepdims=True) * v
    return (y + bonus).reshape(B, T, RW_WIDTH) * g

def rotary(z, pos):
    half = z.shape[-1] // 2
    inv = ROPE_BASE ** (-jnp.arange(half, dtype=jnp.float32) / half)
    ang = pos.astype(jnp.float32)[..., None] * inv
    cos = jnp.cos(ang)[:, :, None, :]
    sin = jnp.sin(ang)[:, :, None, :]
    z1, z2 = z[..., :half], z[..., half:]
    return jnp.concatenate([z1 * cos - z2 * sin, z1 * sin + z2 * cos], axis=-1)

def retention_mixer(p, positions):
    B, T, _ = p.shape
    H, dk, dv, C = RET_HEADS, RET_QK_DIM, RET_V_DIM, RET_CHUNK
    q, k, v, g = _split(p.astype(jnp.float32), RET_SIZES)
    q = rotary(q.reshape(B, T, H, dk), positions)
    k = rotary(k.reshape(B, T, H, dk), positions) * (dk ** -0.5)
    v = v.reshape(B, T, H, dv)
    log_gamma = jnp.log1p(-jnp.exp2(-5.0 - jnp.arange(H, dtype=jnp.float32)))
    idx = jnp.arange(C, dtype=jnp.float32)
    rel = idx[:, None] - idx[None, :]
    decay_mask = jnp.where(rel[None] >= 0,
                           jnp.exp(jnp.maximum(rel, 0.0)[None] * log_gamma[:, None, None]), 0.0)
    q_decay = jnp.exp((idx + 1.0)[:, None] * log_gamma[None, :])[None, :, :, None]
    k_decay = jnp.exp((C - 1.0 - idx)[:, None] * log_gamma[None, :])[None, :, :, None]
    chunk_decay = jnp.exp(C * log_gamma)[None, :, None, None]
    n_chunks = T // C
    chunks = lambda z: jnp.moveaxis(z.reshape(B, n_chunks, C, H, z.shape[-1]), 1, 0)

    def step(R, inp):
        qc, kc, vc = inp
        s = jnp.einsum('bihd,bjhd->bhij', qc, kc) * decay_mask
        inner = jnp.einsum('bhij,bjhe->bihe', s, vc)
        cross = jnp.einsum('bihd,bhde->bihe', qc * q_decay, R)
        R = R * chunk_decay + jnp.einsum('bjhd,bjhe->bhde', kc * k_decay, vc)
        return R, inner + cross

    R0 = jnp.zeros((B, H, dk, dv), jnp.float32)
    _, o = lax.scan(step, R0, (chunks(q), chunks(k), chunks(v)))
    o = jnp.moveaxis(o, 0, 1).reshape(B, T, H, dv)
    o = group_norm_heads(o, RET_GN_EPS).reshape(B, T, RET_V_WIDTH)
    return jax.nn.silu(g) * o

def conv_ffn(h, w_up, conv_w, conv_b, w_down):
    u = h @ w_up
    T = u.shape[1]
    up = jnp.pad(u, ((0, 0), (CONV_WIDTH - 1, 0), (0, 0)))
    u = sum(up[:, i:i + T] * conv_w[i] for i in range(CONV_WIDTH)) + conv_b
    gate, val = jnp.split(u, 2, axis=-1)
    return (jax.nn.gelu(gate, approximate=True) * val) @ w_down

def first_inputs(seed: int = 0) -> dict:
    key = jax.random.key(seed)
    ks = jax.random.split(key, 26)
    f32 = jnp.float32
    L = DEPTH
    nrm = lambda k, shape, s: s * jax.random.normal(k, shape, f32)
    x = jax.random.normal(ks[0], (BATCH, SEQ, D_MODEL), f32)
    offsets = jax.random.randint(ks[1], (BATCH, 1), 0, 4096, dtype=jnp.int32)
    positions = offsets + jnp.arange(SEQ, dtype=jnp.int32)[None, :]
    return {
        "x": x,
        "positions": positions,
        "norm_mix_pre": 1.0 + nrm(ks[2], (L, D_MODEL), 0.1),
        "norm_mix_post": 1.0 + nrm(ks[3], (L, D_MODEL), 0.1),
        "norm_ffn_pre": 1.0 + nrm(ks[4], (L, D_MODEL), 0.1),
        "norm_ffn_post": 1.0 + nrm(ks[5], (L, D_MODEL), 0.1),
        "w_in": nrm(ks[6], (L, D_MODEL, IN_COLS), D_MODEL ** -0.5),
        "rw_mu": jax.random.uniform(ks[7], (L, RW_COLS), f32, 0.0, 1.0),
        "rw_w0": jax.random.uniform(ks[8], (L, RW_WIDTH), f32, -6.0, 1.0),
        "rw_w2": nrm(ks[9], (L, RW_DECAY_RANK, RW_WIDTH), 0.1 * RW_DECAY_RANK ** -0.5),
        "rw_a0": nrm(ks[10], (L, RW_WIDTH), 0.1),
        "rw_a2": nrm(ks[11], (L, RW_ICLR_RANK, RW_WIDTH), 0.5 * RW_ICLR_RANK ** -0.5),
        "rw_g2": nrm(ks[12], (L, RW_GATE_RANK, RW_WIDTH), RW_GATE_RANK ** -0.5),
        "rw_k_k": 0.85 + nrm(ks[13], (L, RW_WIDTH), 0.1),
        "rw_k_a": 1.0 + nrm(ks[14], (L, RW_WIDTH), 0.1),
        "rw_r_k": nrm(ks[15], (L, RW_WIDTH), 0.1),
        "rw_lnx_w": 1.0 + nrm(ks[16], (L, RW_WIDTH), 0.1),
        "rw_lnx_b": nrm(ks[17], (L, RW_WIDTH), 0.01),
        "w_branch_rw": nrm(ks[18], (L, RW_WIDTH, D_MODEL), RW_WIDTH ** -0.5),
        "w_branch_ret": nrm(ks[19], (L, RET_V_WIDTH, D_MODEL), RET_V_WIDTH ** -0.5),
        "w_out": nrm(ks[20], (L, D_MODEL, D_MODEL), D_MODEL ** -0.5),
        "ffn_w_up": nrm(ks[21], (L, D_MODEL, 2 * D_FF), D_MODEL ** -0.5),
        "ffn_conv_w": nrm(ks[22], (L, CONV_WIDTH, 2 * D_FF), CONV_WIDTH ** -0.5),
        "ffn_conv_b": nrm(ks[23], (L, 2 * D_FF), 0.01),
        "ffn_w_down": nrm(ks[24], (L, D_FF, D_MODEL), D_FF ** -0.5),
    }

def first_block(x, positions, norm_mix_pre, norm_mix_post, norm_ffn_pre, norm_ffn_post, w_in,
              rw_mu, rw_w0, rw_w2, rw_a0, rw_a2, rw_g2, rw_k_k, rw_k_a, rw_r_k, rw_lnx_w, rw_lnx_b,
              w_branch_rw, w_branch_ret, w_out, ffn_w_up, ffn_conv_w, ffn_conv_b, ffn_w_down):
    h = x
    for l in range(DEPTH):
        hn = rms_norm(h, norm_mix_pre[l])
        p = hn @ w_in[l]
        p_rw, p_ret, g_rw, g_ret = _split(p, IN_SIZES)
        y_rw = rwkv7_mixer(p_rw, rw_mu[l], rw_w0[l], rw_w2[l], rw_a0[l], rw_a2[l], rw_g2[l],
                           rw_k_k[l], rw_k_a[l], rw_r_k[l], rw_lnx_w[l], rw_lnx_b[l])
        y_ret = retention_mixer(p_ret, positions)
        merged = (jax.nn.sigmoid(g_rw.astype(jnp.float32)) * (y_rw @ w_branch_rw[l])
                  + jax.nn.sigmoid(g_ret.astype(jnp.float32)) * (y_ret @ w_branch_ret[l]))
        h = h + rms_norm(merged @ w_out[l], norm_mix_post[l])
        f = conv_ffn(rms_norm(h, norm_ffn_pre[l]), ffn_w_up[l], ffn_conv_w[l], ffn_conv_b[l], ffn_w_down[l])
        h = h + rms_norm(f, norm_ffn_post[l])
    return h.astype(x.dtype)


DEPTH_2 = 2

N_A_LAYERS = DEPTH_2 // 2
N_B_LAYERS = DEPTH_2 - N_A_LAYERS
SSM_EXPAND = 2
D_INNER = SSM_EXPAND * D_MODEL
SSM_HEAD_DIM = 64
SSM_HEADS = D_INNER // SSM_HEAD_DIM
SSM_GROUPS = 4
SSM_HPG = SSM_HEADS // SSM_GROUPS
D_STATE = 128
CONV_WIDTH_2 = 4
CONV_CH = D_INNER + 2 * SSM_GROUPS * D_STATE
SSM_IN = D_INNER + CONV_CH + SSM_HEADS
CHUNK = 128
ATT_HEADS = 16
KV_HEADS = 4
HEAD_DIM = 64
Q_PER_KV = ATT_HEADS // KV_HEADS
ATT_WIDTH = ATT_HEADS * HEAD_DIM
KV_WIDTH = KV_HEADS * HEAD_DIM
WINDOW = 128
BLOCK = WINDOW
ROPE_THETA = 10000.0
PLE_DIM = 256
EPS = 1e-6


def rms_norm_2(x, w):
    xf = x.astype(jnp.float32)
    y = xf * lax.rsqrt(jnp.mean(xf * xf, axis=-1, keepdims=True) + EPS)
    return (y * w.astype(jnp.float32)).astype(x.dtype)

def rope(x, positions):
    half = HEAD_DIM // 2
    inv_freq = ROPE_THETA ** (-(jnp.arange(half, dtype=jnp.float32) * 2.0 / HEAD_DIM))
    ang = positions.astype(jnp.float32)[..., None] * inv_freq
    cos = jnp.cos(ang)[:, :, None, :]
    sin = jnp.sin(ang)[:, :, None, :]
    xf = x.astype(jnp.float32)
    x1, x2 = xf[..., :half], xf[..., half:]
    return jnp.concatenate([x1 * cos - x2 * sin, x2 * cos + x1 * sin], axis=-1).astype(x.dtype)

def ssd_chunked(xs, dt, a, bm, cm):
    b, s = xs.shape[:2]
    nc = s // CHUNK
    x = xs.astype(jnp.float32).reshape(b, nc, CHUNK, SSM_GROUPS, SSM_HPG, SSM_HEAD_DIM)
    dt = dt.reshape(b, nc, CHUNK, SSM_GROUPS, SSM_HPG)
    bm = bm.astype(jnp.float32).reshape(b, nc, CHUNK, SSM_GROUPS, D_STATE)
    cm = cm.astype(jnp.float32).reshape(b, nc, CHUNK, SSM_GROUPS, D_STATE)
    a_cum = jnp.cumsum(dt * a.reshape(SSM_GROUPS, SSM_HPG), axis=2)
    xdt = x * dt[..., None]
    seg = a_cum[:, :, :, None] - a_cum[:, :, None, :]
    causal = jnp.tril(jnp.ones((CHUNK, CHUNK), bool))[None, None, :, :, None, None]
    decay = jnp.exp(jnp.where(causal, seg, -jnp.inf))
    cb = jnp.einsum('bcign,bcjgn->bcijg', cm, bm)
    y_diag = jnp.einsum('bcijg,bcijgr,bcjgrp->bcigrp', cb, decay, xdt)
    decay_to_end = jnp.exp(a_cum[:, :, -1:] - a_cum)
    states = jnp.einsum('bcjgn,bcjgr,bcjgrp->bcgrpn', bm, decay_to_end, xdt)
    chunk_decay = jnp.exp(a_cum[:, :, -1])

    def step(carry, inp):
        st, dec = inp
        return carry * dec[..., None, None] + st, carry

    init = jnp.zeros((b, SSM_GROUPS, SSM_HPG, SSM_HEAD_DIM, D_STATE), jnp.float32)
    _, prev = lax.scan(step, init, (jnp.moveaxis(states, 1, 0), jnp.moveaxis(chunk_decay, 1, 0)))
    prev = jnp.moveaxis(prev, 0, 1)
    y_off = jnp.einsum('bcign,bcgrpn,bcigr->bcigrp', cm, prev, jnp.exp(a_cum))
    return (y_diag + y_off).reshape(b, s, SSM_HEADS, SSM_HEAD_DIM)

def mamba2_mixer(h, norm_w, in_w, conv_w, conv_b, dt_bias, a_log, d_skip, gnorm_w, out_w):
    b, s, _ = h.shape
    u = rms_norm_2(h, norm_w)
    zxbcdt = u @ in_w
    z, xbc, dt = jnp.split(zxbcdt, [D_INNER, D_INNER + CONV_CH], axis=-1)
    xbc = lax.conv_general_dilated(xbc, conv_w[:, None, :], window_strides=(1,),
                                   padding=[(CONV_WIDTH_2 - 1, 0)],
                                   dimension_numbers=('NWC', 'WIO', 'NWC'),
                                   feature_group_count=CONV_CH) + conv_b
    xbc = jax.nn.silu(xbc)
    xs, bm, cm = jnp.split(xbc, [D_INNER, D_INNER + SSM_GROUPS * D_STATE], axis=-1)
    xs = xs.reshape(b, s, SSM_HEADS, SSM_HEAD_DIM)
    bm = bm.reshape(b, s, SSM_GROUPS, D_STATE)
    cm = cm.reshape(b, s, SSM_GROUPS, D_STATE)
    dt = jax.nn.softplus(dt.astype(jnp.float32) + dt_bias.astype(jnp.float32))
    a = -jnp.exp(a_log.astype(jnp.float32))
    y = ssd_chunked(xs, dt, a, bm, cm)
    y = y + d_skip.astype(jnp.float32)[:, None] * xs.astype(jnp.float32)
    y = y.reshape(b, s, D_INNER) * jax.nn.silu(z.astype(jnp.float32))
    yg = y.reshape(b, s, SSM_GROUPS, D_INNER // SSM_GROUPS)
    yg = yg * lax.rsqrt(jnp.mean(yg * yg, axis=-1, keepdims=True) + EPS)
    y = yg.reshape(b, s, D_INNER) * gnorm_w.astype(jnp.float32)
    return y.astype(h.dtype) @ out_w

def shared_kv(h, positions, kv_norm_w, kv_w, k_norm_w):
    b, s, _ = h.shape
    u = rms_norm_2(h, kv_norm_w)
    k, v = jnp.split(u @ kv_w, 2, axis=-1)
    k = k.reshape(b, s, KV_HEADS, HEAD_DIM)
    v = v.reshape(b, s, KV_HEADS, HEAD_DIM)
    k = rope(rms_norm_2(k, k_norm_w), positions)
    return k, v

def swa_sink_attention(q, k, v, sinks):
    b, s = q.shape[:2]
    nb = s // BLOCK
    qb = q.reshape(b, nb, BLOCK, KV_HEADS, Q_PER_KV, HEAD_DIM)

    def with_prev(t):
        t = t.reshape(b, nb, BLOCK, KV_HEADS, HEAD_DIM)
        prev = jnp.pad(t, ((0, 0), (1, 0), (0, 0), (0, 0), (0, 0)))[:, :-1]
        return jnp.concatenate([prev, t], axis=2)

    kk, vv = with_prev(k), with_prev(v)
    scores = jnp.einsum('bnqhgd,bnkhd->bnhgqk', qb, kk).astype(jnp.float32) * (HEAD_DIM ** -0.5)
    blk = jnp.arange(nb)[:, None, None] * BLOCK
    q_pos = blk + jnp.arange(BLOCK)[None, :, None]
    k_pos = blk - BLOCK + jnp.arange(2 * BLOCK)[None, None, :]
    valid = (k_pos <= q_pos) & (q_pos - k_pos < WINDOW) & (k_pos >= 0)
    scores = jnp.where(valid[None, :, None, None], scores, -jnp.inf)
    sink = sinks.astype(jnp.float32).reshape(KV_HEADS, Q_PER_KV)[None, None, :, :, None, None]
    m = jnp.maximum(jnp.max(scores, axis=-1, keepdims=True), sink)
    e = jnp.exp(scores - m)
    probs = e / (jnp.sum(e, axis=-1, keepdims=True) + jnp.exp(sink - m))
    out = jnp.einsum('bnhgqk,bnkhd->bnqhgd', probs.astype(v.dtype), vv)
    return out.reshape(b, s, ATT_WIDTH)

def swa_layer(h, k, v, positions, norm_w, in_w, q_norm_w, sinks, out_w):
    b, s, _ = h.shape
    u = rms_norm_2(h, norm_w)
    q, gate = jnp.split(u @ in_w, 2, axis=-1)
    q = rope(rms_norm_2(q.reshape(b, s, ATT_HEADS, HEAD_DIM), q_norm_w), positions)
    o = swa_sink_attention(q, k, v, sinks)
    return (o * jax.nn.silu(gate)) @ out_w

def per_layer_embedding(h, p_i, norm_w, gate_w, proj_w):
    g = jax.nn.sigmoid((rms_norm_2(h, norm_w) @ gate_w).astype(jnp.float32))
    return (g * (p_i @ proj_w).astype(jnp.float32)).astype(h.dtype)

def second_inputs(seed: int = 0) -> dict:
    key = jax.random.key(seed)
    ks = jax.random.split(key, 24)
    f32 = jnp.float32

    def nrm(k, shape, scale):
        return jax.random.normal(k, shape, f32) * scale

    dt0 = jnp.exp(jax.random.uniform(ks[7], (N_A_LAYERS, SSM_HEADS), f32, np.log(1e-3), np.log(1e-1)))
    offs = jax.random.randint(ks[3], (BATCH, 1), 0, 1024, jnp.int32)
    return {
        'x': nrm(ks[0], (BATCH, SEQ, D_MODEL), 1.0),
        'p': nrm(ks[1], (DEPTH_2, BATCH, SEQ, PLE_DIM), 1.0),
        'positions': (offs + jnp.arange(SEQ, dtype=jnp.int32)[None, :]).astype(jnp.int32),
        'ssm_norm_w': 1.0 + nrm(ks[2], (N_A_LAYERS, D_MODEL), 0.05),
        'ssm_in_w': nrm(ks[4], (N_A_LAYERS, D_MODEL, SSM_IN), D_MODEL ** -0.5),
        'ssm_conv_w': nrm(ks[5], (N_A_LAYERS, CONV_WIDTH_2, CONV_CH), CONV_WIDTH_2 ** -0.5),
        'ssm_conv_b': nrm(ks[6], (N_A_LAYERS, CONV_CH), 0.02),
        'ssm_dt_bias': dt0 + jnp.log(-jnp.expm1(-dt0)),
        'ssm_a_log': jnp.log(jax.random.uniform(ks[8], (N_A_LAYERS, SSM_HEADS), f32, 1.0, 16.0)),
        'ssm_d': 1.0 + nrm(ks[9], (N_A_LAYERS, SSM_HEADS), 0.1),
        'ssm_gnorm_w': 1.0 + nrm(ks[10], (N_A_LAYERS, D_INNER), 0.05),
        'ssm_out_w': nrm(ks[11], (N_A_LAYERS, D_INNER, D_MODEL), D_INNER ** -0.5),
        'kv_norm_w': 1.0 + nrm(ks[12], (D_MODEL,), 0.05),
        'kv_w': nrm(ks[13], (D_MODEL, 2 * KV_WIDTH), D_MODEL ** -0.5),
        'k_norm_w': 1.0 + nrm(ks[14], (HEAD_DIM,), 0.05),
        'attn_norm_w': 1.0 + nrm(ks[15], (N_B_LAYERS, D_MODEL), 0.05),
        'attn_in_w': nrm(ks[16], (N_B_LAYERS, D_MODEL, 2 * ATT_WIDTH), D_MODEL ** -0.5),
        'q_norm_w': 1.0 + nrm(ks[17], (N_B_LAYERS, HEAD_DIM), 0.05),
        'attn_sinks': nrm(ks[18], (N_B_LAYERS, ATT_HEADS), 0.5),
        'attn_out_w': nrm(ks[19], (N_B_LAYERS, ATT_WIDTH, D_MODEL), ATT_WIDTH ** -0.5),
        'ple_norm_w': 1.0 + nrm(ks[20], (DEPTH_2, D_MODEL), 0.05),
        'ple_gate_w': nrm(ks[21], (DEPTH_2, D_MODEL, D_MODEL), D_MODEL ** -0.5),
        'ple_proj_w': nrm(ks[22], (DEPTH_2, PLE_DIM, D_MODEL), 0.5 * PLE_DIM ** -0.5),
    }

def second_block(x, p, positions, ssm_norm_w, ssm_in_w, ssm_conv_w, ssm_conv_b, ssm_dt_bias, ssm_a_log,
              ssm_d, ssm_gnorm_w, ssm_out_w, kv_norm_w, kv_w, k_norm_w, attn_norm_w, attn_in_w,
              q_norm_w, attn_sinks, attn_out_w, ple_norm_w, ple_gate_w, ple_proj_w):
    h = x
    k_sh = None
    v_sh = None
    for i in range(DEPTH_2):
        if i < N_A_LAYERS:
            h = h + mamba2_mixer(h, ssm_norm_w[i], ssm_in_w[i], ssm_conv_w[i], ssm_conv_b[i],
                                 ssm_dt_bias[i], ssm_a_log[i], ssm_d[i], ssm_gnorm_w[i], ssm_out_w[i])
        else:
            if i == N_A_LAYERS:
                k_sh, v_sh = shared_kv(h, positions, kv_norm_w, kv_w, k_norm_w)
            j = i - N_A_LAYERS
            h = h + swa_layer(h, k_sh, v_sh, positions, attn_norm_w[j], attn_in_w[j], q_norm_w[j],
                              attn_sinks[j], attn_out_w[j])
        h = h + per_layer_embedding(h, p[i], ple_norm_w[i], ple_gate_w[i], ple_proj_w[i])
    return h


def setup_inputs(seed=0):
    out = dict(first_inputs(seed))
    for name, value in second_inputs(seed + 1).items():
        if name != "x":
            out[name + "_2"] = value
    return out


def reference(
    x, positions, norm_mix_pre, norm_mix_post, norm_ffn_pre, norm_ffn_post, w_in, rw_mu, rw_w0,
    rw_w2, rw_a0, rw_a2, rw_g2, rw_k_k, rw_k_a, rw_r_k, rw_lnx_w, rw_lnx_b, w_branch_rw,
    w_branch_ret, w_out, ffn_w_up, ffn_conv_w, ffn_conv_b, ffn_w_down, p_2, positions_2,
    ssm_norm_w_2, ssm_in_w_2, ssm_conv_w_2, ssm_conv_b_2, ssm_dt_bias_2, ssm_a_log_2, ssm_d_2,
    ssm_gnorm_w_2, ssm_out_w_2, kv_norm_w_2, kv_w_2, k_norm_w_2, attn_norm_w_2, attn_in_w_2,
    q_norm_w_2, attn_sinks_2, attn_out_w_2, ple_norm_w_2, ple_gate_w_2, ple_proj_w_2,
):
    x = first_block(
        x, positions, norm_mix_pre, norm_mix_post, norm_ffn_pre, norm_ffn_post, w_in, rw_mu,
        rw_w0, rw_w2, rw_a0, rw_a2, rw_g2, rw_k_k, rw_k_a, rw_r_k, rw_lnx_w, rw_lnx_b,
        w_branch_rw, w_branch_ret, w_out, ffn_w_up, ffn_conv_w, ffn_conv_b, ffn_w_down,
    )
    return second_block(
        x, p_2, positions_2, ssm_norm_w_2, ssm_in_w_2, ssm_conv_w_2, ssm_conv_b_2,
        ssm_dt_bias_2, ssm_a_log_2, ssm_d_2, ssm_gnorm_w_2, ssm_out_w_2, kv_norm_w_2, kv_w_2,
        k_norm_w_2, attn_norm_w_2, attn_in_w_2, q_norm_w_2, attn_sinks_2, attn_out_w_2,
        ple_norm_w_2, ple_gate_w_2, ple_proj_w_2,
    )


_drawn_inputs = setup_inputs


def setup_inputs(seed=0):
    import zlib

    import numpy as np

    out = dict(_drawn_inputs(seed))
    spreads = {}
    factors = {'rw_w2': 8.0,
     'rw_lnx_b': 8.0,
     'ffn_conv_b': 6.115,
     'ssm_conv_b_2': 3.968,
     'kv_norm_w_2': 8.0,
     'k_norm_w_2': 8.0,
     'attn_norm_w_2': 8.0,
     'q_norm_w_2': 8.0,
     'attn_sinks_2': 34.393,
     'ple_norm_w_2': 8.0}
    for name, (base, spread) in spreads.items():
        noise = np.random.default_rng([zlib.crc32(name.encode()), seed]).standard_normal(out[name].shape)
        drawn = base * np.exp(spread * noise) if base else spread * noise
        out[name] = jnp.asarray(drawn.astype(out[name].dtype))
    for name, factor in factors.items():
        out[name] = (out[name] * factor).astype(out[name].dtype)
    return out
```

```python
from contextlib import ExitStack

import numpy as np
import concourse.bass as bass
from concourse import mybir

F32 = mybir.dt.float32
I32 = mybir.dt.int32
ALU = mybir.AluOpType
ACT = mybir.ActivationFunctionType
AX = mybir.AxisListType

P = 128
D = 1024
KT = D // P
T = 256
NEG = -1.0e30
GAMMA = [1.0 - 2.0 ** (-5 - h) for h in range(8)]
LEVELS = 7


def constants():
    r = np.arange(P)
    row, col = r[:, None], r[None, :]
    parts = {}
    parts["ident"] = (row == col)
    parts["incl"] = (row <= col)
    parts["strict"] = (row < col)
    parts["ones"] = np.ones((P, P))
    parts["blk"] = (row // 64 == col // 64)
    parts["blkret"] = np.repeat(parts["blk"][:, ::64], P, axis=1)
    for k in range(LEVELS):
        same = (row >> (k + 1)) == (col >> (k + 1))
        parts[f"off{k}"] = same & (((col >> k) & 1) == 1) & (((row >> k) & 1) == 0)
    parts["off0L"] = parts["off0"].T
    causal = np.where(col <= row, 0.0, NEG)
    before = np.where(col > row, 0.0, NEG)
    parts["att0"] = causal
    parts["att1"] = np.concatenate([before, causal], axis=1)
    lg = np.log1p(-np.exp2(-5.0 - np.arange(8)))
    parts["gq"] = np.exp((r[:, None] + 1.0) * lg[None])
    parts["gk"] = np.exp((127.0 - r[:, None]) * lg[None]) * 0.125
    inv = (10000.0 ** (-np.arange(32) / 32)).astype(np.float32)
    parts["inv"] = np.broadcast_to(inv[None], (P, 32))
    where, at = {}, 0
    for n, a in parts.items():
        where[n] = (at, a.shape[1])
        at += a.shape[1]
    return where, np.concatenate([np.asarray(a, np.float32) for a in parts.values()], axis=1)


def weight_blocks():
    out = []

    def full(name, w, c0, cols):
        out.append((name, [(w, 0, KT, c0, cols)]))

    def deep(name, w, n):
        for t in range(0, n, 4):
            out.append((f"{name}{t // 4}", [(w, t * P, min(4, n - t), 0, D)]))

    for c in range(0, 1792, 512):
        full(f"rw{c // 512}", "w_in", c, min(512, 1792 - c))
    for n, name in enumerate(["q", "k", "v0", "v1", "g0", "g1", "s0", "s1", "s2", "s3"]):
        full("r" + name, "w_in", 1792 + 512 * n, 512)
    deep("brw", "w_branch_rw", 4)
    deep("bret", "w_branch_ret", 8)
    deep("wo", "w_out", 8)
    for j in range(11):
        out.append((f"up{j}", [("ffn_w_up", 0, KT, 256 * j, 256), ("ffn_w_up", 0, KT, 2816 + 256 * j, 256)]))
    deep("dn", "ffn_w_down", 22)
    for j in range(4):
        full(f"z{j}", "ssm_in_w_2", 512 * j, 512)
    for j in range(6):
        full(f"xbc{j}", "ssm_in_w_2", 2048 + 512 * j, 512)
    full("dt", "ssm_in_w_2", 5120, 32)
    deep("so", "ssm_out_w_2", 16)

    def embed(m):
        out.append((f"pp{m}", [(f"ple_proj_w_2:{m}", 0, 2, 0, D)]))
        full(f"pg{m}0", f"ple_gate_w_2:{m}", 0, 512)
        full(f"pg{m}1", f"ple_gate_w_2:{m}", 512, 512)

    embed(0)
    full("kv", "kv_w_2", 0, 512)
    for j in range(4):
        full(f"ain{j}", "attn_in_w_2", 512 * j, 512)
    deep("ao", "attn_out_w_2", 8)
    embed(1)
    return out


SLOTS = 3
SLOT = 4096

STAGES = [
    [("norm_mix_pre", 0, 8), ("norm_ffn_pre", 0, 8), ("ssm_norm_w_2", 0, 8), ("ple_norm_w_2", 0, 8),
     ("kv_norm_w_2", 0, 8), ("attn_norm_w_2", 0, 8), ("ple_norm_w_2", 8, 8), ("rw_mu", 0, 14), ("rw_w0", 0, 4),
     ("rw_a0", 0, 4), ("rw_k_k", 0, 4), ("rw_k_a", 0, 4), ("rw_r_k", 0, 4), ("rw_lnx_w", 0, 4),
     ("rw_lnx_b", 0, 4), ("ssm_gnorm_w_2", 0, 16)],
    [("ffn_conv_w", 0, 88)],
    [("ffn_conv_w", 88, 44), ("ffn_conv_b", 0, 44)],
    [("ssm_conv_w_2", 0, 96), ("ssm_conv_b_2", 0, 24)],
]


def build(nc, io, out, where, ncols):
    ctx = ExitStack()
    with ctx:
        def sb(name, shape, dt=F32):
            return ctx.enter_context(nc.sbuf_tensor(name, shape, dt))

        sems = {}

        def sem(name):
            if name not in sems:
                sems[name] = ctx.enter_context(nc.semaphore(name))
            return sems[name]

        consts = sb("consts", [P, ncols])
        ring = sb("ring", [P, SLOTS * SLOT])
        cols = sb("cols", [P, 512])
        lora = sb("lora", [P, 2, 512])
        postw = sb("postw", [P, D])
        rowp = sb("rowp", [P, 64 + 64 + 16 + 32 * 3])
        h = sb("h", [P, 2, D])
        xT = sb("xT", [P, KT, T])
        small = sb("small", [P, 1400])
        posi = sb("posi", [P, 4], I32)
        arena = sb("arena", [P, 30224])
        PS = [ctx.enter_context(nc.psum_tensor(f"bank{b}", [P, 512], F32)) for b in range(8)]

        def const(name):
            a, n = where[name]
            return consts[:, a:a + n]

        ident = const("ident")

        def ar(at, *shape):
            n = int(np.prod(shape))
            v = arena[:, at:at + n]
            if len(shape) == 2:
                v = v.rearrange("p (a b) -> p a b", a=shape[0])
            if len(shape) == 3:
                v = v.rearrange("p (a b c) -> p a b c", a=shape[0], b=shape[1])
            if len(shape) == 4:
                v = v.rearrange("p (a b c d) -> p a b c d", a=shape[0], b=shape[1], c=shape[2])
            return v

        def sm(at, *shape):
            n = int(np.prod(shape))
            v = small[:, at:at + n]
            if len(shape) == 2:
                v = v.rearrange("p (a b) -> p a b", a=shape[0])
            if len(shape) == 3:
                v = v.rearrange("p (a b c) -> p a b c", a=shape[0], b=shape[1])
            return v

        hs = ar(0, 2, D)
        tmph = hs
        pr = ar(2048, 14, 257)
        dif = ar(5648, 14, 256)
        ld, av, kn = ar(5648, 4, 256), ar(6672, 4, 256), ar(7696, 4, 256)
        qr, kr = ar(9232, 2, 512), ar(10256, 2, 512)
        cc, gT = ar(11280, 4, 256), ar(12304, 4, 256)
        zr = ar(13328, 4, 2, 256)
        bt, kt = ar(15376, 4, 2, P), ar(16400, 4, 2, P)
        vrow, yrow = ar(17424, 2, 512), ar(18448, 2, 512)
        krow, brow = ar(19472, 512), ar(19984, 512)
        sa, rhs = ar(20496, 512), ar(21008, 512)
        s0 = ar(21520, 4, P)
        mats = ar(22032, 8, 4, P)
        ex = ar(22032, 4, 256)
        ex2 = ar(23056, 4, 256)
        ex3 = ar(24080, 4, 256)
        lor = ar(25104, 2, 256)
        inv, invT, t1, lk = ar(26128, 8, P), ar(27152, 8, P), ar(28176, 8, P), ar(29200, 8, P)
        yrwT = ar(16400, 4, T)
        stage = ar(18448, 4, P)
        vr, gr = ar(22032, 2, D), ar(24080, 2, D)
        sg = ar(26128, 2, 2, D)
        qT, kTr = ar(5648, 4, T), ar(6672, 4, T)
        sT = ar(7696, 8, P)
        rst = ar(11280, 4, T)
        orow = ar(13328, 2, D)
        oT = ar(2048, KT, T)
        ro1, ro2 = ar(17424, 2, 512), ar(18448, 2, 512)
        mrow, mT = ar(13328, 2, D), ar(9232, KT, T)
        mtmp = ar(17424, 512)
        actT = ar(2048, 22, T)
        acc = ar(8192, 2, 4, T)
        zrow = ar(2048, 2, 2048)
        xbc = ar(6144, 24, T)
        xs = ar(12288, 2, 2048)
        xd = ar(16384, 2, 2048)
        xdd = ar(20480, 2048)
        wT = ar(22528, 2, 8, P)
        eT2 = ar(24576, 2, 512)
        bR = ar(25600, 512)
        ss0 = ar(26112, 4, 512)
        cbm = ar(28160, 2, 512)
        cacc = ar(29184, 4, T)
        ygT = ar(16384, 16, T)
        prow, pT = ar(2048, 2, T), ar(2560, 2, T)
        psg = ar(3072, 2, 512)
        xT2 = ar(2048, KT, T)
        kvr = ar(4096, 2, 512)
        aq, ag = ar(5120, 2, D), ar(7168, 2, D)
        at1, at2 = ar(9216, 2, D), ar(11264, 2, D)
        aqr = ar(13312, 2, D)
        aqT = ar(15360, 2, 4, T)
        akT = ar(17408, 2, T)
        akr = ar(17920, 2, T)
        asb = ar(18432, 2, 512)
        aeT = ar(20480, 2, 512)
        ao = ar(21504, 2, D)
        aoT = ar(23552, KT, T)
        ssq, rstd = sm(0, 4), sm(4, 4)
        mean, var, rs8 = sm(8, 2, 32), sm(72, 2, 32), sm(136, 2, 32)
        dtv, adt, acs = sm(200, 2, 32), sm(264, 2, 32), sm(328, 2, 32)
        tot, dte, eac = sm(392, 32), sm(424, 32), sm(456, 32)
        arow = sm(488, 32)
        ang, cosd, sind = sm(520, 4, 32), sm(648, 4, 64), sm(904, 4, 64)
        angn = sm(1160, 4, 32)
        posf = sm(1288, 4)
        fcol = sm(1292, 4)
        om = sm(1296, 4)
        mx, den, dsk = sm(1300, 2, 4), sm(1308, 12, 4), sm(1356, 2, 4)
        eps6 = sm(1364, 1)
        qn, kn_, sinks, dtb, alog, dsk_ = (rowp[:, 0:64], rowp[:, 64:128], rowp[:, 128:144], rowp[:, 144:176],
                                           rowp[:, 176:208], rowp[:, 208:240])

        colat, at = {}, 0
        for g, parts in enumerate(STAGES):
            at = [0, 114, 202, 290][g]
            for name, r0, n in parts:
                colat[(name, r0)] = at
                at += n

        def pc(name, j, r0=0):
            a = colat[(name, r0)] + j
            return cols[:, a:a + 1]

        def pcs(name, n, r0=0):
            a = colat[(name, r0)]
            return cols[:, a:a + n]

        def fcw(tap, c):
            return cols[:, 114 + 44 * tap + c:115 + 44 * tap + c]

        def fcb(c):
            return cols[:, 202 + 44 + c:203 + 44 + c]

        def scw(tap, c):
            return cols[:, 290 + 24 * tap + c:291 + 24 * tap + c]

        def scb(c):
            return cols[:, 290 + 96 + c:291 + 96 + c]

        blocks = weight_blocks()
        index = {name: n for n, (name, _) in enumerate(blocks)}
        landed_at, count = [], [0] * SLOTS
        for n, (_, pieces) in enumerate(blocks):
            count[n % SLOTS] += 16 * len(pieces)
            landed_at.append(count[n % SLOTS])
        weights_landed = [sem(f"weights_landed{s}") for s in range(SLOTS)]
        weights_used, deep_used = sem("weights_used"), [0]
        block_done = {}

        def slot(name, nk, width, piece=0):
            n = index[name]
            at = (n % SLOTS) * SLOT + piece * nk * width
            return ring[:, at:at + nk * width].rearrange("p (k c) -> p k c", k=nk)

        def landed(eng, name):
            n = index[name]
            eng.wait_ge(weights_landed[n % SLOTS], landed_at[n])

        psum_full = [sem(f"psum_full{b}") for b in range(8)]
        psum_emptied = [sem(f"psum_emptied{b}") for b in range(8)]
        uses, use_of = [0] * 8, {}

        def take(pe, key, bank):
            if uses[bank]:
                pe.wait_ge(psum_emptied[bank], uses[bank])
            uses[bank] += 1
            use_of[key] = (bank, uses[bank])
            return PS[bank]

        def fill(ins, key):
            ins.then_inc(psum_full[use_of[key][0]], 1)

        def full(eng, key):
            bank, n = use_of[key]
            eng.wait_ge(psum_full[bank], n)
            return PS[bank]

        def empty(ins, key):
            ins.then_inc(psum_emptied[use_of[key][0]], 1)

        def emptied(eng, *keys):
            for key in keys:
                bank, n = use_of[key]
                eng.wait_ge(psum_emptied[bank], n)

        NORMS = ["norm_mix_pre", "norm_ffn_pre", "ssm_norm_w_2", "ple_norm_w_2", "attn_norm_w_2", "ple_norm_w_2"]
        norm_keys = lambda n: [("nT", n, i, q) for i in range(2) for q in range(2)]
        UNITS = [(0, u, o, 0) for u in range(2) for o in range(2)] + \
                [(1, u, o, g) for u in range(2) for o in range(2) for g in range(2)]
        HR = {1: 2, 2: 4, 3: 6, 4: 8, 5: 10}
        block = ctx.enter_context(nc.Block())

        @block.tensor
        def _(pe):
            mm = pe.matmul

            def turns(key, bank, ins):
                ps = take(pe, key, bank)
                for j, a in enumerate(ins):
                    m, n = a.shape
                    last = pe.transpose(ps[0:n, j * P:j * P + m], a, ident[0:m, 0:m])
                fill(last, key)

            def norm_turns(n):
                for i in range(2):
                    pe.wait_ge(sem("rows_scaled"), 2 * n + i + 1)
                    for q in range(2):
                        turns(("nT", n, i, q), 4 + 2 * i + q, [hs[:, i, P * (4 * q + j):P * (4 * q + j + 1)]
                                                               for j in range(4)])

            def turned_product(name, c, width, key, bank, piece=0):
                w = slot(name, KT, width, piece)
                ps = take(pe, key, bank)
                for k in range(KT):
                    last = mm(ps[:, 0:T], w[:, k, c * P:(c + 1) * P], xT[:, k, :], start=(k == 0), stop=(k == KT - 1))
                fill(last, key)

            def used(name, key):
                block_done[name] = (psum_full[use_of[key][0]], use_of[key][1])

            def deep_product(name, n, xt, key, banks):
                ps = {(i, f): take(pe, (key, i, f), banks + 2 * i + f) for i in range(2) for f in range(2)}
                for t in range(n):
                    if t % 4 == 0:
                        landed(pe, f"{name}{t // 4}")
                        w = slot(f"{name}{t // 4}", min(4, n - t), D)
                    for i in range(2):
                        for f in range(2):
                            last = mm(ps[i, f][:, :], xt[:, t, i * P:(i + 1) * P], w[:, t % 4, 512 * f:512 * f + 512],
                                      start=(t == 0), stop=(t == n - 1))
                            if t == n - 1:
                                fill(last, (key, i, f))
                    if t == n - 1:
                        used(f"{name}{t // 4}", (key, 1, 1))
                    elif t % 4 == 3:
                        last.then_inc(weights_used, 1)
                        deep_used[0] += 1
                        block_done[f"{name}{t // 4}"] = (weights_used, deep_used[0])

            def rows(name, keys, banks, x, width=512):
                landed(pe, name)
                w = slot(name, KT, width)
                for i in range(2):
                    ps = take(pe, keys[i], banks[i])
                    for k in range(KT):
                        last = mm(ps[:, 0:width], x[:, k, i * P:(i + 1) * P], w[:, k, :],
                                  start=(k == 0), stop=(k == KT - 1))
                    fill(last, keys[i])
                used(name, keys[1])

            pe.wait_ge(sem("consts_landed"), 16)
            pe.wait_ge(sem("stage_landed"), 16 * sum(len(s) for s in STAGES))
            for g, parts in enumerate(STAGES):
                n = sum(p[2] for p in parts)
                turns(("cols", g), g, [stage[0:n, g, :]])
            norm_turns(0)
            emptied(pe, *norm_keys(0))
            for c in range(14):
                b, cw = c // 4, (512 if c < 12 else 256)
                if c % 4 == 0:
                    landed(pe, f"rw{b}")
                turned_product(f"rw{b}", c % 4, cw, ("rw", c), c % 4)
                if c % 4 == 3 or c == 13:
                    used(f"rw{b}", ("rw", c))
            rows("rq", [("rq", i) for i in range(2)], (4, 5), xT)
            rows("rk", [("rk", i) for i in range(2)], (6, 7), xT)
            pe.wait_ge(sem("lora_in"), 2)
            pe.wait_ge(sem("shifted"), 14)
            pe.wait_ge(sem("lora_landed"), 48)
            for p in range(4):
                ps = take(pe, ("w", p), p % 2)
                fill(mm(ps[:, 0:T], lora[0:64, 0, P * p:P * p + P], lor[0:64, 0, :], start=True, stop=True), ("w", p))
                ps = take(pe, ("a", p), 2 + p % 2)
                fill(mm(ps[:, 0:T], lora[64:128, 0, P * p:P * p + P], pr[64:128, 12, 1:257],
                        start=True, stop=True), ("a", p))
                ps = take(pe, ("g", p), 4 + p % 2)
                fill(mm(ps[:, 0:T], lora[:, 1, P * p:P * p + P], lor[:, 1, :], start=True, stop=True), ("g", p))
            for i in range(2):
                turns(("vT", i), 6 + i, [pr[:, 8 + p, 1 + P * i:1 + P * i + P] for p in range(4)])
            for p in range(4):
                if p == 0:
                    pe.wait_ge(sem("kk_squared"), 1)
                ps = take(pe, ("ss", p), p)
                fill(mm(ps[:, 0:T], const("blk"), ex[:, p, :], start=True, stop=True), ("ss", p))
            for p in range(4):
                if p == 0:
                    pe.wait_ge(sem("rk_ready"), 1)
                ps = take(pe, ("bs", p), 4 + p)
                fill(mm(ps[:, 0:T], const("blk"), ex2[:, p, :], start=True, stop=True), ("bs", p))
            pe.wait_ge(sem("decayed"), 1)
            for n in range(2):
                if n == 0:
                    turns(("kbT", 0), 6, [kt[:, p, 0, :] for p in range(4)])
                    turns(("kbT", 1), 7, [bt[:, p, 0, :] for p in range(4)])
                for hd in range(8):
                    p, o = hd // 2, hd % 2
                    r = slice(64 * o, 64 * o + 64)
                    ps = take(pe, ("m", n, hd), hd % 4)
                    mm(ps[:, 0:256], bt[r, p, n, :], zr[r, p, n, :], start=True, stop=True)
                    fill(mm(ps[:, 256:512], kt[r, p, n, :], zr[r, p, n, :], start=True, stop=True), ("m", n, hd))
                for o in range(2):
                    r = slice(64 * o, 64 * o + 64)
                    ps = take(pe, ("L", n, o), 4 + o)
                    for p in range(4):
                        last = mm(ps[:, P * p:P * p + P], zr[r, p, n, 0:P], bt[r, p, n, :], start=True, stop=True)
                    fill(last, ("L", n, o))
                pe.wait_ge(sem("inv_start"), n + 1)
                for k in range(1, LEVELS):
                    for q in range(2):
                        pe.wait_ge(sem("lk_ready"), 12 * n + 2 * (k - 1) + q + 1)
                        if k > 1:
                            emptied(pe, ("x", n, k - 1, q), ("xt", n, k - 1, q))
                        ps = take(pe, ("t1", n, k, q), 4 + q)
                        for e in range(4):
                            last = mm(ps[:, P * e:P * e + P], lk[:, 4 * q + e, :], inv[:, 4 * q + e, :],
                                      start=True, stop=True)
                        fill(last, ("t1", n, k, q))
                    for q in range(2):
                        emptied(pe, ("t1", n, k, q))
                        for key, a, b, bank in ((("x", n, k, q), invT, t1, 2 * q), (("xt", n, k, q), t1, invT, 2 * q + 1)):
                            ps = take(pe, key, bank)
                            for e in range(4):
                                hd = 4 * q + e
                                last = mm(ps[:, P * e:P * e + P], a[:, hd, :], b[:, hd, :], start=True, stop=True)
                            fill(last, key)
                emptied(pe, ("vT", 0), ("vT", 1))
                if n:
                    pe.wait_ge(sem("state_ready"), 1)
                ps = take(pe, ("rhs", n), 6)
                for p in range(4):
                    if n:
                        mm(ps[:, P * p:P * p + P], zr[:, p, n, 0:P], s0[:, p, :], start=True, stop=False)
                    for o in range(2):
                        hd = 2 * p + o
                        last = mm(ps[:, 64 * hd:64 * hd + 64], mats[:, hd, 2, :], vrow[:, n, 64 * hd:64 * hd + 64],
                                  start=(n == 0), stop=(n == 0 or o == 1))
                fill(last, ("rhs", n))
                emptied(pe, ("rhs", n), ("x", n, LEVELS - 1, 0), ("x", n, LEVELS - 1, 1),
                        ("xt", n, LEVELS - 1, 0), ("xt", n, LEVELS - 1, 1))
                ps = take(pe, ("sa", n), 7)
                for hd in range(8):
                    last = mm(ps[:, 64 * hd:64 * hd + 64], invT[:, hd, :], rhs[:, 64 * hd:64 * hd + 64],
                              start=True, stop=True)
                fill(last, ("sa", n))
                emptied(pe, ("sa", n))
                ps = take(pe, ("y", n), 6)
                for p in range(4):
                    if n:
                        mm(ps[:, P * p:P * p + P], zr[:, p, n, P:2 * P], s0[:, p, :], start=True, stop=False)
                    for o in range(2):
                        hd = 2 * p + o
                        c = slice(64 * hd, 64 * hd + 64)
                        mm(ps[:, c], mats[:, hd, 3, :], vrow[:, n, c], start=(n == 0), stop=False)
                        last = mm(ps[:, c], mats[:, hd, 1, :], sa[:, c], start=False, stop=(n == 0 or o == 1))
                fill(last, ("y", n))
                if n == 0:
                    emptied(pe, ("kbT", 0), ("kbT", 1))
                    ps = take(pe, ("st",), 7)
                    for p in range(4):
                        c = slice(P * p, P * p + P)
                        mm(ps[:, c], krow[:, c], vrow[:, 0, c], start=True, stop=False)
                        last = mm(ps[:, c], brow[:, c], sa[:, c], start=False, stop=True)
                    fill(last, ("st",))
            for f in range(2):
                rows(f"rv{f}", [("rv", f, i) for i in range(2)], (0, 1) if f == 0 else (2, 3), xT)
            for f in range(2):
                rows(f"rg{f}", [("rg", f, i) for i in range(2)], (0, 1) if f == 0 else (2, 3), xT)
            for f in range(4):
                rows(f"rs{f}", [("rs", f, i) for i in range(2)], (0, 1) if f % 2 == 0 else (2, 3), xT)
            pe.wait_ge(sem("y_rows"), 1)
            for i in range(2):
                turns(("yT", i), 4 + i, [yrow[:, i, P * p:P * p + P] for p in range(4)])
            pe.wait_ge(sem("qk_rope"), 2)
            for i in range(2):
                turns(("qT", i), 6, [qr[:, i, P * p:P * p + P] for p in range(4)])
                turns(("kTr", i), 7, [kr[:, i, P * p:P * p + P] for p in range(4)])
            emptied(pe, ("rv", 0, 0), ("rv", 1, 0), ("rv", 0, 1), ("rv", 1, 1))
            for g in range(2):
                ps = take(pe, ("R", g), 4 + g)
                for e in range(2):
                    p = 2 * g + e
                    last = mm(ps[:, 256 * e:256 * e + 256], kr[:, 0, P * p:P * p + P], vr[:, 0, 256 * p:256 * p + 256],
                              start=True, stop=True)
                fill(last, ("R", g))
            emptied(pe, ("qT", 0), ("qT", 1), ("kTr", 0), ("kTr", 1))
            for n in range(2):
                for o in range(2):
                    r = slice(64 * o, 64 * o + 64)
                    ps = take(pe, ("s", n, o), o)
                    for p in range(4):
                        last = mm(ps[:, P * p:P * p + P], kTr[r, p, P * n:P * n + P], qT[r, p, P * n:P * n + P],
                                  start=True, stop=True)
                    fill(last, ("s", n, o))
                emptied(pe, ("s", n, 0), ("s", n, 1))
                if n:
                    emptied(pe, ("R", 0), ("R", 1))
                for g in range(2):
                    ps = take(pe, ("o", n, g), 2 + g)
                    for e in range(2):
                        p = 2 * g + e
                        if n:
                            mm(ps[:, 256 * e:256 * e + 256], qT[:, p, P:2 * P], rst[:, p, :], start=True, stop=False)
                        for o in range(2):
                            hd = 2 * p + o
                            last = mm(ps[:, 256 * e + P * o:256 * e + P * o + P], sT[:, hd, :],
                                      vr[:, n, P * hd:P * hd + P], start=(n == 0), stop=(n == 0 or o == 1))
                    fill(last, ("o", n, g))
            pe.wait_ge(sem("o_rows"), 1)
            for i in range(2):
                for q in range(2):
                    turns(("oT", i, q), 4 + 2 * i + q, [orow[:, i, P * (4 * q + j):P * (4 * q + j) + P] for j in range(4)])
            pe.wait_ge(sem("yrwT_ready"), 1)
            deep_product("brw", 4, yrwT, "brw", 0)
            emptied(pe, *[("oT", i, q) for i in range(2) for q in range(2)])
            deep_product("bret", 8, oT, "bret", 4)
            pe.wait_ge(sem("merged"), 1)
            for i in range(2):
                for q in range(2):
                    turns(("mT", i, q), 4 + 2 * i + q, [mrow[:, i, P * (4 * q + j):P * (4 * q + j) + P] for j in range(4)])
            emptied(pe, *[("mT", i, q) for i in range(2) for q in range(2)])
            deep_product("wo", 8, mT, "wo", 0)
            norm_turns(1)
            emptied(pe, *norm_keys(1))
            for j in range(11):
                landed(pe, f"up{j}")
                for c in range(4):
                    turned_product(f"up{j}", c % 2, 256, ("up", j, c), 4 * (j % 2) + c, piece=c // 2)
                used(f"up{j}", ("up", j, 3))
            pe.wait_ge(sem("act_ready"), 22)
            deep_product("dn", 22, actT, "dn", 0)
            norm_turns(2)
            emptied(pe, *norm_keys(2))
            for j in range(4):
                rows(f"z{j}", [("z", j, i) for i in range(2)], (0, 1) if j % 2 == 0 else (2, 3), xT)
            for c in range(24):
                if c % 4 == 0:
                    landed(pe, f"xbc{c // 4}")
                turned_product(f"xbc{c // 4}", c % 4, 512, ("xbc", c), c % 4)
                if c % 4 == 3:
                    used(f"xbc{c // 4}", ("xbc", c))
            landed(pe, "dt")
            ps = take(pe, ("dt",), 4)
            w = slot("dt", KT, 32)
            for i in range(2):
                for k in range(KT):
                    last = mm(ps[:, 32 * i:32 * i + 32], xT[:, k, i * P:(i + 1) * P], w[:, k, :],
                              start=(k == 0), stop=(k == KT - 1))
            fill(last, ("dt",))
            used("dt", ("dt",))
            pe.wait_ge(sem("adt_ready"), 1)
            ps = take(pe, ("ac",), 5)
            for n in range(2):
                mm(ps[:, 32 * n:32 * n + 32], const("incl"), adt[:, n, :], start=True, stop=True)
            fill(mm(ps[:, 64:96], const("ones"), adt[:, 0, :], start=True, stop=True), ("ac",))
            pe.wait_ge(sem("xbc_ready"), 24)
            for i in range(2):
                for q in range(4):
                    turns(("xsT", i, q), 6 + q % 2, [xbc[:, 4 * q + j, P * i:P * i + P] for j in range(4)])
            turns(("bR",), 6, [xbc[:, 16 + g, 0:P] for g in range(4)])
            for n in range(2):
                ps = take(pe, ("cb", n), 7)
                for g in range(4):
                    last = mm(ps[:, P * g:P * g + P], xbc[:, 16 + g, P * n:P * n + P], xbc[:, 20 + g, P * n:P * n + P],
                              start=True, stop=True)
                fill(last, ("cb", n))
            pe.wait_ge(sem("xd_ready"), 3)
            emptied(pe, ("bR",))
            for g in range(4):
                ps = take(pe, ("sst", g), 4 + g % 2)
                fill(mm(ps[:, :], bR[:, P * g:P * g + P], xdd[:, 512 * g:512 * g + 512], start=True, stop=True), ("sst", g))

            def spread(n, u):
                ps = take(pe, ("bc", n, u), u % 2)
                for e in range(4):
                    hd = 4 * u + e
                    last = mm(ps[:, P * e:P * e + P], adt[:, n, hd:hd + 1].to_broadcast([P, P]), const("incl"),
                              start=True, stop=True)
                fill(last, ("bc", n, u))

            spread(0, 0)
            spread(0, 1)
            for n in range(2):
                for g in range(4):
                    if 4 * n + g < 7:
                        nn, ng = divmod(4 * n + g + 1, 4)
                        spread(nn, 2 * ng)
                        spread(nn, 2 * ng + 1)
                    pe.wait_ge(sem("wT_ready"), 2 * (4 * n + g) + 2)
                    ps = take(pe, ("yd", n, g), 2 + g % 2)
                    for e in range(8):
                        hd = 8 * g + e
                        last = mm(ps[:, 64 * e:64 * e + 64], wT[:, g % 2, e, :], xd[:, n, 64 * hd:64 * hd + 64],
                                  start=True, stop=True)
                    fill(last, ("yd", n, g))
                    if n:
                        emptied(pe, ("sst", g))
                        ps = take(pe, ("yo", g), 4 + g % 2)
                        fill(mm(ps[:, :], xbc[:, 20 + g, P:2 * P], ss0[:, g, :], start=True, stop=True), ("yo", g))
            pe.wait_ge(sem("yg_rows"), 2)
            for i in range(2):
                for q in range(4):
                    turns(("gT", i, q), 6 + q % 2, [xs[:, i, P * (4 * q + j):P * (4 * q + j) + P] for j in range(4)])
            emptied(pe, *[("gT", i, q) for i in range(2) for q in range(4)])
            deep_product("so", 16, ygT, "so", 0)

            def embed(m):
                norm_turns(3 if m == 0 else 5)
                pe.wait_ge(sem("p_landed"), 16 * (m + 1))
                turns(("pT", m), 0, [prow[:, i, P * k:P * k + P] for k in range(2) for i in range(2)])
                emptied(pe, *norm_keys(3 if m == 0 else 5))
                emptied(pe, ("pT", m))
                landed(pe, f"pp{m}")
                w = slot(f"pp{m}", 2, D)
                for f in range(2):
                    for i in range(2):
                        ps = take(pe, ("pp", m, f, i), 4 + 2 * f + i)
                        for k in range(2):
                            last = mm(ps[:, :], pT[:, k, i * P:(i + 1) * P], w[:, k, 512 * f:512 * f + 512],
                                      start=(k == 0), stop=(k == 1))
                        fill(last, ("pp", m, f, i))
                used(f"pp{m}", ("pp", m, 1, 1))
                for f in range(2):
                    rows(f"pg{m}{f}", [("pg", m, f, i) for i in range(2)], (2 * f, 2 * f + 1), xT)

            embed(0)
            norm_turns(4)
            pe.wait_ge(sem("xT2_ready"), 4)
            rows("kv", [("kv", i) for i in range(2)], (0, 1), xT2)
            emptied(pe, *norm_keys(4))
            for j in range(4):
                rows(f"ain{j}", [("ain", j, i) for i in range(2)], (2, 3) if j % 2 == 0 else (0, 1), xT)
            pe.wait_ge(sem("ak_rows"), 1)
            turns(("akT",), 6, [akr[:, i, P * u:P * u + P] for u in range(2) for i in range(2)])
            pe.wait_ge(sem("aq_rows"), 1)
            for i in range(2):
                for u in range(2):
                    turns(("aqT", i, u), 4 + u, [aqr[:, i, 512 * u + P * g:512 * u + P * g + P] for g in range(4)])
            emptied(pe, ("akT",), *[("aqT", i, u) for i in range(2) for u in range(2)])

            def scores(z):
                n, u, o, gh = UNITS[z]
                r = slice(64 * o, 64 * o + 64)
                ps = take(pe, ("as", z), 2 * (z % 2) + o)
                nh, w = (4, P) if n == 0 else (2, 2 * P)
                for e in range(nh):
                    last = mm(ps[:, w * e:w * e + w], aqT[r, u, nh * gh * n + e, P * n:P * n + P], akT[r, u, 0:w],
                              start=True, stop=True)
                fill(last, ("as", z))

            def values(z):
                n, u, o, gh = UNITS[z]
                pe.wait_ge(sem("exps"), z + 1)
                turns(("eT", z), 4 + z % 2, [asb[:, z % 2, P * j:P * j + P] for j in range(4)])
                emptied(pe, ("eT", z))
                ps = take(pe, ("ao", z), 6 + z % 2)
                nh, kt_ = (4, 1) if n == 0 else (2, 2)
                for e in range(nh):
                    for s in range(kt_):
                        last = mm(ps[:, 64 * e:64 * e + 64], aeT[:, z % 2, P * (kt_ * e + s):P * (kt_ * e + s) + P],
                                  kvr[:, s, 256 + 64 * (2 * u + o):256 + 64 * (2 * u + o) + 64],
                                  start=(s == 0), stop=(s == kt_ - 1))
                fill(last, ("ao", z))

            scores(0)
            for z in range(len(UNITS)):
                if z + 1 < len(UNITS):
                    scores(z + 1)
                values(z)
            pe.wait_ge(sem("ao_rows"), 1)
            for i in range(2):
                for q in range(2):
                    turns(("aoT", i, q), 4 + 2 * i + q, [ao[:, i, P * (4 * q + j):P * (4 * q + j) + P] for j in range(4)])
            emptied(pe, *[("aoT", i, q) for i in range(2) for q in range(2)])
            deep_product("ao", 8, aoT, "fo", 0)
            embed(1)

        @block.sync
        def _(sp):
            sp.dma_start(h[:, :, :], io["x"].rearrange("o (i p) d -> p (o i) d", p=P)).then_inc(sem("x_landed"), 16)
            sp.dma_start(consts[:, :], io["table"]).then_inc(sem("consts_landed"), 16)

            def source(w):
                name, _, layer = w.partition(":")
                a = io[name]
                return a[int(layer or 0)] if len(a.shape) == 3 else a

            for n, (name, pieces) in enumerate(blocks):
                if n >= SLOTS:
                    sp.wait_ge(*block_done[blocks[n - SLOTS][0]])
                for j, (w, r0, nk, c0, width) in enumerate(pieces):
                    src = source(w)[r0:r0 + nk * P, c0:c0 + width].rearrange("(k p) c -> p k c", p=P)
                    sp.dma_start(slot(name, nk, width, j), src).then_inc(weights_landed[n % SLOTS], 16)
            sp.wait_ge(sem("out_ready"), 4)
            sp.dma_start(out.rearrange("o (i p) d -> p (o i) d", p=P), h[:, :, :]).then_inc(sem("out_written"), 16)
            sp.wait_ge(sem("out_written"), 16)

        @block.gpsimd
        def _(pool):
            for g, parts in enumerate(STAGES):
                at = 0
                for name, r0, n in parts:
                    src = io[name]
                    if len(src.shape) == 3:
                        src = src[0].rearrange("t (r c) -> (t r) c", c=P)
                    elif len(src.shape) == 2 and name == "ple_norm_w_2":
                        src = src.rearrange("l (r c) -> (l r) c", c=P)
                    elif len(src.shape) == 2:
                        src = src[0].rearrange("(r c) -> r c", c=P)
                    else:
                        src = src.rearrange("(r c) -> r c", c=P)
                    pool.dma_start(stage[at:at + n, g, :], src[r0:r0 + n, :]).then_inc(sem("stage_landed"), 16)
                    at += n
            pool.dma_start(lora[0:64, 0, :], io["rw_w2"][0]).then_inc(sem("lora_landed"), 16)
            pool.dma_start(lora[64:128, 0, :], io["rw_a2"][0]).then_inc(sem("lora_landed"), 16)
            pool.dma_start(lora[:, 1, :], io["rw_g2"][0]).then_inc(sem("lora_landed"), 16)

            def spread_row(dst, src, s):
                pool.dma_start(dst, src.partition_broadcast(P)).then_inc(sem(s), 16)

            spread_row(postw[:, :], io["norm_mix_post"][0], "postw_landed")
            for dst, src in ((qn, io["q_norm_w_2"][0]), (kn_, io["k_norm_w_2"]), (sinks, io["attn_sinks_2"][0]),
                             (dtb, io["ssm_dt_bias_2"][0]), (alog, io["ssm_a_log_2"][0]), (dsk_, io["ssm_d_2"][0])):
                spread_row(dst, src, "rowp_landed")
            for m, name in enumerate(["positions", "positions_2"]):
                pool.dma_start(posi[:, 2 * m:2 * m + 2], io[name].rearrange("o (i p) -> p (o i)", p=P),
                               allow_slow_non_contiguous=True).then_inc(sem("pos_landed"), 16)
            for n in range(2):
                for k in range(1, LEVELS):
                    if k == 1:
                        pool.wait_ge(sem("mats_ready"), 8 * (n + 1))
                    for q in range(2):
                        if k > 1:
                            full(pool, ("t1", n, k - 1, q))
                        elif n:
                            full(pool, ("t1", 0, LEVELS - 1, q))
                        pool.tensor_tensor(lk[:, 4 * q:4 * q + 4, :], mats[:, 4 * q:4 * q + 4, 0, :],
                                           const(f"off{k}").unsqueeze(1).broadcast_to([P, 4, P]), ALU.mult) \
                            .then_inc(sem("lk_ready"), 1)
            pool.wait_ge(sem("joined"), 4)
            spread_row(postw[:, :], io["norm_ffn_post"][0], "postw_landed")
            for m in range(2):
                pool.wait_ge(sem("h_ready"), 6 if m == 0 else 10)
                pool.dma_start(prow[:, :, :], io["p_2"][m].rearrange("o (i p) c -> p (o i) c", p=P)) \
                    .then_inc(sem("p_landed"), 16)

        @block.scalar
        def _(act):
            chain = [0]

            def link(ins):
                chain[0] += 1
                ins.then_inc(sem("act_chain"), 1)
                act.wait_ge(sem("act_chain"), chain[0])

            A = act.activation

            def norm(n):
                if n == 0:
                    act.wait_ge(sem("x_landed"), 16)
                else:
                    act.wait_ge(sem("h_ready"), HR[n])
                for i in range(2):
                    A(hs[:, i, :], h[:, i, :], ACT.Square, accum_out=ssq[:, i:i + 1]).then_inc(sem("sq_done"), 1)
                act.wait_ge(sem("sq_done"), 2 * (n + 1))
                act.wait_ge(sem("eps_set"), 1)
                A(rstd[:, 0:2], ssq[:, 0:2], ACT.Sqrt, scale=1.0 / D, bias=eps6).then_inc(sem("root"), 1)

            def post_norm(key, count):
                for i in range(2):
                    for f in range(2):
                        ps = full(act, (key, i, f))
                        A(hs[:, i, 512 * f:512 * f + 512], ps[:, :], ACT.Square,
                          accum_out=ssq[:, 2 * i + f:2 * i + f + 1]).then_inc(sem("post_sq"), 1)
                act.wait_ge(sem("post_sum"), count)
                A(rstd[:, 0:2], ssq[:, 0:2], ACT.Sqrt, scale=1.0 / D, bias=eps6).then_inc(sem("root2"), 1)

            def copy(dst, key, w=512, func=ACT.Copy):
                ps = full(act, key)
                empty(A(dst, ps[:, 0:w], func), key)

            norm(0)
            for c in range(14):
                copy(pr[:, c, 1:257], ("rw", c), T)
            act.wait_ge(sem("angles"), 1)
            A(cosd[:, :, 0:32], angn[:, :, :], ACT.Sin).then_inc(sem("trig"), 1)
            A(sind[:, :, 32:64], ang[:, :, :], ACT.Sin).then_inc(sem("trig"), 1)
            for i in range(2):
                copy(qr[:, i, :], ("rq", i))
                copy(kr[:, i, :], ("rk", i))
            act.wait_ge(sem("shifted"), 14)
            A(lor[0:64, 0, :], pr[0:64, 12, 1:257], ACT.Tanh).then_inc(sem("lora_in"), 1)
            A(lor[:, 1, :], pr[:, 13, 1:257], ACT.Sigmoid).then_inc(sem("lora_in"), 1)
            for p in range(4):
                ps = full(act, ("w", p))
                empty(A(ld[:, p, :], ps[:, 0:T], ACT.Sigmoid, bias=pc("rw_w0", p)), ("w", p))
                ps = full(act, ("a", p))
                empty(A(av[:, p, :], ps[:, 0:T], ACT.Sigmoid, bias=pc("rw_a0", p)), ("a", p))
                copy(gT[:, p, :], ("g", p), T)
            for i in range(2):
                copy(vrow[:, i, :], ("vT", i))
            act.wait_ge(sem("knorm_in"), 1)
            A(ex[:, :, :], ex3[:, :, :], ACT.Sqrt).then_inc(sem("knorm_root"), 1)
            act.wait_ge(sem("cum_ready"), 1)
            A(ex3[:, :, :], cc[:, :, :], ACT.Exp).then_inc(sem("e_done"), 1)
            act.wait_ge(sem("prev_ready"), 1)
            A(ex[:, :, :], ld[:, :, :], ACT.Exp).then_inc(sem("e_done"), 1)
            act.wait_ge(sem("rk_ready"), 1)
            for p in range(4):
                full(act, ("bs", p))
            A(ex2[:, :, :], cc[:, :, :], ACT.Exp, scale=-1.0).then_inc(sem("e_done"), 1)
            act.wait_ge(sem("fcol_in"), 1)
            A(fcol[:, :], fcol[:, :], ACT.Exp).then_inc(sem("f_done"), 1)
            copy(krow[:], ("kbT", 0))
            copy(brow[:], ("kbT", 1))
            for n in range(2):
                for k in range(1, LEVELS):
                    for q in range(2):
                        copy(t1[:, 4 * q:4 * q + 4, :], ("t1", n, k, q))
                copy(rhs[:], ("rhs", n))
                copy(sa[:], ("sa", n))
                copy(yrow[:, n, :], ("y", n))
            for f in range(2):
                for i in range(2):
                    copy(vr[:, i, 512 * f:512 * f + 512], ("rv", f, i))
            for f in range(2):
                for i in range(2):
                    copy(gr[:, i, 512 * f:512 * f + 512], ("rg", f, i), func=ACT.Silu)
            for f in range(4):
                for i in range(2):
                    copy(sg[:, i, f // 2, 512 * (f % 2):512 * (f % 2) + 512], ("rs", f, i), func=ACT.Sigmoid)
            act.wait_ge(sem("gn_var"), 1)
            A(rs8[:, :, 0:8], var[:, :, 0:8], ACT.Sqrt).then_inc(sem("gn_root"), 1)
            for i in range(2):
                ps = full(act, ("qT", i))
                empty(A(qT[:, :, P * i:P * i + P], ps[:, :].rearrange("p (a b) -> p a b", a=4), ACT.Copy), ("qT", i))
                ps = full(act, ("kTr", i))
                empty(A(kTr[:, :, P * i:P * i + P], ps[:, :].rearrange("p (a b) -> p a b", a=4), ACT.Copy), ("kTr", i))
            act.wait_ge(sem("gn_var"), 2)
            A(rs8[:, :, 0:8], var[:, :, 0:8], ACT.Sqrt).then_inc(sem("gn_root"), 1)
            for i in range(2):
                for q in range(2):
                    ps = full(act, ("oT", i, q))
                    empty(A(oT[:, 4 * q:4 * q + 4, P * i:P * i + P], ps[:, :].rearrange("p (a b) -> p a b", a=4),
                            ACT.Copy), ("oT", i, q))
            for i in range(2):
                for q in range(2):
                    ps = full(act, ("mT", i, q))
                    empty(A(mT[:, 4 * q:4 * q + 4, P * i:P * i + P], ps[:, :].rearrange("p (a b) -> p a b", a=4),
                            ACT.Copy), ("mT", i, q))
            post_norm("wo", 1)
            norm(1)
            for j in range(11):
                for c in range(4):
                    ch = 2 * j + c % 2 + 22 * (c // 2)
                    ps = full(act, ("up", j, c))
                    if j >= 2:
                        act.wait_ge(sem("act_ready"), 2 * (j - 1))
                    A(acc[:, j % 2, c, :], ps[:, 0:T], ACT.Identity, bias=fcb(ch), scale=fcw(2, ch)) \
                        .then_inc(sem("tap0"), 1)
                for c in range(2):
                    emptied(act, ("up", j, c))
                    A(acc[:, j % 2, c, :], acc[:, j % 2, c, :], ACT.Gelu_apprx_tanh).then_inc(sem("gelu"), 1)
            post_norm("dn", 2)
            norm(2)
            for j in range(4):
                for i in range(2):
                    copy(zrow[:, i, 512 * j:512 * j + 512], ("z", j, i), func=ACT.Silu)
            for c in range(24):
                ps = full(act, ("xbc", c))
                if c >= 4:
                    act.wait_ge(sem("xbc_ready"), c - 3)
                A(cacc[:, c % 4, :], ps[:, 0:T], ACT.Identity, bias=scb(c), scale=scw(3, c)).then_inc(sem("stap0"), 1)
                if c >= 1:
                    emptied(act, ("xbc", c - 1))
                    A(xbc[:, c - 1, :], cacc[:, (c - 1) % 4, :], ACT.Silu).then_inc(sem("xbc_ready"), 1)
            emptied(act, ("xbc", 23))
            A(xbc[:, 23, :], cacc[:, 3, :], ACT.Silu).then_inc(sem("xbc_ready"), 1)
            act.wait_ge(sem("dt_in"), 1)
            link(A(adt[:, :, :], adt[:, :, :], ACT.Exp))
            link(A(adt[:, :, :], adt[:, :, :], ACT.Ln, bias=1.0))
            act.wait_ge(sem("rowp_landed"), 96)
            A(arow[:, :], alog, ACT.Exp).then_inc(sem("dt_log"), 1)
            for i in range(2):
                for q in range(4):
                    copy(xs[:, i, 512 * q:512 * q + 512], ("xsT", i, q))
            copy(bR[:], ("bR",))
            act.wait_ge(sem("dte_in"), 1)
            A(dte[:, :], tot[:, :], ACT.Exp).then_inc(sem("dte_done"), 1)
            A(eac[:, :], acs[:, 1, :], ACT.Exp).then_inc(sem("dte_done"), 1)
            for g in range(4):
                copy(ss0[:, g, :], ("sst", g))
            for u in range(16):
                act.wait_ge(sem("seg_ready"), u + 1)
                A(eT2[:, u % 2, :], eT2[:, u % 2, :], ACT.Exp).then_inc(sem("seg_exp"), 1)
            for i in range(2):
                for g in range(4):
                    act.wait_ge(sem("yz_ready"), i + 1)
                    A(xd[:, i, 512 * g:512 * g + 512], xs[:, i, 512 * g:512 * g + 512], ACT.Square,
                      accum_out=mean[:, i, g:g + 1]).then_inc(sem("yg_sq"), 1)
            act.wait_ge(sem("yg_sq"), 8)
            A(var[:, :, 0:4], mean[:, :, 0:4], ACT.Sqrt, scale=1.0 / 512, bias=eps6).then_inc(sem("yg_root"), 1)

            def embed(m):
                n = 3 if m == 0 else 5
                norm(n)
                ps = full(act, ("pT", m))
                empty(A(pT[:, :, :], ps[:, :].rearrange("p (a b) -> p a b", a=2), ACT.Copy), ("pT", m))
                for f in range(2):
                    for i in range(2):
                        z = 2 * f + i
                        ps = full(act, ("pg", m, f, i))
                        if z >= 2 or m:
                            act.wait_ge(sem("ple_used"), 4 * m + z - 1)
                        empty(A(psg[:, z % 2, :], ps[:, :], ACT.Sigmoid), ("pg", m, f, i))

            embed(0)
            norm(4)
            for i in range(2):
                copy(kvr[:, i, :], ("kv", i))
            for j in range(2):
                for i in range(2):
                    copy(aq[:, i, 512 * j:512 * j + 512], ("ain", j, i))
            for j in range(2):
                for i in range(2):
                    copy(ag[:, i, 512 * j:512 * j + 512], ("ain", 2 + j, i), func=ACT.Silu)
            act.wait_ge(sem("hn_in"), 1)
            A(rs8[:, :, 0:4], var[:, :, 0:4], ACT.Sqrt).then_inc(sem("hn_root"), 1)
            act.wait_ge(sem("hn_in"), 2)
            A(rs8[:, :, 0:16], var[:, :, 0:16], ACT.Sqrt).then_inc(sem("hn_root"), 1)
            ps = full(act, ("akT",))
            empty(A(akT[:, :, :], ps[:, :].rearrange("p (a b) -> p a b", a=2), ACT.Copy), ("akT",))
            for i in range(2):
                for u in range(2):
                    ps = full(act, ("aqT", i, u))
                    empty(A(aqT[:, u, :, P * i:P * i + P], ps[:, :].rearrange("p (a b) -> p a b", a=4), ACT.Copy),
                          ("aqT", i, u))
            for z in range(len(UNITS)):
                act.wait_ge(sem("sub_ready"), z + 1)
                nh = 4 if UNITS[z][0] == 0 else 2
                A(dsk[:, z % 2, 0:nh], dsk[:, z % 2, 0:nh], ACT.Exp).then_inc(sem("sink_exp"), 1)
                A(asb[:, z % 2, :], asb[:, z % 2, :], ACT.Exp).then_inc(sem("exps"), 1)
                copy(aeT[:, z % 2, :], ("eT", z))
            for i in range(2):
                for q in range(2):
                    ps = full(act, ("aoT", i, q))
                    empty(A(aoT[:, 4 * q:4 * q + 4, P * i:P * i + P], ps[:, :].rearrange("p (a b) -> p a b", a=4),
                            ACT.Copy), ("aoT", i, q))
            embed(1)

        @block.vector
        def _(ve):
            chain = [0]

            def link(ins):
                chain[0] += 1
                ins.then_inc(sem("ve_chain"), 1)
                ve.wait_ge(sem("ve_chain"), chain[0])

            TT, TS, STT = ve.tensor_tensor, ve.tensor_scalar, ve.scalar_tensor_tensor
            mul, add, sub, mx_ = ALU.mult, ALU.add, ALU.subtract, ALU.max

            def bc(a, *shape):
                return a.broadcast_to(list(shape))

            def four(ps, a=4):
                return ps[:, :].rearrange("p (a b) -> p a b", a=a)

            link(ve.memset(eps6, 1e-6))
            ve.memset(pr[:, :, 0:1], 0.0).then_inc(sem("eps_set"), 1)

            def norm(n, name, r0=0):
                ve.wait_ge(sem("root"), n + 1)
                link(ve.reciprocal(rstd[:, 0:2], rstd[:, 0:2]))
                for i in range(2):
                    TS(hs[:, i, :], h[:, i, :], rstd[:, i:i + 1], None, mul).then_inc(sem("rows_scaled"), 1)
                for i in range(2):
                    for q in range(2):
                        ps = full(ve, ("nT", n, i, q))
                        if n == 4:
                            g = cols[:, colat[("kv_norm_w_2", 0)] + 4 * q:colat[("kv_norm_w_2", 0)] + 4 * q + 4]
                            TT(xT2[:, 4 * q:4 * q + 4, P * i:P * i + P], four(ps), bc(g.unsqueeze(2), P, 4, P), mul) \
                                .then_inc(sem("xT2_ready"), 1)
                        g = cols[:, colat[(name, r0)] + 4 * q:colat[(name, r0)] + 4 * q + 4]
                        empty(TT(xT[:, 4 * q:4 * q + 4, P * i:P * i + P], four(ps), bc(g.unsqueeze(2), P, 4, P), mul),
                              ("nT", n, i, q))

            def post_norm(key, n):
                ve.wait_ge(sem("post_sq"), 4 * n)
                v = ssq[:, :].rearrange("p (a b) -> p a b", a=2)
                link(TT(rstd[:, 2:4], v[:, :, 0], v[:, :, 1], add))
                ve.tensor_copy(ssq[:, 0:2], rstd[:, 2:4]).then_inc(sem("post_sum"), 1)
                ve.wait_ge(sem("root2"), n)
                link(ve.reciprocal(rstd[:, 0:2], rstd[:, 0:2]))
                ve.wait_ge(sem("postw_landed"), 16 * n)
                for i in range(2):
                    for f in range(2):
                        c = slice(512 * f, 512 * f + 512)
                        ps = full(ve, (key, i, f))
                        empty(STT(out=tmph[:, i, c], in0=ps[:, :], scalar=rstd[:, i:i + 1], in1=postw[:, c],
                                  op0=mul, op1=mul), (key, i, f))
                emptied(ve, *[(key, i, f) for i in range(2) for f in range(2)])
                for i in range(2):
                    for f in range(2):
                        c = slice(512 * f, 512 * f + 512)
                        TT(h[:, i, c], h[:, i, c], tmph[:, i, c], add).then_inc(sem("joined"), 1)
                ve.wait_ge(sem("joined"), 4 * n)
                ve.nop().then_inc(sem("h_ready"), 2)

            for g, parts in enumerate(STAGES):
                n = sum(p[2] for p in parts)
                ps = full(ve, ("cols", g))
                at = [0, 114, 202, 290][g]
                empty(ve.tensor_copy(cols[:, at:at + n], ps[:, 0:n]), ("cols", g))
            emptied(ve, *[("cols", g) for g in range(4)])
            norm(0, "norm_mix_pre")
            ve.wait_ge(sem("pos_landed"), 32)
            link(ve.tensor_copy(posf[:, :], posi[:, :]))
            link(TT(ang[:, :, :], bc(posf[:, :].unsqueeze(2), P, 4, 32), bc(const("inv").unsqueeze(1), P, 4, 32), mul))
            magic = 1.5 * 2.0 ** 23
            link(TS(angn[:, :, :], ang[:, :, :], 1.0 / (2 * np.pi), magic, mul, add))
            link(TS(angn[:, :, :], angn[:, :, :], magic, None, sub))
            two_pi = 2 * np.pi
            c1 = float(np.float32(6.28125))
            c2 = float((two_pi - c1) // 2.0 ** -19 * 2.0 ** -19)
            for part in (c1, c2, two_pi - c1 - c2):
                link(STT(out=ang[:, :, :], in0=angn[:, :, :], scalar=-part, in1=ang[:, :, :], op0=mul, op1=add))
            link(TS(ang[:, :, :], ang[:, :, :], 3.1415925, -3.1415925, ALU.min, mx_))
            link(TS(angn[:, :, :], ang[:, :, :], float(np.pi / 2), None, add))
            link(TS(cosd[:, :, 32:64], angn[:, :, :], float(np.pi), -two_pi, ALU.is_gt, mul))
            link(TT(angn[:, :, :], angn[:, :, :], cosd[:, :, 32:64], add))
            TS(angn[:, :, :], angn[:, :, :], 3.1415925, -3.1415925, ALU.min, mx_).then_inc(sem("angles"), 1)
            ve.wait_ge(sem("trig"), 2)
            link(ve.tensor_copy(cosd[:, :, 32:64], cosd[:, :, 0:32]))
            link(TS(sind[:, :, 0:32], sind[:, :, 32:64], -1.0, None, mul))
            for c in range(14):
                emptied(ve, ("rw", c))
            link(TT(dif[:, :, :], pr[:, :, 0:256], pr[:, :, 1:257], sub))
            for c in range(14):
                STT(out=pr[:, c, 1:257], in0=dif[:, c, :], scalar=pc("rw_mu", c), in1=pr[:, c, 1:257],
                    op0=mul, op1=add).then_inc(sem("shifted"), 1)
            ve.wait_ge(sem("shifted"), 14)
            r_, k_, v_ = pr[:, 0:4, 1:257], pr[:, 4:8, 1:257], pr[:, 8:12, 1:257]
            for p in range(4):
                ins = TS(kn[:, p, :], k_[:, p, :], pc("rw_k_k", p), None, mul)
            link(ins)
            TT(ex[:, :, :], kn[:, :, :], kn[:, :, :], mul).then_inc(sem("kk_squared"), 1)
            for p in range(4):
                ps = full(ve, ("ss", p))
                empty(TS(ex3[:, p, :], ps[:, 0:T], 1e-24, None, mx_), ("ss", p))
            for p in range(4):
                emptied(ve, ("ss", p))
            ve.nop().then_inc(sem("knorm_in"), 1)
            link(TS(om[:, :], pcs("rw_k_a", 4), -1.0, 1.0, mul, add))
            for p in range(4):
                emptied(ve, ("a", p), ("w", p))
            for p in range(4):
                TS(cc[:, p, :], av[:, p, :], pc("rw_k_a", p), om[:, p:p + 1], mul, add).then_inc(sem("ka"), 1)
            ve.wait_ge(sem("ka"), 4)
            link(TT(k_, k_, cc[:, :, :], mul))
            for p in range(4):
                ins = STT(out=ex2[:, p, :], in0=r_[:, p, :], scalar=pc("rw_r_k", p), in1=k_[:, p, :], op0=mul, op1=mul)
                ins.then_inc(sem("rk1"), 1)
            ve.wait_ge(sem("rk1"), 4)
            ve.nop().then_inc(sem("rk_ready"), 1)
            ve.wait_ge(sem("knorm_root"), 1)
            link(ve.reciprocal(ex[:, :, :], ex[:, :, :]))
            link(TT(kn[:, :, :], kn[:, :, :], ex[:, :, :], mul))
            link(TS(ld[:, :, :], ld[:, :, :], -float(np.exp(-0.5)), None, mul))
            for p in range(4):
                for n in range(2):
                    c = slice(P * n, P * n + P)
                    ins = ve.tensor_tensor_scan(cc[:, p, c], bc(const("ones")[:, 0:1], P, P), ld[:, p, c], 0.0, mul, add)
                    ins.then_inc(sem("scan"), 1)
            ve.wait_ge(sem("scan"), 8)
            link(ve.tensor_copy(fcol[:, :], cc[:, :, 191]))
            c4 = cc[:, :, :].rearrange("p a (n t) -> p (a n) t", n=2)
            mid = ar(25616, 8)
            link(ve.tensor_copy(mid, c4[:, :, 63]))
            link(TT(c4, c4, bc(mid.unsqueeze(2), P, 8, P), sub))
            link(TT(ld[:, :, :], cc[:, :, :], ld[:, :, :], sub))
            ve.nop().then_inc(sem("cum_ready"), 1)
            ve.nop().then_inc(sem("prev_ready"), 1)
            TT(fcol[:, :], fcol[:, :], cc[:, :, 127], add).then_inc(sem("fcol_in"), 1)
            emptied(ve, ("vT", 0), ("vT", 1))
            for p in range(4):
                ps = full(ve, ("bs", p))
                empty(TT(v_[:, p, :], v_[:, p, :], ps[:, 0:T], mul), ("bs", p))
            z_ = zr[:, :, :, 0:P]
            rr = zr[:, :, :, P:256]
            s4 = lambda a: a.rearrange("p a (n t) -> p a n t", n=2)
            ve.wait_ge(sem("e_done"), 3)
            link(TT(rr, s4(r_), s4(ex3[:, :, :]), mul))
            link(TT(ld[:, :, :], kn[:, :, :], ex[:, :, :], mul))
            link(TS(z_, s4(ld[:, :, :]), -1.0, None, mul))
            link(TT(kn[:, :, :], kn[:, :, :], av[:, :, :], mul))
            link(TT(bt[:, :, :, :], s4(kn[:, :, :]), s4(ex2[:, :, :]), mul))
            TT(kt[:, :, :, :], s4(k_), s4(ex2[:, :, :]), mul).then_inc(sem("decayed"), 1)
            strict, incl = const("strict"), const("incl")
            for n in range(2):
                if n == 0:
                    ve.wait_ge(sem("decayed"), 1)
                for hd in range(8):
                    ps = full(ve, ("m", n, hd))
                    if n:
                        if hd == 0:
                            full(ve, ("y", 0))
                    v = ps[:, :].rearrange("p (a b c) -> p a b c", a=2, b=2)
                    m = mats[:, hd, :, :].rearrange("p (a b) c -> p a b c", a=2)
                    link(TT(m[:, :, 0, :], v[:, :, 0, :], bc(strict.unsqueeze(1), P, 2, P), mul))
                    empty(TT(m[:, :, 1, :], v[:, :, 1, :], bc(incl.unsqueeze(1), P, 2, P), mul), ("m", n, hd))
                emptied(ve, *[("m", n, hd) for hd in range(8)])
                ve.nop().then_inc(sem("mats_ready"), 8)
                iv = inv.rearrange("p (a o) c -> p a o c", o=2)
                for o in range(2):
                    ps = full(ve, ("L", n, o))
                    empty(TT(iv[:, :, o, :], four(ps), bc(const("off0L").unsqueeze(1), P, 4, P), mul), ("L", n, o))
                emptied(ve, ("L", n, 0), ("L", n, 1))
                link(TT(inv[:, :, :], inv[:, :, :], bc(ident.unsqueeze(1), P, 8, P), add))
                link(TT(invT[:, :, :], mats[:, :, 0, :], bc(const("off0").unsqueeze(1), P, 8, P), mul))
                TT(invT[:, :, :], invT[:, :, :], bc(ident.unsqueeze(1), P, 8, P), add).then_inc(sem("inv_start"), 1)
                ve.wait_ge(sem("inv_start"), n + 1)
                for k in range(1, LEVELS):
                    for q in range(2):
                        for key, dst in ((("x", n, k, q), inv), (("xt", n, k, q), invT)):
                            ps = full(ve, ("xt", n, k, q))
                            ps = full(ve, key)
                            d = dst[:, 4 * q:4 * q + 4, :]
                            empty(TT(d, d, four(ps), add), key)
                        emptied(ve, ("x", n, k, q), ("xt", n, k, q))
                if n == 0:
                    ps = full(ve, ("st",))
                    empty(TT(s0[:, :, :], four(ps), bc(const("blk").unsqueeze(1), P, 4, P), mul), ("st",))
                    emptied(ve, ("st",))
                    ve.wait_ge(sem("f_done"), 1)
                    for p in range(4):
                        ins = TS(s0[:, p, :], s0[:, p, :], fcol[:, p:p + 1], None, mul)
                        ins.then_inc(sem("s0c"), 1)
                    ve.wait_ge(sem("s0c"), 4)
                    ve.nop().then_inc(sem("state_ready"), 1)

            def centre(rows_, n, w, eps, sqbuf, count):
                x = rows_[:, :, 0:n * w].rearrange("p i (a b) -> p i a b", a=n)
                sq = sqbuf[:, :, 0:n * w].rearrange("p i (a b) -> p i a b", a=n)
                for i in range(2):
                    ins = ve.tensor_reduce(mean[:, i, 0:n], x[:, i, :, :], AX.X, add)
                link(ins)
                link(TS(mean[:, :, 0:n], mean[:, :, 0:n], 1.0 / w, None, mul))
                for i in range(2):
                    link(TT(x[:, i, :, :], x[:, i, :, :], bc(mean[:, i, 0:n].unsqueeze(2), P, n, w), sub))
                for i in range(2):
                    link(TT(sq[:, i, :, :], x[:, i, :, :], x[:, i, :, :], mul))
                for i in range(2):
                    link(ve.tensor_reduce(var[:, i, 0:n], sq[:, i, :, :], AX.X, add))
                TS(var[:, :, 0:n], var[:, :, 0:n], 1.0 / w, eps, mul, add).then_inc(sem("gn_var"), 1)
                ve.wait_ge(sem("gn_root"), count)
                link(ve.reciprocal(rs8[:, :, 0:n], rs8[:, :, 0:n]))
                return x

            emptied(ve, ("y", 0), ("y", 1))
            x = centre(yrow, 8, 64, 64e-5, ar(5648, 2, 512), 1)
            for i in range(2):
                ins = TT(x[:, i, :, :], x[:, i, :, :], bc(rs8[:, i, 0:8].unsqueeze(2), P, 8, 64), mul)
                ins.then_inc(sem("yn"), 1)
            ve.wait_ge(sem("yn"), 2)
            ve.nop().then_inc(sem("y_rows"), 1)
            for i in range(2):
                ps = full(ve, ("yT", i))
                for p in range(4):
                    ins = TS(yrwT[:, p, P * i:P * i + P], ps[:, P * p:P * p + P], pc("rw_lnx_w", p), pc("rw_lnx_b", p),
                             mul, add)
                empty(ins, ("yT", i))
            emptied(ve, ("yT", 0), ("yT", 1))
            link(TT(yrwT[:, :, :], yrwT[:, :, :], v_, add))
            TT(yrwT[:, :, :], yrwT[:, :, :], gT[:, :, :], mul).then_inc(sem("yrwT_ready"), 1)

            def rope(x, n, tab, t1_, t2_, dst):
                for i in range(2):
                    c = bc(cosd[:, tab + i, :].unsqueeze(1), P, n, 64)
                    s1 = bc(sind[:, tab + i, 0:32].unsqueeze(1), P, n, 32)
                    s2 = bc(sind[:, tab + i, 32:64].unsqueeze(1), P, n, 32)
                    TT(t1_[:, i, :, :], x[:, i, :, :], c, mul)
                    TT(t2_[:, i, :, 0:32], x[:, i, :, 32:64], s1, mul)
                    link(TT(t2_[:, i, :, 32:64], x[:, i, :, 0:32], s2, mul))
                for i in range(2):
                    link(TT(dst[:, i, :, :], t1_[:, i, :, :], t2_[:, i, :, :], add))

            h8 = lambda a, n=8: a[:, :, :].rearrange("p i (a b) -> p i a b", a=n)
            full(ve, ("yT", 0))
            full(ve, ("yT", 1))
            emptied(ve, ("rq", 0), ("rq", 1), ("rk", 0), ("rk", 1))
            for x, g in ((qr, "gq"), (kr, "gk")):
                rope(h8(x), 8, 0, h8(ro1), h8(ro2), h8(x))
                ins = TT(h8(x), h8(x), bc(const(g).unsqueeze(1).unsqueeze(3), P, 2, 8, 64), mul)
                ins.then_inc(sem("qk_rope"), 1)
            for g in range(2):
                ps = full(ve, ("R", g))
                empty(TT(rst[:, 2 * g:2 * g + 2, :], four(ps, 2), bc(const("blkret").unsqueeze(1), P, 2, 256), mul),
                      ("R", g))
            for n in range(2):
                for o in range(2):
                    ps = full(ve, ("s", n, o))
                    if n:
                        full(ve, ("o", 0, 0))
                        full(ve, ("o", 0, 1))
                    for p in range(4):
                        hd = 2 * p + o
                        ins = STT(out=sT[:, hd, :], in0=ps[:, P * p:P * p + P], scalar=float(GAMMA[hd] ** -128.0),
                                  in1=incl, op0=mul, op1=mul)
                    empty(ins, ("s", n, o))
                for g in range(2):
                    ps = full(ve, ("o", n, g))
                    empty(ve.tensor_copy(orow[:, n, 512 * g:512 * g + 512], ps[:, :]), ("o", n, g))
            emptied(ve, ("o", 1, 0), ("o", 1, 1), ("o", 0, 0), ("o", 0, 1))
            x = centre(orow, 8, P, 1e-5, ar(2048, 2, D), 2)
            for i in range(2):
                link(TT(x[:, i, :, :], x[:, i, :, :], bc(rs8[:, i, 0:8].unsqueeze(2), P, 8, P), mul))
            for f in range(2):
                for i in range(2):
                    emptied(ve, ("rg", f, i))
            TT(orow[:, :, :], orow[:, :, :], gr[:, :, :], mul).then_inc(sem("o_rows"), 1)
            for f in range(4):
                for i in range(2):
                    emptied(ve, ("rs", f, i))
            for i in range(2):
                for q in range(2):
                    full(ve, ("oT", i, q))
            for i in range(2):
                for f in range(2):
                    c = slice(512 * f, 512 * f + 512)
                    ps = full(ve, ("brw", i, f))
                    empty(TT(mrow[:, i, c], ps[:, :], sg[:, i, 0, c], mul), ("brw", i, f))
            emptied(ve, *[("brw", i, f) for i in range(2) for f in range(2)])
            for i in range(2):
                for f in range(2):
                    c = slice(512 * f, 512 * f + 512)
                    ps = full(ve, ("bret", i, f))
                    empty(TT(mtmp, ps[:, :], sg[:, i, 1, c], mul), ("bret", i, f))
                    emptied(ve, ("bret", i, f))
                    link(TT(mrow[:, i, c], mrow[:, i, c], mtmp, add))
            ve.nop().then_inc(sem("merged"), 1)
            post_norm("wo", 1)
            norm(1, "norm_ffn_pre")
            for j in range(11):
                b = j % 2
                for c in range(4):
                    ch = 2 * j + c % 2 + 22 * (c // 2)
                    ps = full(ve, ("up", j, c))
                    ve.wait_ge(sem("tap0"), 4 * j + c + 1)
                    for tap in (1, 0):
                        sft = 2 - tap
                        a = acc[:, b, c, sft:T]
                        ins = STT(out=a, in0=ps[:, 0:T - sft], scalar=fcw(tap, ch), in1=a, op0=mul, op1=add)
                        if tap:
                            link(ins)
                    empty(ins, ("up", j, c))
                for c in range(2):
                    ve.wait_ge(sem("gelu"), 2 * j + c + 1)
                    emptied(ve, ("up", j, c + 2))
                    TT(actT[:, 2 * j + c, :], acc[:, b, c, :], acc[:, b, 2 + c, :], mul).then_inc(sem("act_ready"), 1)
            post_norm("dn", 2)
            norm(2, "ssm_norm_w_2")
            for c in range(24):
                ps = full(ve, ("xbc", c))
                ve.wait_ge(sem("stap0"), c + 1)
                for sft in (1, 2, 3):
                    a = cacc[:, c % 4, sft:T]
                    ins = STT(out=a, in0=ps[:, 0:T - sft], scalar=scw(3 - sft, c), in1=a, op0=mul, op1=add)
                    if sft < 3:
                        link(ins)
                empty(ins, ("xbc", c))
            ps = full(ve, ("dt",))
            ve.wait_ge(sem("rowp_landed"), 96)
            d2 = ps[:, 0:64].rearrange("p (a b) -> p a b", a=2)
            empty(TT(dtv[:, :, :], d2, bc(dtb.unsqueeze(1), P, 2, 32), add), ("dt",))
            emptied(ve, ("dt",))
            link(TS(acs[:, :, :], dtv[:, :, :], -1.0, None, mul))
            TT(adt[:, :, :], dtv[:, :, :], acs[:, :, :], ALU.min).then_inc(sem("dt_in"), 1)
            link(TS(dtv[:, :, :], dtv[:, :, :], 0.0, None, mx_))
            ve.wait_ge(sem("dt_log"), 1)
            link(TT(dtv[:, :, :], dtv[:, :, :], adt[:, :, :], add))
            link(TS(arow, arow, -1.0, None, mul))
            TT(adt[:, :, :], dtv[:, :, :], bc(arow.unsqueeze(1), P, 2, 32), mul).then_inc(sem("adt_ready"), 1)
            ps = full(ve, ("ac",))
            link(ve.tensor_copy(acs[:, :, :], ps[:, 0:64].rearrange("p (a b) -> p a b", a=2)))
            empty(TT(tot, ps[:, 64:96], acs[:, 0, :], sub), ("ac",))
            emptied(ve, ("ac",))
            ve.nop().then_inc(sem("dte_in"), 1)
            hv = lambda a: a.rearrange("p (a b) -> p a b", a=32)
            for i in range(2):
                emptied(ve, *[("xsT", i, q) for q in range(4)])
                TT(hv(xd[:, i, :]), hv(xs[:, i, :]), bc(dtv[:, i, :].unsqueeze(2), P, 32, 64), mul) \
                    .then_inc(sem("xd_ready"), 1)
                if i == 0:
                    ve.wait_ge(sem("dte_done"), 2)
                    ve.wait_ge(sem("xd_ready"), 1)
                    TT(hv(xdd[:]), hv(xd[:, 0, :]), bc(dte.unsqueeze(2), P, 32, 64), mul).then_inc(sem("xd_ready"), 1)
            for i in range(2):
                link(TT(hv(xs[:, i, :]), hv(xs[:, i, :]), bc(dsk_.unsqueeze(2), P, 32, 64), mul))
            for n in range(2):
                ps = full(ve, ("cb", n))
                empty(TT(cbm[:, n, :].rearrange("p (a b) -> p a b", a=4), four(ps), bc(incl.unsqueeze(1), P, 4, P), mul),
                      ("cb", n))
            emptied(ve, ("cb", 0), ("cb", 1))

            def segs(z):
                n, u = divmod(z, 8)
                ps = full(ve, ("bc", n, u))
                if z >= 2:
                    ve.wait_ge(sem("wT_ready"), z - 1)
                for e in range(4):
                    hd = 4 * u + e
                    ins = TS(eT2[:, z % 2, P * e:P * e + P], ps[:, P * e:P * e + P], acs[:, n, hd:hd + 1], 0.0, sub, ALU.min)
                empty(ins, ("bc", n, u))
                emptied(ve, ("bc", n, u))
                ve.nop().then_inc(sem("seg_ready"), 1)

            def weigh(z):
                n, u = divmod(z, 8)
                g = u // 2
                ve.wait_ge(sem("seg_exp"), z + 1)
                if z >= 4:
                    zz = (z // 2) - 2
                    full(ve, ("yd", zz // 4, zz % 4))
                TT(wT[:, g % 2, 4 * (u % 2):4 * (u % 2) + 4, :], eT2[:, z % 2, :].rearrange("p (a b) -> p a b", a=4),
                   bc(cbm[:, n, P * g:P * g + P].unsqueeze(1), P, 4, P), mul).then_inc(sem("wT_ready"), 1)

            def join(z):
                n, g = divmod(z, 4)
                c = slice(512 * g, 512 * g + 512)
                ps = full(ve, ("yd", n, g))
                empty(TT(xs[:, n, c], xs[:, n, c], ps[:, :], add), ("yd", n, g))
                if n:
                    ps = full(ve, ("yo", g))
                    e8 = lambda a: a.rearrange("p (a b) -> p a b", a=8)
                    empty(TT(e8(xdd[:, c]), e8(ps[:, :]), bc(eac[:, 8 * g:8 * g + 8].unsqueeze(2), P, 8, 64), mul),
                          ("yo", g))
                    emptied(ve, ("yo", g), ("yd", n, g))
                    link(TT(xs[:, n, c], xs[:, n, c], xdd[:, c], add))

            for g in range(4):
                full(ve, ("sst", g))
            segs(0)
            for z in range(16):
                if z + 1 < 16:
                    segs(z + 1)
                weigh(z)
                if z % 2 == 1 and z >= 3:
                    join(z // 2 - 1)
            join(7)
            emptied(ve, *[("yd", n, g) for n in range(2) for g in range(4)])
            for j in range(4):
                for i in range(2):
                    emptied(ve, ("z", j, i))
            for i in range(2):
                TT(xs[:, i, :], xs[:, i, :], zrow[:, i, :], mul).then_inc(sem("yz_ready"), 1)
            ve.wait_ge(sem("yg_root"), 1)
            link(ve.reciprocal(var[:, :, 0:4], var[:, :, 0:4]))
            for i in range(2):
                v = xs[:, i, :].rearrange("p (a b) -> p a b", a=4)
                TT(v, v, bc(var[:, i, 0:4].unsqueeze(2), P, 4, 512), mul).then_inc(sem("yg_rows"), 1)
            for i in range(2):
                for q in range(4):
                    ps = full(ve, ("gT", i, q))
                    a = colat[("ssm_gnorm_w_2", 0)] + 4 * q
                    empty(TT(ygT[:, 4 * q:4 * q + 4, P * i:P * i + P], four(ps), bc(cols[:, a:a + 4].unsqueeze(2), P, 4, P),
                             mul), ("gT", i, q))

            def plain_join(key):
                for i in range(2):
                    for f in range(2):
                        c = slice(512 * f, 512 * f + 512)
                        ps = full(ve, (key, i, f))
                        empty(TT(h[:, i, c], h[:, i, c], ps[:, :], add), (key, i, f))
                emptied(ve, *[(key, i, f) for i in range(2) for f in range(2)])
                ve.nop().then_inc(sem("h_ready"), 2)

            def embed(m):
                n = 3 if m == 0 else 5
                norm(n, "ple_norm_w_2", 8 * m)
                for f in range(2):
                    for i in range(2):
                        z = 2 * f + i
                        c = slice(512 * f, 512 * f + 512)
                        emptied(ve, ("pg", m, f, i))
                        ps = full(ve, ("pp", m, f, i))
                        empty(TT(tmph[:, i, c], psg[:, z % 2, :], ps[:, :], mul), ("pp", m, f, i))
                        emptied(ve, ("pp", m, f, i))
                        ve.nop().then_inc(sem("ple_used"), 1)
                        TT(h[:, i, c], h[:, i, c], tmph[:, i, c], add).then_inc(sem("out_ready") if m else sem("ple_joined"), 1)
                if m == 0:
                    ve.wait_ge(sem("ple_joined"), 4)
                    ve.nop().then_inc(sem("h_ready"), 2)

            plain_join("so")
            embed(0)
            norm(4, "attn_norm_w_2")

            def head_norm(x, n, w, t_, count):
                for i in range(2):
                    link(TT(t_[:, i, :, :], x[:, i, :, :], x[:, i, :, :], mul))
                for i in range(2):
                    link(ve.tensor_reduce(var[:, i, 0:n], t_[:, i, :, :], AX.X, add))
                TS(var[:, :, 0:n], var[:, :, 0:n], 1.0 / 64, 1e-6, mul, add).then_inc(sem("hn_in"), 1)
                ve.wait_ge(sem("hn_root"), count)
                link(ve.reciprocal(rs8[:, :, 0:n], rs8[:, :, 0:n]))
                for i in range(2):
                    link(TT(x[:, i, :, :], x[:, i, :, :], bc(rs8[:, i, 0:n].unsqueeze(2), P, n, 64), mul))
                for i in range(2):
                    link(TT(x[:, i, :, :], x[:, i, :, :], bc(w.unsqueeze(1), P, n, 64), mul))

            emptied(ve, ("kv", 0), ("kv", 1))
            kx = kvr[:, :, 0:256].rearrange("p i (a b) -> p i a b", a=4)
            cut = lambda a, n: a[:, :, 0:64 * n].rearrange("p i (a b) -> p i a b", a=n)
            head_norm(kx, 4, kn_, cut(at1, 4), 1)
            rope(kx, 4, 2, cut(at1, 4), cut(at2, 4), cut(akr, 4))
            ve.nop().then_inc(sem("ak_rows"), 1)
            emptied(ve, *[("ain", j, i) for j in range(2) for i in range(2)])
            head_norm(h8(aq, 16), 16, qn, h8(at1, 16), 2)
            rope(h8(aq, 16), 16, 2, h8(at1, 16), h8(at2, 16), h8(aq, 16))
            for i in range(2):
                for u in range(2):
                    for o in range(2):
                        src = aq[:, i, 512 * u + 256 * o:512 * u + 256 * o + 256].rearrange("p (g d) -> p g d", g=4)
                        dst = aqr[:, i, 512 * u:512 * u + 512].rearrange("p (g o d) -> p g o d", g=4, o=2)[:, :, o, :]
                        ins = ve.tensor_copy(dst, src)
            ins.then_inc(sem("aq_rows"), 1)

            def softmax_in(z):
                n, u, o, gh = UNITS[z]
                nh, w = (4, P) if n == 0 else (2, 2 * P)
                hd = 8 * u + 4 * o + 2 * gh
                ps = full(ve, ("as", z))
                if z >= 2:
                    full(ve, ("eT", z - 2))
                s = asb[:, z % 2, :].rearrange("p (a b) -> p a b", a=nh)
                link(TS(asb[:, z % 2, :], ps[:, :], 0.125, None, mul))
                empty(TT(s, s, bc(const(f"att{n}").unsqueeze(1), P, nh, w), add), ("as", z))
                emptied(ve, ("as", z))
                m = mx[:, z % 2, 0:nh]
                link(ve.tensor_reduce(m, s, AX.X, mx_))
                link(TT(m, m, sinks[:, hd:hd + nh], mx_))
                link(TT(dsk[:, z % 2, 0:nh], sinks[:, hd:hd + nh], m, sub))
                TT(s, s, bc(m.unsqueeze(2), P, nh, w), sub).then_inc(sem("sub_ready"), 1)

            def softmax_out(z):
                n, u, o, gh = UNITS[z]
                nh, w = (4, P) if n == 0 else (2, 2 * P)
                hd = 8 * u + 4 * o + 2 * gh
                s = asb[:, z % 2, :].rearrange("p (a b) -> p a b", a=nh)
                ve.wait_ge(sem("exps"), z + 1)
                ve.wait_ge(sem("sink_exp"), z + 1)
                link(ve.tensor_reduce(den[:, z, 0:nh], s, AX.X, add))
                link(TT(den[:, z, 0:nh], den[:, z, 0:nh], dsk[:, z % 2, 0:nh], add))
                link(ve.reciprocal(den[:, z, 0:nh], den[:, z, 0:nh]))
                ps = full(ve, ("ao", z))
                dst = ao[:, n, 64 * hd:64 * hd + 64 * nh].rearrange("p (a b) -> p a b", a=nh)
                empty(TT(dst, ps[:, 0:64 * nh].rearrange("p (a b) -> p a b", a=nh),
                         bc(den[:, z, 0:nh].unsqueeze(2), P, nh, 64), mul), ("ao", z))

            softmax_in(0)
            for z in range(len(UNITS)):
                if z + 1 < len(UNITS):
                    softmax_in(z + 1)
                softmax_out(z)
            emptied(ve, *[("ao", z) for z in range(len(UNITS))])
            emptied(ve, *[("ain", 2 + j, i) for j in range(2) for i in range(2)])
            TT(ao[:, :, :], ao[:, :, :], ag[:, :, :], mul).then_inc(sem("ao_rows"), 1)
            plain_join("fo")
            embed(1)


def kernel(**inputs):
    import concourse.bacc as bacc
    from concourse.bass_utils import run_bass_kernel_spmd as run

    nc = bacc.Bacc("TRN2", target_bir_lowering=False, num_devices=1)
    where, table = constants()
    arrays, io = {}, {}
    for name, a in list(inputs.items()) + [("table", table)]:
        a = np.ascontiguousarray(a)
        arrays[f"in_{name}"] = a
        io[name] = nc.dram_tensor(f"in_{name}", a.shape, mybir.dt.from_np(a.dtype), kind="ExternalInput").ap()
    out = nc.dram_tensor("out", (1, T, D), F32, kind="ExternalOutput").ap()
    build(nc, io, out, where, table.shape[1])
    r = run(nc, [arrays], core_ids=[0])
    return r.results[0]["out"]
```

```python
from contextlib import ExitStack

import numpy as np
import concourse.bass as bass
from concourse import mybir

F32 = mybir.dt.float32
F32R = mybir.dt.float32r
I32 = mybir.dt.int32
ALU = mybir.AluOpType
ACT = mybir.ActivationFunctionType
AX = mybir.AxisListType

P = 128
D = 1024
KT = D // P
T = 256
NEG = -1.0e30
GAMMA = [1.0 - 2.0 ** (-5 - h) for h in range(8)]
LEVELS = 7


def constants():
    r = np.arange(P)
    row, col = r[:, None], r[None, :]
    parts = {}
    parts["ident"] = (row == col)
    parts["incl"] = (row <= col)
    parts["strict"] = (row < col)
    parts["ones"] = np.ones((P, P))
    parts["blk"] = (row // 64 == col // 64)
    parts["blkret"] = np.repeat(parts["blk"][:, ::64], P, axis=1)
    for k in range(LEVELS):
        same = (row >> (k + 1)) == (col >> (k + 1))
        parts[f"off{k}"] = same & (((col >> k) & 1) == 1) & (((row >> k) & 1) == 0)
    parts["off0L"] = parts["off0"].T
    causal = np.where(col <= row, 0.0, NEG)
    before = np.where(col > row, 0.0, NEG)
    parts["att0"] = causal
    parts["att1"] = np.concatenate([before, causal], axis=1)
    lg = np.log1p(-np.exp2(-5.0 - np.arange(8)))
    parts["gq"] = np.exp((r[:, None] + 1.0) * lg[None])
    parts["gk"] = np.exp((127.0 - r[:, None]) * lg[None]) * 0.125
    inv = (10000.0 ** (-np.arange(32) / 32)).astype(np.float32)
    parts["inv"] = np.broadcast_to(inv[None], (P, 32))
    where, at = {}, 0
    for n, a in parts.items():
        where[n] = (at, a.shape[1])
        at += a.shape[1]
    return where, np.concatenate([np.asarray(a, np.float32) for a in parts.values()], axis=1)


def weight_units():
    out = []

    def turned(name, w, c0, cols):
        for j in range(cols // 256):
            out.append((f"{name}{j}", w, 0, KT, c0 + 256 * j, 256))

    def rows(name, w, c0):
        for half in range(2):
            out.append((f"{name}.{half}", w, 4 * half * P, 4, c0, 512))

    def deep(name, w, n):
        for t in range(0, n, 2):
            out.append((f"{name}{t // 2}", w, t * P, 2, 0, D))

    turned("rw", "w_in", 0, 1792)
    for n, name in enumerate(["q", "k", "v0", "v1", "g0", "g1", "s0", "s1", "s2", "s3"]):
        rows("r" + name, "w_in", 1792 + 512 * n)
    deep("brw", "w_branch_rw", 4)
    deep("bret", "w_branch_ret", 8)
    deep("wo", "w_out", 8)
    for j in range(11):
        for part, c0 in (("g", 0), ("v", 2816)):
            out.append((f"up{j}{part}", "ffn_w_up", 0, KT, c0 + 256 * j, 256))
    deep("dn", "ffn_w_down", 22)
    turned("xbc", "ssm_in_w_2", 2048, 3072)
    out.append(("dt", "ssm_in_w_2", 0, KT, 5120, 32))
    for j in range(4):
        rows(f"z{j}", "ssm_in_w_2", 512 * j)
    deep("so", "ssm_out_w_2", 16)

    def embed(m):
        out.append((f"pp{m}", f"ple_proj_w_2:{m}", 0, 2, 0, D))
        rows(f"pg{m}0", f"ple_gate_w_2:{m}", 0)
        rows(f"pg{m}1", f"ple_gate_w_2:{m}", 512)

    embed(0)
    rows("kv", "kv_w_2", 0)
    for j in range(4):
        rows(f"ain{j}", "attn_in_w_2", 512 * j)
    deep("ao", "attn_out_w_2", 8)
    embed(1)
    return out


LOADS = 3
PARTS = 2
SLOT = 2048
ARENA = 26128

STAGES = [
    [("norm_mix_pre", 0, 8), ("norm_ffn_pre", 0, 8), ("ssm_norm_w_2", 0, 8), ("ple_norm_w_2", 0, 8),
     ("kv_norm_w_2", 0, 8), ("attn_norm_w_2", 0, 8), ("ple_norm_w_2", 8, 8), ("rw_mu", 0, 14), ("rw_w0", 0, 4),
     ("rw_a0", 0, 4), ("rw_k_k", 0, 4), ("rw_k_a", 0, 4), ("rw_r_k", 0, 4), ("rw_lnx_w", 0, 4),
     ("rw_lnx_b", 0, 4), ("ssm_gnorm_w_2", 0, 16)],
    [("ffn_conv_w", 0, 88)],
    [("ffn_conv_w", 88, 44), ("ffn_conv_b", 0, 44)],
    [("ssm_conv_w_2", 0, 96), ("ssm_conv_b_2", 0, 24)],
]


def build(nc, io, out, where, ncols):
    ctx = ExitStack()
    with ctx:
        def sb(name, shape, dt=F32):
            return ctx.enter_context(nc.sbuf_tensor(name, shape, dt))

        sems = {}

        def sem(name):
            if name not in sems:
                sems[name] = ctx.enter_context(nc.semaphore(name))
            return sems[name]

        consts = sb("consts", [P, ncols])
        loaded = sb("loaded", [P, LOADS * SLOT])
        upper = sb("upper", [P, PARTS * SLOT], F32R)
        lower = sb("lower", [P, PARTS * SLOT], F32R)
        cols = sb("cols", [P, 512])
        lora = sb("lora", [P, 2, 512])
        postw = sb("postw", [P, D])
        rowp = sb("rowp", [P, 64 + 64 + 16 + 32 * 3])
        h = sb("h", [P, 2, D])
        xT = (sb("xT_upper", [P, KT, T], F32R), sb("xT_lower", [P, KT, T], F32R))
        small = sb("small", [P, 1400])
        posi = sb("posi", [P, 4], I32)
        arena_at = (nc.sbuf_base + 31) // 32 * 32
        arena = sb("arena", [P, ARENA])
        split_arena = nc.alloc_sbuf_tensor_at("split_arena", [P, ARENA], F32R, offset=arena_at)
        PS = [ctx.enter_context(nc.psum_tensor(f"bank{b}", [P, 512], F32)) for b in range(8)]

        def const(name):
            a, n = where[name]
            return consts[:, a:a + n]

        ident = const("ident")

        def ar(at, *shape, of=arena):
            n = int(np.prod(shape))
            v = of[:, at:at + n]
            if len(shape) == 2:
                v = v.rearrange("p (a b) -> p a b", a=shape[0])
            if len(shape) == 3:
                v = v.rearrange("p (a b c) -> p a b c", a=shape[0], b=shape[1])
            if len(shape) == 4:
                v = v.rearrange("p (a b c d) -> p a b c d", a=shape[0], b=shape[1], c=shape[2])
            return v

        def sm(at, *shape):
            n = int(np.prod(shape))
            v = small[:, at:at + n]
            if len(shape) == 2:
                v = v.rearrange("p (a b) -> p a b", a=shape[0])
            if len(shape) == 3:
                v = v.rearrange("p (a b c) -> p a b c", a=shape[0], b=shape[1])
            return v

        def two(at, at2, *shape):
            return ar(at, *shape, of=split_arena), ar(at2, *shape, of=split_arena)

        hs = ar(0, 2, D)
        tmph = hs
        pr = ar(2048, 14, 257)
        dif = ar(5648, 14, 256)
        ld, av, kn = ar(5648, 4, 256), ar(6672, 4, 256), ar(7696, 4, 256)
        qr, kr = ar(9232, 2, 512), ar(10256, 2, 512)
        cc, gT = ar(11280, 4, 256), ar(12304, 4, 256)
        zr = ar(13328, 4, 2, 256)
        bt, kt = ar(15376, 4, 2, P), ar(16400, 4, 2, P)
        vrow, yrow = ar(17424, 2, 512), ar(5648, 2, 512)
        krow, brow, sa, rhs = ar(0, 512), ar(512, 512), ar(1024, 512), ar(1536, 512)
        s0 = ar(18448, 4, P)
        stage = ar(18448, 4, P)
        mats = ar(18960, 8, 4, P)
        ex, ex2, ex3 = ar(18960, 4, 256), ar(19984, 4, 256), ar(21008, 4, 256)
        lor = ar(22032, 2, 256)
        inv, invT, t1, lk = ar(23056, 8, P), ar(24080, 8, P), ar(25104, 8, P), ar(11280, 8, P)
        mid = ar(25616, 8)
        yrw = ar(16400, 4, T)
        yrwT = two(15376, 12304, 4, T)
        vr, gr = h, ar(19472, 2, D)
        sg = ar(21520, 2, 2, D)
        qT, kTr = ar(5648, 4, T), ar(6672, 4, T)
        sT = ar(7696, 8, P)
        rst = ar(11280, 4, T)
        orow = ar(13328, 2, D)
        oT = two(2048, 4096, KT, T)
        ro = lora
        mrow, mT = ar(13328, 2, D), two(9232, 11280, KT, T)
        mtmp = ar(17424, 512)
        actT = two(2048, 7680, 22, T)
        acc = ar(13312, 2, 4, T)
        zrow = ar(2048, 2, 2048)
        xbc = ar(6144, 24, T)
        cbm = ar(6144, 2, 512)
        xs = ar(12288, 2, 2048)
        cacc = ar(16384, 4, T)
        xd = ar(16384, 2, 2048)
        xdd = ar(20480, 2048)
        wT = ar(22528, 2, 8, P)
        eT2 = ar(24576, 2, 512)
        bR = ar(25600, 512)
        ss0 = ar(0, 4, 512)
        yg = ar(2048, 2, 4, 512)
        ygT = two(16384, 20480, 16, T)
        prow, pT = ar(2048, 2, T), two(2560, 3072, 2, T)
        psg = ar(3584, 2, 512)
        xT2 = two(20480, 22528, KT, T)
        kvr = ar(4096, 2, 512)
        aq, ag = ar(5120, 2, D), ar(7168, 2, D)
        at1, at2 = ar(9216, 2, D), ar(11264, 2, D)
        aqr = ar(13312, 2, D)
        aqT = ar(15360, 2, 4, T)
        akT = ar(17408, 2, T)
        akr = ar(17920, 2, T)
        asb = ar(18432, 2, 512)
        aeT = ar(20480, 2, 512)
        ao = ar(21504, 2, D)
        aoT = two(9216, 11264, KT, T)
        ssq, rstd = sm(0, 4), sm(4, 4)
        mean, var, rs8 = sm(8, 2, 32), sm(72, 2, 32), sm(136, 2, 32)
        dtv, adt, acs = sm(200, 2, 32), sm(264, 2, 32), sm(328, 2, 32)
        tot, dte, eac = sm(392, 32), sm(424, 32), sm(456, 32)
        arow = sm(488, 32)
        ang, cosd, sind = sm(520, 4, 32), sm(648, 4, 64), sm(904, 4, 64)
        angn = sm(1160, 4, 32)
        posf = sm(1288, 4)
        fcol = sm(1292, 4)
        om = sm(1296, 4)
        mx, den, dsk = sm(1300, 2, 4), sm(1308, 12, 4), sm(1356, 2, 4)
        eps6 = sm(1364, 1)
        qn, kn_, sinks, dtb, alog, dsk_ = (rowp[:, 0:64], rowp[:, 64:128], rowp[:, 128:144], rowp[:, 144:176],
                                           rowp[:, 176:208], rowp[:, 208:240])

        colat, at = {}, 0
        for g, parts in enumerate(STAGES):
            at = [0, 114, 202, 290][g]
            for name, r0, n in parts:
                colat[(name, r0)] = at
                at += n

        def pc(name, j, r0=0):
            a = colat[(name, r0)] + j
            return cols[:, a:a + 1]

        def pcs(name, n, r0=0):
            a = colat[(name, r0)]
            return cols[:, a:a + n]

        def fcw(tap, c):
            return cols[:, 114 + 44 * tap + c:115 + 44 * tap + c]

        def fcb(c):
            return cols[:, 202 + 44 + c:203 + 44 + c]

        def scw(tap, c):
            return cols[:, 290 + 24 * tap + c:291 + 24 * tap + c]

        def scb(c):
            return cols[:, 290 + 96 + c:291 + 96 + c]

        units = weight_units()
        index = {u[0]: n for n, u in enumerate(units)}
        unit_landed = [sem(f"unit_landed{s}") for s in range(LOADS)]
        uppers, lowers = sem("unit_uppers"), sem("unit_lowers")
        units_used, used_count = sem("units_used"), [0]
        unit_done = {}

        def part(of, slots, n):
            nk, width = units[n][3], units[n][5]
            at = (n % slots) * SLOT
            return of[:, at:at + nk * width]

        def tiles(ap, n):
            return ap.rearrange("p (k c) -> p k c", k=units[n][3])

        def part_free(eng, n):
            if n >= PARTS:
                eng.wait_ge(*unit_done[n - PARTS])

        psum_full = [sem(f"psum_full{b}") for b in range(8)]
        psum_emptied = [sem(f"psum_emptied{b}") for b in range(8)]
        uses, use_of = [0] * 8, {}

        def take(pe, key, bank):
            if uses[bank]:
                pe.wait_ge(psum_emptied[bank], uses[bank])
            uses[bank] += 1
            use_of[key] = (bank, uses[bank])
            return PS[bank]

        def fill(ins, key):
            ins.then_inc(psum_full[use_of[key][0]], 1)

        def full(eng, key):
            bank, n = use_of[key]
            eng.wait_ge(psum_full[bank], n)
            return PS[bank]

        def empty(ins, key):
            ins.then_inc(psum_emptied[use_of[key][0]], 1)

        def emptied(eng, *keys):
            for key in keys:
                bank, n = use_of[key]
                eng.wait_ge(psum_emptied[bank], n)

        NORMS = ["norm_mix_pre", "norm_ffn_pre", "ssm_norm_w_2", "ple_norm_w_2", "attn_norm_w_2", "ple_norm_w_2"]
        norm_keys = lambda n: [("nT", n, i, q) for i in range(2) for q in range(2)]
        UNITS = [(0, u, o, 0) for u in range(2) for o in range(2)] + \
                [(1, u, o, g) for u in range(2) for o in range(2) for g in range(2)]
        HR = {1: 2, 2: 4, 3: 6, 4: 8, 5: 10}
        block = ctx.enter_context(nc.Block())

        @block.tensor
        def _(pe):
            mm = pe.matmul

            def turns(key, bank, ins):
                ps = take(pe, key, bank)
                for j, a in enumerate(ins):
                    m, n = a.shape
                    last = pe.transpose(ps[0:n, j * P:j * P + m], a, ident[0:m, 0:m])
                fill(last, key)

            def norm_turns(n):
                for i in range(2):
                    pe.wait_ge(sem("rows_scaled"), 2 * n + i + 1)
                    for q in range(2):
                        turns(("nT", n, i, q), 4 + 2 * i + q, [hs[:, i, P * (4 * q + j):P * (4 * q + j + 1)]
                                                               for j in range(4)])

            def mm3(out, a, b, start, stop):
                mm(out, a[0], b[0], start=start, stop=False)
                mm(out, a[0], b[1], start=False, stop=False)
                return mm(out, a[1], b[0], start=False, stop=stop)

            def unit(name):
                n = index[name]
                pe.wait_ge(lowers, n + 1)
                return tiles(part(upper, PARTS, n), n), tiles(part(lower, PARTS, n), n)

            def both(x, *at):
                return x[0][at], x[1][at]

            def used(name, last=None, key=None):
                if key is None:
                    used_count[0] += 1
                    last.then_inc(units_used, 1)
                    unit_done[index[name]] = (units_used, used_count[0])
                else:
                    unit_done[index[name]] = (psum_full[use_of[key][0]], use_of[key][1])

            every = slice(None)

            def turned(name, keys, banks):
                w = unit(name)
                for c in range(2):
                    ps = take(pe, keys[c], banks[c])
                    for k in range(KT):
                        last = mm3(ps[:, 0:T], both(w, every, k, slice(c * P, c * P + P)), both(xT, every, k, every),
                                   k == 0, k == KT - 1)
                    fill(last, keys[c])
                used(name, key=keys[1])

            def deep_product(name, n, xt, key, banks):
                ps = {(i, f): take(pe, (key, i, f), banks + 2 * i + f) for i in range(2) for f in range(2)}
                for t in range(n):
                    if t % 2 == 0:
                        w = unit(f"{name}{t // 2}")
                    for i in range(2):
                        for f in range(2):
                            last = mm3(ps[i, f][:, :], both(xt, every, t, slice(i * P, i * P + P)),
                                       both(w, every, t % 2, slice(512 * f, 512 * f + 512)), t == 0, t == n - 1)
                            if t == n - 1:
                                fill(last, (key, i, f))
                    if t == n - 1:
                        used(f"{name}{t // 2}", key=(key, 1, 1))
                    elif t % 2:
                        used(f"{name}{t // 2}", last)

            def rows_half(name, half, ps, keys, x):
                w = unit(f"{name}.{half}")
                for i in range(2):
                    for k in range(4):
                        last = mm3(ps[i][:, :], both(x, every, 4 * half + k, slice(i * P, i * P + P)),
                                   both(w, every, k, every), half + k == 0, half == 1 and k == 3)
                    if half:
                        fill(last, keys[i])
                used(f"{name}.{half}", *((last,) if half == 0 else (None, keys[1])))

            def rows(name, keys, banks, x):
                ps = [take(pe, keys[i], banks[i]) for i in range(2)]
                for half in range(2):
                    rows_half(name, half, ps, keys, x)

            def xT_ready(n):
                pe.wait_ge(sem("xT_lower_ready"), 4 * (n + 1))

            pe.wait_ge(sem("consts_landed"), 16)
            norm_turns(0)
            pe.wait_ge(sem("stage_landed"), 16 * sum(len(s) for s in STAGES))
            for g, parts in enumerate(STAGES):
                n = sum(p[2] for p in parts)
                turns(("cols", g), g, [stage[0:n, g, :]])
            xT_ready(0)
            for j in range(7):
                turned(f"rw{j}", [("rw", 2 * j), ("rw", 2 * j + 1)], (2 * (j % 2), 2 * (j % 2) + 1))
            rows("rq", [("rq", i) for i in range(2)], (4, 5), xT)
            pe.wait_ge(sem("lora_in"), 2)
            pe.wait_ge(sem("shifted"), 14)
            pe.wait_ge(sem("lora_landed"), 48)
            for p in range(4):
                ps = take(pe, ("w", p), p % 2)
                fill(mm(ps[:, 0:T], lora[0:64, 0, P * p:P * p + P], lor[0:64, 0, :], start=True, stop=True), ("w", p))
                ps = take(pe, ("a", p), 2 + p % 2)
                fill(mm(ps[:, 0:T], lora[64:128, 0, P * p:P * p + P], pr[64:128, 12, 1:257],
                        start=True, stop=True), ("a", p))
                ps = take(pe, ("g", p), 4 + p % 2)
                fill(mm(ps[:, 0:T], lora[:, 1, P * p:P * p + P], lor[:, 1, :], start=True, stop=True), ("g", p))
            rows("rk", [("rk", i) for i in range(2)], (6, 7), xT)
            pe.wait_ge(sem("kk_squared"), 1)
            for p in range(4):
                ps = take(pe, ("ss", p), p)
                fill(mm(ps[:, 0:T], const("blk"), ex[:, p, :], start=True, stop=True), ("ss", p))
            for i in range(2):
                turns(("vT", i), 6 + i, [pr[:, 8 + p, 1 + P * i:1 + P * i + P] for p in range(4)])
            rows("rv0", [("rv", 0, i) for i in range(2)], (4, 5), xT)
            pe.wait_ge(sem("rk_ready"), 1)
            for p in range(4):
                ps = take(pe, ("bs", p), p)
                fill(mm(ps[:, 0:T], const("blk"), ex2[:, p, :], start=True, stop=True), ("bs", p))
            rows("rv1", [("rv", 1, i) for i in range(2)], (6, 7), xT)
            pe.wait_ge(sem("decayed"), 1)
            for n in range(2):
                if n == 0:
                    turns(("kbT", 0), 6, [kt[:, p, 0, :] for p in range(4)])
                    turns(("kbT", 1), 7, [bt[:, p, 0, :] for p in range(4)])
                for hd in range(8):
                    p, o = hd // 2, hd % 2
                    r = slice(64 * o, 64 * o + 64)
                    ps = take(pe, ("m", n, hd), hd % 4)
                    mm(ps[:, 0:256], bt[r, p, n, :], zr[r, p, n, :], start=True, stop=True)
                    fill(mm(ps[:, 256:512], kt[r, p, n, :], zr[r, p, n, :], start=True, stop=True), ("m", n, hd))
                for o in range(2):
                    r = slice(64 * o, 64 * o + 64)
                    ps = take(pe, ("L", n, o), 4 + o)
                    for p in range(4):
                        last = mm(ps[:, P * p:P * p + P], zr[r, p, n, 0:P], bt[r, p, n, :], start=True, stop=True)
                    fill(last, ("L", n, o))
                pe.wait_ge(sem("inv_start"), n + 1)
                for k in range(1, LEVELS):
                    for q in range(2):
                        pe.wait_ge(sem("lk_ready"), 12 * n + 2 * (k - 1) + q + 1)
                        if k > 1:
                            emptied(pe, ("x", n, k - 1, q), ("xt", n, k - 1, q))
                        ps = take(pe, ("t1", n, k, q), 4 + q)
                        for e in range(4):
                            last = mm(ps[:, P * e:P * e + P], lk[:, 4 * q + e, :], inv[:, 4 * q + e, :],
                                      start=True, stop=True)
                        fill(last, ("t1", n, k, q))
                    for q in range(2):
                        emptied(pe, ("t1", n, k, q))
                        for key, a, b, bank in ((("x", n, k, q), invT, t1, 2 * q), (("xt", n, k, q), t1, invT, 2 * q + 1)):
                            ps = take(pe, key, bank)
                            for e in range(4):
                                hd = 4 * q + e
                                last = mm(ps[:, P * e:P * e + P], a[:, hd, :], b[:, hd, :], start=True, stop=True)
                            fill(last, key)
                emptied(pe, ("vT", 0), ("vT", 1))
                if n:
                    pe.wait_ge(sem("state_ready"), 1)
                ps = take(pe, ("rhs", n), 6)
                for p in range(4):
                    if n:
                        mm(ps[:, P * p:P * p + P], zr[:, p, n, 0:P], s0[:, p, :], start=True, stop=False)
                    for o in range(2):
                        hd = 2 * p + o
                        last = mm(ps[:, 64 * hd:64 * hd + 64], mats[:, hd, 2, :], vrow[:, n, 64 * hd:64 * hd + 64],
                                  start=(n == 0), stop=(n == 0 or o == 1))
                fill(last, ("rhs", n))
                emptied(pe, ("rhs", n), ("x", n, LEVELS - 1, 0), ("x", n, LEVELS - 1, 1),
                        ("xt", n, LEVELS - 1, 0), ("xt", n, LEVELS - 1, 1))
                ps = take(pe, ("sa", n), 7)
                for hd in range(8):
                    last = mm(ps[:, 64 * hd:64 * hd + 64], invT[:, hd, :], rhs[:, 64 * hd:64 * hd + 64],
                              start=True, stop=True)
                fill(last, ("sa", n))
                emptied(pe, ("sa", n))
                ps = take(pe, ("y", n), 6)
                for p in range(4):
                    if n:
                        mm(ps[:, P * p:P * p + P], zr[:, p, n, P:2 * P], s0[:, p, :], start=True, stop=False)
                    for o in range(2):
                        hd = 2 * p + o
                        c = slice(64 * hd, 64 * hd + 64)
                        mm(ps[:, c], mats[:, hd, 3, :], vrow[:, n, c], start=(n == 0), stop=False)
                        last = mm(ps[:, c], mats[:, hd, 1, :], sa[:, c], start=False, stop=(n == 0 or o == 1))
                fill(last, ("y", n))
                if n == 0:
                    emptied(pe, ("kbT", 0), ("kbT", 1))
                    ps = take(pe, ("st",), 7)
                    for p in range(4):
                        c = slice(P * p, P * p + P)
                        mm(ps[:, c], krow[:, c], vrow[:, 0, c], start=True, stop=False)
                        last = mm(ps[:, c], brow[:, c], sa[:, c], start=False, stop=True)
                    fill(last, ("st",))
            def gate(f):
                name, key = (f"rg{f}", "rg") if f < 2 else (f"rs{f - 2}", "rs")
                rows(name, [(key, f % 2 if f < 2 else f - 2, i) for i in range(2)], (0, 1) if f % 2 == 0 else (2, 3), xT)

            def scores_of(n):
                for o in range(2):
                    r = slice(64 * o, 64 * o + 64)
                    ps = take(pe, ("s", n, o), 6 + o)
                    for p in range(4):
                        last = mm(ps[:, P * p:P * p + P], kTr[r, p, P * n:P * n + P], qT[r, p, P * n:P * n + P],
                                  start=True, stop=True)
                    fill(last, ("s", n, o))

            def outputs_of(n):
                emptied(pe, ("s", n, 0), ("s", n, 1))
                if n:
                    emptied(pe, ("R", 0), ("R", 1))
                for g in range(2):
                    ps = take(pe, ("o", n, g), 4 + g)
                    for e in range(2):
                        p = 2 * g + e
                        if n:
                            mm(ps[:, 256 * e:256 * e + 256], qT[:, p, P:2 * P], rst[:, p, :], start=True, stop=False)
                        for o in range(2):
                            hd = 2 * p + o
                            last = mm(ps[:, 256 * e + P * o:256 * e + P * o + P], sT[:, hd, :],
                                      vr[:, n, P * hd:P * hd + P], start=(n == 0), stop=(n == 0 or o == 1))
                    fill(last, ("o", n, g))

            gate(0)
            pe.wait_ge(sem("y_rows"), 1)
            for i in range(2):
                turns(("yT", i), 4 + i, [yrow[:, i, P * p:P * p + P] for p in range(4)])
            pe.wait_ge(sem("qk_rope"), 2)
            for i in range(2):
                turns(("qT", i), 6, [qr[:, i, P * p:P * p + P] for p in range(4)])
                turns(("kTr", i), 7, [kr[:, i, P * p:P * p + P] for p in range(4)])
            gate(1)
            emptied(pe, ("rv", 0, 0), ("rv", 1, 0), ("rv", 0, 1), ("rv", 1, 1))
            for g in range(2):
                ps = take(pe, ("R", g), 4 + g)
                for e in range(2):
                    p = 2 * g + e
                    last = mm(ps[:, 256 * e:256 * e + 256], kr[:, 0, P * p:P * p + P], vr[:, 0, 256 * p:256 * p + 256],
                              start=True, stop=True)
                fill(last, ("R", g))
            emptied(pe, ("qT", 0), ("qT", 1), ("kTr", 0), ("kTr", 1))
            scores_of(0)
            gate(2)
            outputs_of(0)
            scores_of(1)
            gate(3)
            outputs_of(1)
            gate(4)
            gate(5)
            pe.wait_ge(sem("o_rows"), 1)
            for i in range(2):
                for q in range(2):
                    turns(("oT", i, q), 4 + 2 * i + q, [orow[:, i, P * (4 * q + j):P * (4 * q + j) + P] for j in range(4)])
            pe.wait_ge(sem("yrwT_ready"), 1)
            deep_product("brw", 4, yrwT, "brw", 0)
            emptied(pe, *[("oT", i, q) for i in range(2) for q in range(2)])
            deep_product("bret", 8, oT, "bret", 4)
            pe.wait_ge(sem("merged"), 1)
            for i in range(2):
                for q in range(2):
                    turns(("mT", i, q), 4 + 2 * i + q, [mrow[:, i, P * (4 * q + j):P * (4 * q + j) + P] for j in range(4)])
            emptied(pe, *[("mT", i, q) for i in range(2) for q in range(2)])
            deep_product("wo", 8, mT, "wo", 0)
            norm_turns(1)
            xT_ready(1)
            for j in range(11):
                for v, name in enumerate("gv"):
                    b = 4 * (j % 2) + 2 * v
                    turned(f"up{j}{name}", [("up", j, 2 * v), ("up", j, 2 * v + 1)], (b, b + 1))
            pe.wait_ge(sem("act_ready"), 22)
            deep_product("dn", 22, actT, "dn", 0)
            norm_turns(2)
            xT_ready(2)
            for j in range(12):
                turned(f"xbc{j}", [("xbc", 2 * j), ("xbc", 2 * j + 1)], (2 * (j % 2), 2 * (j % 2) + 1))
            ps = take(pe, ("dt",), 4)
            w = unit("dt")
            for i in range(2):
                for k in range(KT):
                    last = mm3(ps[:, 32 * i:32 * i + 32], both(xT, every, k, slice(i * P, i * P + P)),
                               both(w, every, k, every), k == 0, k == KT - 1)
            fill(last, ("dt",))
            used("dt", key=("dt",))
            z_keys = lambda j: [("z", j, i) for i in range(2)]
            rows("z0", z_keys(0), (0, 1), xT)
            pe.wait_ge(sem("adt_ready"), 1)
            ps = take(pe, ("ac",), 5)
            for n in range(2):
                mm(ps[:, 32 * n:32 * n + 32], const("incl"), adt[:, n, :], start=True, stop=True)
            fill(mm(ps[:, 64:96], const("ones"), adt[:, 0, :], start=True, stop=True), ("ac",))
            pe.wait_ge(sem("xbc_ready"), 24)
            for i in range(2):
                for q in range(4):
                    turns(("xsT", i, q), 6 + q % 2, [xbc[:, 4 * q + j, P * i:P * i + P] for j in range(4)])
            turns(("bR",), 6, [xbc[:, 16 + g, 0:P] for g in range(4)])
            rows("z1", z_keys(1), (2, 3), xT)
            for n in range(2):
                ps = take(pe, ("cb", n), 7)
                for g in range(4):
                    last = mm(ps[:, P * g:P * g + P], xbc[:, 16 + g, P * n:P * n + P], xbc[:, 20 + g, P * n:P * n + P],
                              start=True, stop=True)
                fill(last, ("cb", n))
            pe.wait_ge(sem("xd_ready"), 3)
            emptied(pe, ("bR",))
            for g in range(4):
                ps = take(pe, ("sst", g), 4 + g % 2)
                fill(mm(ps[:, :], bR[:, P * g:P * g + P], xdd[:, 512 * g:512 * g + 512], start=True, stop=True), ("sst", g))

            def spread(n, u):
                ps = take(pe, ("bc", n, u), u % 2)
                for e in range(4):
                    hd = 4 * u + e
                    last = mm(ps[:, P * e:P * e + P], adt[:, n, hd:hd + 1].to_broadcast([P, P]), const("incl"),
                              start=True, stop=True)
                fill(last, ("bc", n, u))

            spread(0, 0)
            spread(0, 1)
            for n in range(2):
                for g in range(4):
                    if 4 * n + g < 7:
                        nn, ng = divmod(4 * n + g + 1, 4)
                        spread(nn, 2 * ng)
                        spread(nn, 2 * ng + 1)
                    pe.wait_ge(sem("wT_ready"), 2 * (4 * n + g) + 2)
                    ps = take(pe, ("yd", n, g), 2 + g % 2)
                    for e in range(8):
                        hd = 8 * g + e
                        last = mm(ps[:, 64 * e:64 * e + 64], wT[:, g % 2, e, :], xd[:, n, 64 * hd:64 * hd + 64],
                                  start=True, stop=True)
                    fill(last, ("yd", n, g))
                    if n:
                        emptied(pe, ("sst", g))
                        ps = take(pe, ("yo", g), 4 + g % 2)
                        fill(mm(ps[:, :], xbc[:, 20 + g, P:2 * P], ss0[:, g, :], start=True, stop=True), ("yo", g))
                    if g % 2 == 0:
                        m = 2 * n + g // 2
                        if m % 2 == 0:
                            zps = [take(pe, key, 6 + i) for i, key in enumerate(z_keys(2 + m // 2))]
                        rows_half(f"z{2 + m // 2}", m % 2, zps, z_keys(2 + m // 2), xT)
            pe.wait_ge(sem("yg_rows"), 2)
            for i in range(2):
                for q in range(4):
                    turns(("gT", i, q), 6 + q % 2, [xs[:, i, P * (4 * q + j):P * (4 * q + j) + P] for j in range(4)])
            pe.wait_ge(sem("ygT_ready"), 8)
            deep_product("so", 16, ygT, "so", 0)

            def embed(m):
                norm_turns(3 if m == 0 else 5)
                pe.wait_ge(sem("p_landed"), 16 * (m + 1))
                turns(("pT", m), 0, [prow[:, i, P * k:P * k + P] for k in range(2) for i in range(2)])
                xT_ready(3 if m == 0 else 5)
                emptied(pe, ("pT", m))
                w = unit(f"pp{m}")
                for f in range(2):
                    for i in range(2):
                        ps = take(pe, ("pp", m, f, i), 4 + 2 * f + i)
                        for k in range(2):
                            last = mm3(ps[:, :], both(pT, every, k, slice(i * P, i * P + P)),
                                       both(w, every, k, slice(512 * f, 512 * f + 512)), k == 0, k == 1)
                        fill(last, ("pp", m, f, i))
                used(f"pp{m}", key=("pp", m, 1, 1))
                for f in range(2):
                    rows(f"pg{m}{f}", [("pg", m, f, i) for i in range(2)], (2 * f, 2 * f + 1), xT)

            embed(0)
            norm_turns(4)
            pe.wait_ge(sem("xT2_lower_ready"), 4)
            rows("kv", [("kv", i) for i in range(2)], (0, 1), xT2)
            xT_ready(4)
            for j in range(4):
                rows(f"ain{j}", [("ain", j, i) for i in range(2)], (2, 3) if j % 2 == 0 else (0, 1), xT)
            pe.wait_ge(sem("ak_rows"), 1)
            turns(("akT",), 6, [akr[:, i, P * u:P * u + P] for u in range(2) for i in range(2)])
            pe.wait_ge(sem("aq_rows"), 1)
            for i in range(2):
                for u in range(2):
                    turns(("aqT", i, u), 4 + u, [aqr[:, i, 512 * u + P * g:512 * u + P * g + P] for g in range(4)])
            emptied(pe, ("akT",), *[("aqT", i, u) for i in range(2) for u in range(2)])

            def scores(z):
                n, u, o, gh = UNITS[z]
                r = slice(64 * o, 64 * o + 64)
                ps = take(pe, ("as", z), 2 * (z % 2) + o)
                nh, w = (4, P) if n == 0 else (2, 2 * P)
                for e in range(nh):
                    last = mm(ps[:, w * e:w * e + w], aqT[r, u, nh * gh * n + e, P * n:P * n + P], akT[r, u, 0:w],
                              start=True, stop=True)
                fill(last, ("as", z))

            def values(z):
                n, u, o, gh = UNITS[z]
                pe.wait_ge(sem("exps"), z + 1)
                turns(("eT", z), 4 + z % 2, [asb[:, z % 2, P * j:P * j + P] for j in range(4)])
                emptied(pe, ("eT", z))
                ps = take(pe, ("ao", z), 6 + z % 2)
                nh, kt_ = (4, 1) if n == 0 else (2, 2)
                for e in range(nh):
                    for s in range(kt_):
                        last = mm(ps[:, 64 * e:64 * e + 64], aeT[:, z % 2, P * (kt_ * e + s):P * (kt_ * e + s) + P],
                                  kvr[:, s, 256 + 64 * (2 * u + o):256 + 64 * (2 * u + o) + 64],
                                  start=(s == 0), stop=(s == kt_ - 1))
                fill(last, ("ao", z))

            scores(0)
            for z in range(len(UNITS)):
                if z + 1 < len(UNITS):
                    scores(z + 1)
                values(z)
            pe.wait_ge(sem("ao_rows"), 1)
            for i in range(2):
                for q in range(2):
                    turns(("aoT", i, q), 4 + 2 * i + q, [ao[:, i, P * (4 * q + j):P * (4 * q + j) + P] for j in range(4)])
            emptied(pe, *[("aoT", i, q) for i in range(2) for q in range(2)])
            deep_product("ao", 8, aoT, "fo", 0)
            embed(1)

        @block.sync
        def _(sp):
            sp.dma_start(h[:, :, :], io["x"].rearrange("o (i p) d -> p (o i) d", p=P)).then_inc(sem("x_landed"), 16)
            sp.dma_start(consts[:, :], io["table"]).then_inc(sem("consts_landed"), 16)

            for n, (name, w, r0, nk, c0, width) in enumerate(units):
                w, _, layer = w.partition(":")
                src = io[w][int(layer or 0)] if len(io[w].shape) == 3 else io[w]
                if n >= LOADS:
                    sp.wait_ge(lowers, n - LOADS + 1)
                sp.dma_start(tiles(part(loaded, LOADS, n), n),
                             src[r0:r0 + nk * P, c0:c0 + width].rearrange("(k p) c -> p k c", p=P)) \
                    .then_inc(unit_landed[n % LOADS], 16)
            sp.wait_ge(sem("out_ready"), 4)
            sp.dma_start(out.rearrange("o (i p) d -> p (o i) d", p=P), h[:, :, :]).then_inc(sem("out_written"), 16)
            sp.wait_ge(sem("out_written"), 16)

        @block.gpsimd
        def _(pool):
            for g, parts in enumerate(STAGES):
                at = 0
                for name, r0, n in parts:
                    src = io[name]
                    if len(src.shape) == 3:
                        src = src[0].rearrange("t (r c) -> (t r) c", c=P)
                    elif len(src.shape) == 2 and name == "ple_norm_w_2":
                        src = src.rearrange("l (r c) -> (l r) c", c=P)
                    elif len(src.shape) == 2:
                        src = src[0].rearrange("(r c) -> r c", c=P)
                    else:
                        src = src.rearrange("(r c) -> r c", c=P)
                    pool.dma_start(stage[at:at + n, g, :], src[r0:r0 + n, :]).then_inc(sem("stage_landed"), 16)
                    at += n
            pool.dma_start(lora[0:64, 0, :], io["rw_w2"][0]).then_inc(sem("lora_landed"), 16)
            pool.dma_start(lora[64:128, 0, :], io["rw_a2"][0]).then_inc(sem("lora_landed"), 16)
            pool.dma_start(lora[:, 1, :], io["rw_g2"][0]).then_inc(sem("lora_landed"), 16)

            def spread_row(dst, src, s):
                pool.dma_start(dst, src.partition_broadcast(P)).then_inc(sem(s), 16)

            spread_row(postw[:, :], io["norm_mix_post"][0], "postw_landed")
            for dst, src in ((qn, io["q_norm_w_2"][0]), (kn_, io["k_norm_w_2"]), (sinks, io["attn_sinks_2"][0]),
                             (dtb, io["ssm_dt_bias_2"][0]), (alog, io["ssm_a_log_2"][0]), (dsk_, io["ssm_d_2"][0])):
                spread_row(dst, src, "rowp_landed")
            for m, name in enumerate(["positions", "positions_2"]):
                pool.dma_start(posi[:, 2 * m:2 * m + 2], io[name].rearrange("o (i p) -> p (o i)", p=P),
                               allow_slow_non_contiguous=True).then_inc(sem("pos_landed"), 16)
            for n in range(2):
                for k in range(1, LEVELS):
                    if k == 1:
                        pool.wait_ge(sem("mats_ready"), 8 * (n + 1))
                    for q in range(2):
                        if k > 1:
                            full(pool, ("t1", n, k - 1, q))
                        elif n:
                            full(pool, ("t1", 0, LEVELS - 1, q))
                        pool.tensor_tensor(lk[:, 4 * q:4 * q + 4, :], mats[:, 4 * q:4 * q + 4, 0, :],
                                           const(f"off{k}").unsqueeze(1).broadcast_to([P, 4, P]), ALU.mult) \
                            .then_inc(sem("lk_ready"), 1)
            full(pool, ("o", 1, 0))
            full(pool, ("o", 1, 1))
            pool.dma_start(h[:, :, :], io["x"].rearrange("o (i p) d -> p (o i) d", p=P)).then_inc(sem("x_again"), 16)
            pool.wait_ge(sem("joined"), 4)
            spread_row(postw[:, :], io["norm_ffn_post"][0], "postw_landed")
            for m in range(2):
                pool.wait_ge(sem("h_ready"), 6 if m == 0 else 10)
                pool.dma_start(prow[:, :, :], io["p_2"][m].rearrange("o (i p) c -> p (o i) c", p=P)) \
                    .then_inc(sem("p_landed"), 16)

        @block.scalar
        def _(act):
            chain = [0]

            def link(ins):
                chain[0] += 1
                ins.then_inc(sem("act_chain"), 1)
                act.wait_ge(sem("act_chain"), chain[0])

            A = act.activation

            split_at = [0]

            def split_to(name, more=0):
                while split_at[0] <= min(index[name] + more, len(units) - 1):
                    n = split_at[0]
                    act.wait_ge(unit_landed[n % LOADS], 16 * (n // LOADS + 1))
                    part_free(act, n)
                    A(part(upper, PARTS, n), part(loaded, LOADS, n), ACT.Copy).then_inc(uppers, 1)
                    split_at[0] += 1

            def upper_of(dst, key, k0, i, n=4):
                ps = full(act, key)
                A(dst[0][:, k0:k0 + n, P * i:P * i + P], ps[:, :].rearrange("p (a b) -> p a b", a=n), ACT.Copy) \
                    .then_inc(sem("operand_uppers"), 1)

            def norm_upper(n):
                for x in ((xT2, xT) if n == 4 else (xT,)):
                    for i in range(2):
                        for q in range(2):
                            xs_count[0] += 1
                            act.wait_ge(sem("xT_scaled"), xs_count[0])
                            A(x[0][:, 4 * q:4 * q + 4, P * i:P * i + P],
                              hs[:, i, 512 * q:512 * q + 512].rearrange("p (a b) -> p a b", a=4), ACT.Copy) \
                                .then_inc(sem("xT_upper_ready"), 1)

            xs_count = [0]

            def norm(n):
                if n == 0:
                    act.wait_ge(sem("x_landed"), 16)
                else:
                    act.wait_ge(sem("h_ready"), HR[n])
                for i in range(2):
                    A(hs[:, i, :], h[:, i, :], ACT.Square, accum_out=ssq[:, i:i + 1]).then_inc(sem("sq_done"), 1)
                act.wait_ge(sem("sq_done"), 2 * (n + 1))
                act.wait_ge(sem("eps_set"), 1)
                A(rstd[:, 0:2], ssq[:, 0:2], ACT.Sqrt, scale=1.0 / D, bias=eps6).then_inc(sem("root"), 1)

            def post_norm(key, count):
                for i in range(2):
                    for f in range(2):
                        ps = full(act, (key, i, f))
                        A(hs[:, i, 512 * f:512 * f + 512], ps[:, :], ACT.Square,
                          accum_out=ssq[:, 2 * i + f:2 * i + f + 1]).then_inc(sem("post_sq"), 1)
                act.wait_ge(sem("post_sum"), count)
                A(rstd[:, 0:2], ssq[:, 0:2], ACT.Sqrt, scale=1.0 / D, bias=eps6).then_inc(sem("root2"), 1)

            def copy(dst, key, w=512, func=ACT.Copy):
                ps = full(act, key)
                empty(A(dst, ps[:, 0:w], func), key)

            norm(0)
            split_to("rw1")
            norm_upper(0)
            for c in range(14):
                if c % 2 == 1:
                    split_to(f"rw{c // 2}", 2)
                copy(pr[:, c, 1:257], ("rw", c), T)
            act.wait_ge(sem("angles"), 1)
            A(cosd[:, :, 0:32], angn[:, :, :], ACT.Sin).then_inc(sem("trig"), 1)
            A(sind[:, :, 32:64], ang[:, :, :], ACT.Sin).then_inc(sem("trig"), 1)
            split_to("rq.1")
            act.wait_ge(sem("shifted"), 2)
            A(lor[0:64, 0, :], pr[0:64, 12, 1:257], ACT.Tanh).then_inc(sem("lora_in"), 1)
            A(lor[:, 1, :], pr[:, 13, 1:257], ACT.Sigmoid).then_inc(sem("lora_in"), 1)
            split_to("rq.1", 2)
            for i in range(2):
                copy(qr[:, i, :], ("rq", i))
            for p in range(4):
                ps = full(act, ("w", p))
                empty(A(ld[:, p, :], ps[:, 0:T], ACT.Sigmoid, bias=pc("rw_w0", p)), ("w", p))
                ps = full(act, ("a", p))
                empty(A(av[:, p, :], ps[:, 0:T], ACT.Sigmoid, bias=pc("rw_a0", p)), ("a", p))
                copy(gT[:, p, :], ("g", p), T)
            split_to("rk.1", 2)
            for i in range(2):
                copy(kr[:, i, :], ("rk", i))
            act.wait_ge(sem("knorm_in"), 1)
            A(ex[:, :, :], ex3[:, :, :], ACT.Sqrt).then_inc(sem("knorm_root"), 1)
            for i in range(2):
                copy(vrow[:, i, :], ("vT", i))
            split_to("rv0.1", 2)
            for i in range(2):
                copy(vr[:, i, 0:512], ("rv", 0, i))
            act.wait_ge(sem("cum_ready"), 1)
            A(ex3[:, :, :], cc[:, :, :], ACT.Exp).then_inc(sem("e_done"), 1)
            act.wait_ge(sem("prev_ready"), 1)
            A(ex[:, :, :], ld[:, :, :], ACT.Exp).then_inc(sem("e_done"), 1)
            act.wait_ge(sem("rk_ready"), 1)
            for p in range(4):
                full(act, ("bs", p))
            A(ex2[:, :, :], cc[:, :, :], ACT.Exp, scale=-1.0).then_inc(sem("e_done"), 1)
            act.wait_ge(sem("fcol_in"), 1)
            A(fcol[:, :], fcol[:, :], ACT.Exp).then_inc(sem("f_done"), 1)
            split_to("rv1.1", 2)
            for i in range(2):
                copy(vr[:, i, 512:1024], ("rv", 1, i))
            copy(krow[:], ("kbT", 0))
            copy(brow[:], ("kbT", 1))
            for n in range(2):
                for k in range(1, LEVELS):
                    for q in range(2):
                        copy(t1[:, 4 * q:4 * q + 4, :], ("t1", n, k, q))
                copy(rhs[:], ("rhs", n))
                copy(sa[:], ("sa", n))
                copy(yrow[:, n, :], ("y", n))
            split_to("rg0.1", 2)
            act.wait_ge(sem("gn_var"), 1)
            A(rs8[:, :, 0:8], var[:, :, 0:8], ACT.Sqrt).then_inc(sem("gn_root"), 1)
            for i in range(2):
                copy(gr[:, i, 0:512], ("rg", 0, i), func=ACT.Silu)
            for i in range(2):
                ps = full(act, ("qT", i))
                empty(A(qT[:, :, P * i:P * i + P], ps[:, :].rearrange("p (a b) -> p a b", a=4), ACT.Copy), ("qT", i))
                ps = full(act, ("kTr", i))
                empty(A(kTr[:, :, P * i:P * i + P], ps[:, :].rearrange("p (a b) -> p a b", a=4), ACT.Copy), ("kTr", i))
            split_to("rg1.1", 2)
            for i in range(2):
                copy(gr[:, i, 512:1024], ("rg", 1, i), func=ACT.Silu)
            for f in range(4):
                split_to(f"rs{f}.1", 2)
                for i in range(2):
                    copy(sg[:, i, f // 2, 512 * (f % 2):512 * (f % 2) + 512], ("rs", f, i), func=ACT.Sigmoid)
                if f == 2:
                    act.wait_ge(sem("gn_var"), 2)
                    A(rs8[:, :, 0:8], var[:, :, 0:8], ACT.Sqrt).then_inc(sem("gn_root"), 1)
            act.wait_ge(sem("yrw_ready"), 1)
            A(yrwT[0][:, :, :], yrw[:, :, :], ACT.Copy).then_inc(sem("yrwT_upper"), 1)
            for i in range(2):
                for q in range(2):
                    upper_of(oT, ("oT", i, q), 4 * q, i)
            split_to("bret3", 2)
            for i in range(2):
                for q in range(2):
                    upper_of(mT, ("mT", i, q), 4 * q, i)
            split_to("wo3", 2)
            post_norm("wo", 1)
            norm(1)
            norm_upper(1)
            def act_upper(j):
                for c in range(2):
                    act.wait_ge(sem("act_product"), 2 * j + c + 1)
                    A(actT[0][:, 2 * j + c, :], acc[:, j % 2, c, :], ACT.Copy).then_inc(sem("actT_upper"), 1)

            for j in range(11):
                for c in range(4):
                    if c % 2 == 1:
                        split_to(f"up{j}" + "gv"[c // 2], 2)
                    if c == 2 and j:
                        act_upper(j - 1)
                    ch = 2 * j + c % 2 + 22 * (c // 2)
                    ps = full(act, ("up", j, c))
                    if j >= 2:
                        act.wait_ge(sem("act_ready"), 2 * (j - 1))
                    A(acc[:, j % 2, c, :], ps[:, 0:T], ACT.Identity, bias=fcb(ch), scale=fcw(2, ch)) \
                        .then_inc(sem("tap0"), 1)
                for c in range(2):
                    emptied(act, ("up", j, c))
                    A(acc[:, j % 2, c, :], acc[:, j % 2, c, :], ACT.Gelu_apprx_tanh).then_inc(sem("gelu"), 1)
            act_upper(10)
            split_to("dn10", 2)
            post_norm("dn", 2)
            norm(2)
            norm_upper(2)
            def z_copy(j):
                for i in range(2):
                    copy(zrow[:, i, 512 * j:512 * j + 512], ("z", j, i))

            for c in range(24):
                if c % 2 == 1:
                    split_to(f"xbc{c // 2}", 2)
                ps = full(act, ("xbc", c))
                if c >= 4:
                    act.wait_ge(sem("xbc_ready"), c - 3)
                A(cacc[:, c % 4, :], ps[:, 0:T], ACT.Identity, bias=scb(c), scale=scw(3, c)).then_inc(sem("stap0"), 1)
                if c >= 1:
                    emptied(act, ("xbc", c - 1))
                    A(xbc[:, c - 1, :], cacc[:, (c - 1) % 4, :], ACT.Silu).then_inc(sem("xbc_ready"), 1)
            emptied(act, ("xbc", 23))
            A(xbc[:, 23, :], cacc[:, 3, :], ACT.Silu).then_inc(sem("xbc_ready"), 1)
            split_to("dt", 2)
            act.wait_ge(sem("dt_in"), 1)
            link(A(adt[:, :, :], adt[:, :, :], ACT.Exp))
            link(A(adt[:, :, :], adt[:, :, :], ACT.Ln, bias=1.0))
            act.wait_ge(sem("rowp_landed"), 96)
            A(arow[:, :], alog, ACT.Exp).then_inc(sem("dt_log"), 1)
            split_to("z0.1", 2)
            z_copy(0)
            for i in range(2):
                for q in range(4):
                    copy(xs[:, i, 512 * q:512 * q + 512], ("xsT", i, q))
            copy(bR[:], ("bR",))
            act.wait_ge(sem("dte_in"), 1)
            A(dte[:, :], tot[:, :], ACT.Exp).then_inc(sem("dte_done"), 1)
            A(eac[:, :], acs[:, 1, :], ACT.Exp).then_inc(sem("dte_done"), 1)
            split_to("z1.1", 2)
            z_copy(1)
            for g in range(4):
                copy(ss0[:, g, :], ("sst", g))
            for u in range(16):
                act.wait_ge(sem("seg_ready"), u + 1)
                A(eT2[:, u % 2, :], eT2[:, u % 2, :], ACT.Exp).then_inc(sem("seg_exp"), 1)
                if u % 4 == 3:
                    m = u // 4
                    split_to(f"z{2 + m // 2}.{m % 2}", 2)
                    if m % 2:
                        z_copy(2 + m // 2)
            for j in range(4):
                emptied(act, ("z", j, 0), ("z", j, 1))
            for i in range(2):
                A(zrow[:, i, :], zrow[:, i, :], ACT.Silu).then_inc(sem("z_silu"), 1)
            for i in range(2):
                for g in range(4):
                    act.wait_ge(sem("yz_ready"), i + 1)
                    A(xd[:, i, 512 * g:512 * g + 512], xs[:, i, 512 * g:512 * g + 512], ACT.Square,
                      accum_out=mean[:, i, g:g + 1]).then_inc(sem("yg_sq"), 1)
            act.wait_ge(sem("yg_sq"), 8)
            A(var[:, :, 0:4], mean[:, :, 0:4], ACT.Sqrt, scale=1.0 / 512, bias=eps6).then_inc(sem("yg_root"), 1)

            for i in range(2):
                for q in range(4):
                    act.wait_ge(sem("yg_scaled"), 4 * i + q + 1)
                    A(ygT[0][:, 4 * q:4 * q + 4, P * i:P * i + P],
                      yg[:, i, q, :].rearrange("p (a b) -> p a b", a=4), ACT.Copy).then_inc(sem("yg_upper"), 1)
            split_to("so7", 2)

            def embed(m):
                n = 3 if m == 0 else 5
                norm(n)
                norm_upper(n)
                ps = full(act, ("pT", m))
                A(pT[0][:, :, :], ps[:, :].rearrange("p (a b) -> p a b", a=2), ACT.Copy).then_inc(sem("operand_uppers"), 1)
                split_to(f"pp{m}", 2)
                for f in range(2):
                    split_to(f"pg{m}{f}.1", 2)
                    for i in range(2):
                        z = 2 * f + i
                        ps = full(act, ("pg", m, f, i))
                        if z >= 2 or m:
                            act.wait_ge(sem("ple_used"), 4 * m + z - 1)
                        empty(A(psg[:, z % 2, :], ps[:, :], ACT.Sigmoid), ("pg", m, f, i))

            embed(0)
            norm(4)
            norm_upper(4)
            split_to("kv.1", 2)
            for i in range(2):
                copy(kvr[:, i, :], ("kv", i))
            for j in range(2):
                split_to(f"ain{j}.1", 2)
                for i in range(2):
                    copy(aq[:, i, 512 * j:512 * j + 512], ("ain", j, i))
            for j in range(2):
                split_to(f"ain{2 + j}.1", 2)
                for i in range(2):
                    copy(ag[:, i, 512 * j:512 * j + 512], ("ain", 2 + j, i), func=ACT.Silu)
            act.wait_ge(sem("hn_in"), 1)
            A(rs8[:, :, 0:4], var[:, :, 0:4], ACT.Sqrt).then_inc(sem("hn_root"), 1)
            act.wait_ge(sem("hn_in"), 2)
            A(rs8[:, :, 0:16], var[:, :, 0:16], ACT.Sqrt).then_inc(sem("hn_root"), 1)
            ps = full(act, ("akT",))
            empty(A(akT[:, :, :], ps[:, :].rearrange("p (a b) -> p a b", a=2), ACT.Copy), ("akT",))
            for i in range(2):
                for u in range(2):
                    ps = full(act, ("aqT", i, u))
                    empty(A(aqT[:, u, :, P * i:P * i + P], ps[:, :].rearrange("p (a b) -> p a b", a=4), ACT.Copy),
                          ("aqT", i, u))
            for z in range(len(UNITS)):
                act.wait_ge(sem("sub_ready"), z + 1)
                nh = 4 if UNITS[z][0] == 0 else 2
                A(dsk[:, z % 2, 0:nh], dsk[:, z % 2, 0:nh], ACT.Exp).then_inc(sem("sink_exp"), 1)
                A(asb[:, z % 2, :], asb[:, z % 2, :], ACT.Exp).then_inc(sem("exps"), 1)
                copy(aeT[:, z % 2, :], ("eT", z))
            for i in range(2):
                for q in range(2):
                    upper_of(aoT, ("aoT", i, q), 4 * q, i)
            split_to("ao3", 2)
            embed(1)

        @block.vector
        def _(ve):
            chain = [0]

            def link(ins):
                chain[0] += 1
                ins.then_inc(sem("ve_chain"), 1)
                ve.wait_ge(sem("ve_chain"), chain[0])

            TT, TS, STT = ve.tensor_tensor, ve.tensor_scalar, ve.scalar_tensor_tensor
            mul, add, sub, mx_ = ALU.mult, ALU.add, ALU.subtract, ALU.max

            def bc(a, *shape):
                return a.broadcast_to(list(shape))

            def four(ps, a=4):
                return ps[:, :].rearrange("p (a b) -> p a b", a=a)

            split_at, xl, lowered = [0], [0], [0]

            def split_to(name, more=0):
                while split_at[0] <= min(index[name] + more, len(units) - 1):
                    n = split_at[0]
                    ve.wait_ge(uppers, n + 1)
                    TT(part(lower, PARTS, n), part(loaded, LOADS, n), part(upper, PARTS, n).bitcast(F32), sub) \
                        .then_inc(lowers, 1)
                    split_at[0] += 1

            def lower_of(dst, key, k0, i, n=4):
                lowered[0] += 1
                ve.wait_ge(sem("operand_uppers"), lowered[0])
                ps = full(ve, key)
                c = (slice(None), slice(k0, k0 + n), slice(P * i, P * i + P))
                empty(TT(dst[1][c], four(ps, n), dst[0][c].bitcast(F32), sub), key)

            link(ve.memset(eps6, 1e-6))
            ve.memset(pr[:, :, 0:1], 0.0).then_inc(sem("eps_set"), 1)

            def norm(n, name, r0=0):
                ve.wait_ge(sem("root"), n + 1)
                link(ve.reciprocal(rstd[:, 0:2], rstd[:, 0:2]))
                for i in range(2):
                    TS(hs[:, i, :], h[:, i, :], rstd[:, i:i + 1], None, mul).then_inc(sem("rows_scaled"), 1)
                if n == 0:
                    for g, parts in enumerate(STAGES):
                        m = sum(p[2] for p in parts)
                        ps = full(ve, ("cols", g))
                        at = [0, 114, 202, 290][g]
                        empty(ve.tensor_copy(cols[:, at:at + m], ps[:, 0:m]), ("cols", g))
                    emptied(ve, *[("cols", g) for g in range(4)])
                    split_to("rw1")
                for x, w in (((xT2, "kv_norm_w_2"), (xT, name)) if n == 4 else ((xT, name),)):
                    for i in range(2):
                        for q in range(2):
                            ps = full(ve, ("nT", n, i, q))
                            g = cols[:, colat[(w, r0)] + 4 * q:colat[(w, r0)] + 4 * q + 4]
                            if x is xT and n == 4:
                                ve.wait_ge(sem("xT2_lower_ready"), 2 * i + q + 1)
                            TT(four(hs[:, i, 512 * q:512 * q + 512]), four(ps), bc(g.unsqueeze(2), P, 4, P), mul) \
                                .then_inc(sem("xT_scaled"), 1)
                    for i in range(2):
                        for q in range(2):
                            xl[0] += 1
                            ve.wait_ge(sem("xT_upper_ready"), xl[0])
                            c = (slice(None), slice(4 * q, 4 * q + 4), slice(P * i, P * i + P))
                            TT(x[1][c], four(hs[:, i, 512 * q:512 * q + 512]), x[0][c].bitcast(F32), sub) \
                                .then_inc(sem("xT2_lower_ready" if x is xT2 else "xT_lower_ready"), 1)
                for i in range(2):
                    for q in range(2):
                        empty(ve.nop(), ("nT", n, i, q))

            def post_norm(key, n):
                ve.wait_ge(sem("post_sq"), 4 * n)
                v = ssq[:, :].rearrange("p (a b) -> p a b", a=2)
                link(TT(rstd[:, 2:4], v[:, :, 0], v[:, :, 1], add))
                ve.tensor_copy(ssq[:, 0:2], rstd[:, 2:4]).then_inc(sem("post_sum"), 1)
                ve.wait_ge(sem("root2"), n)
                link(ve.reciprocal(rstd[:, 0:2], rstd[:, 0:2]))
                ve.wait_ge(sem("postw_landed"), 16 * n)
                for i in range(2):
                    for f in range(2):
                        c = slice(512 * f, 512 * f + 512)
                        ps = full(ve, (key, i, f))
                        empty(STT(out=tmph[:, i, c], in0=ps[:, :], scalar=rstd[:, i:i + 1], in1=postw[:, c],
                                  op0=mul, op1=mul), (key, i, f))
                emptied(ve, *[(key, i, f) for i in range(2) for f in range(2)])
                ve.wait_ge(sem("x_again"), 16)
                for i in range(2):
                    for f in range(2):
                        c = slice(512 * f, 512 * f + 512)
                        TT(h[:, i, c], h[:, i, c], tmph[:, i, c], add).then_inc(sem("joined"), 1)
                ve.wait_ge(sem("joined"), 4 * n)
                ve.nop().then_inc(sem("h_ready"), 2)

            norm(0, "norm_mix_pre")
            for j in range(7):
                split_to(f"rw{j}", 2)
            ve.wait_ge(sem("pos_landed"), 32)
            link(ve.tensor_copy(posf[:, :], posi[:, :]))
            link(TT(ang[:, :, :], bc(posf[:, :].unsqueeze(2), P, 4, 32), bc(const("inv").unsqueeze(1), P, 4, 32), mul))
            magic = 1.5 * 2.0 ** 23
            link(TS(angn[:, :, :], ang[:, :, :], 1.0 / (2 * np.pi), magic, mul, add))
            link(TS(angn[:, :, :], angn[:, :, :], magic, None, sub))
            two_pi = 2 * np.pi
            c1 = float(np.float32(6.28125))
            c2 = float((two_pi - c1) // 2.0 ** -19 * 2.0 ** -19)
            for piece in (c1, c2, two_pi - c1 - c2):
                link(STT(out=ang[:, :, :], in0=angn[:, :, :], scalar=-piece, in1=ang[:, :, :], op0=mul, op1=add))
            link(TS(ang[:, :, :], ang[:, :, :], 3.1415925, -3.1415925, ALU.min, mx_))
            link(TS(angn[:, :, :], ang[:, :, :], float(np.pi / 2), None, add))
            link(TS(cosd[:, :, 32:64], angn[:, :, :], float(np.pi), -two_pi, ALU.is_gt, mul))
            link(TT(angn[:, :, :], angn[:, :, :], cosd[:, :, 32:64], add))
            TS(angn[:, :, :], angn[:, :, :], 3.1415925, -3.1415925, ALU.min, mx_).then_inc(sem("angles"), 1)
            ve.wait_ge(sem("trig"), 2)
            link(ve.tensor_copy(cosd[:, :, 32:64], cosd[:, :, 0:32]))
            link(TS(sind[:, :, 0:32], sind[:, :, 32:64], -1.0, None, mul))
            for c in range(14):
                emptied(ve, ("rw", c))
            link(TT(dif[:, :, :], pr[:, :, 0:256], pr[:, :, 1:257], sub))
            for c in (12, 13, *range(12)):
                STT(out=pr[:, c, 1:257], in0=dif[:, c, :], scalar=pc("rw_mu", c), in1=pr[:, c, 1:257],
                    op0=mul, op1=add).then_inc(sem("shifted"), 1)
            ve.wait_ge(sem("shifted"), 14)
            split_to("rq.1", 2)
            r_, k_, v_ = pr[:, 0:4, 1:257], pr[:, 4:8, 1:257], pr[:, 8:12, 1:257]
            for p in range(4):
                ins = TS(kn[:, p, :], k_[:, p, :], pc("rw_k_k", p), None, mul)
            link(ins)
            TT(ex[:, :, :], kn[:, :, :], kn[:, :, :], mul).then_inc(sem("kk_squared"), 1)
            split_to("rk.1", 2)
            for p in range(4):
                ps = full(ve, ("ss", p))
                empty(TS(ex3[:, p, :], ps[:, 0:T], 1e-24, None, mx_), ("ss", p))
            for p in range(4):
                emptied(ve, ("ss", p))
            ve.nop().then_inc(sem("knorm_in"), 1)
            split_to("rv0.0", 2)
            link(TS(om[:, :], pcs("rw_k_a", 4), -1.0, 1.0, mul, add))
            for p in range(4):
                emptied(ve, ("a", p), ("w", p))
            for p in range(4):
                TS(cc[:, p, :], av[:, p, :], pc("rw_k_a", p), om[:, p:p + 1], mul, add).then_inc(sem("ka"), 1)
            ve.wait_ge(sem("ka"), 4)
            link(TT(k_, k_, cc[:, :, :], mul))
            for p in range(4):
                ins = STT(out=ex2[:, p, :], in0=r_[:, p, :], scalar=pc("rw_r_k", p), in1=k_[:, p, :], op0=mul, op1=mul)
                ins.then_inc(sem("rk1"), 1)
            ve.wait_ge(sem("rk1"), 4)
            ve.nop().then_inc(sem("rk_ready"), 1)
            split_to("rv0.1", 2)
            ve.wait_ge(sem("knorm_root"), 1)
            link(ve.reciprocal(ex[:, :, :], ex[:, :, :]))
            link(TT(kn[:, :, :], kn[:, :, :], ex[:, :, :], mul))
            link(TS(ld[:, :, :], ld[:, :, :], -float(np.exp(-0.5)), None, mul))
            for p in range(4):
                for n in range(2):
                    c = slice(P * n, P * n + P)
                    ins = ve.tensor_tensor_scan(cc[:, p, c], bc(const("ones")[:, 0:1], P, P), ld[:, p, c], 0.0, mul, add)
                    ins.then_inc(sem("scan"), 1)
            ve.wait_ge(sem("scan"), 8)
            link(ve.tensor_copy(fcol[:, :], cc[:, :, 191]))
            c4 = cc[:, :, :].rearrange("p a (n t) -> p (a n) t", n=2)
            link(ve.tensor_copy(mid, c4[:, :, 63]))
            link(TT(c4, c4, bc(mid.unsqueeze(2), P, 8, P), sub))
            link(TT(ld[:, :, :], cc[:, :, :], ld[:, :, :], sub))
            ve.nop().then_inc(sem("cum_ready"), 1)
            ve.nop().then_inc(sem("prev_ready"), 1)
            TT(fcol[:, :], fcol[:, :], cc[:, :, 127], add).then_inc(sem("fcol_in"), 1)
            emptied(ve, ("vT", 0), ("vT", 1))
            for p in range(4):
                ps = full(ve, ("bs", p))
                empty(TT(v_[:, p, :], v_[:, p, :], ps[:, 0:T], mul), ("bs", p))
            split_to("rv1.0", 2)
            z_ = zr[:, :, :, 0:P]
            rr = zr[:, :, :, P:256]
            s4 = lambda a: a.rearrange("p a (n t) -> p a n t", n=2)
            ve.wait_ge(sem("e_done"), 3)
            link(TT(rr, s4(r_), s4(ex3[:, :, :]), mul))
            link(TT(ld[:, :, :], kn[:, :, :], ex[:, :, :], mul))
            link(TS(z_, s4(ld[:, :, :]), -1.0, None, mul))
            link(TT(kn[:, :, :], kn[:, :, :], av[:, :, :], mul))
            link(TT(bt[:, :, :, :], s4(kn[:, :, :]), s4(ex2[:, :, :]), mul))
            TT(kt[:, :, :, :], s4(k_), s4(ex2[:, :, :]), mul).then_inc(sem("decayed"), 1)
            split_to("rv1.1", 2)
            strict, incl = const("strict"), const("incl")
            h8 = lambda a, n=8: a[:, :, :].rearrange("p i (a b) -> p i a b", a=n)

            def rope_tile(x, n, tab, t1_, t2_, dst):
                c = bc(cosd[:, tab, :].unsqueeze(1), P, n, 64)
                s1 = bc(sind[:, tab, 0:32].unsqueeze(1), P, n, 32)
                s2 = bc(sind[:, tab, 32:64].unsqueeze(1), P, n, 32)
                TT(t1_, x, c, mul)
                TT(t2_[:, :, 0:32], x[:, :, 32:64], s1, mul)
                link(TT(t2_[:, :, 32:64], x[:, :, 0:32], s2, mul))
                link(TT(dst, t1_, t2_, add))

            def rope_piece(z):
                x, g = ((qr, "gq"), (kr, "gk"))[z // 2]
                i = z % 2
                emptied(ve, ("rq", i), ("rk", i))
                t = [ro[:, m, :].rearrange("p (a b) -> p a b", a=8) for m in range(2)]
                v = h8(x)[:, i, :, :]
                rope_tile(v, 8, i, t[0], t[1], v)
                ins = TT(v, v, bc(const(g).unsqueeze(2), P, 8, 64), mul)
                if z % 2:
                    ins.then_inc(sem("qk_rope"), 1)
                else:
                    link(ins)

            for n in range(2):
                if n == 0:
                    ve.wait_ge(sem("decayed"), 1)
                for hd in range(8):
                    ps = full(ve, ("m", n, hd))
                    if n:
                        if hd == 0:
                            full(ve, ("y", 0))
                    v = ps[:, :].rearrange("p (a b c) -> p a b c", a=2, b=2)
                    m = mats[:, hd, :, :].rearrange("p (a b) c -> p a b c", a=2)
                    link(TT(m[:, :, 0, :], v[:, :, 0, :], bc(strict.unsqueeze(1), P, 2, P), mul))
                    empty(TT(m[:, :, 1, :], v[:, :, 1, :], bc(incl.unsqueeze(1), P, 2, P), mul), ("m", n, hd))
                emptied(ve, *[("m", n, hd) for hd in range(8)])
                ve.nop().then_inc(sem("mats_ready"), 8)
                iv = inv.rearrange("p (a o) c -> p a o c", o=2)
                for o in range(2):
                    ps = full(ve, ("L", n, o))
                    empty(TT(iv[:, :, o, :], four(ps), bc(const("off0L").unsqueeze(1), P, 4, P), mul), ("L", n, o))
                emptied(ve, ("L", n, 0), ("L", n, 1))
                link(TT(inv[:, :, :], inv[:, :, :], bc(ident.unsqueeze(1), P, 8, P), add))
                link(TT(invT[:, :, :], mats[:, :, 0, :], bc(const("off0").unsqueeze(1), P, 8, P), mul))
                TT(invT[:, :, :], invT[:, :, :], bc(ident.unsqueeze(1), P, 8, P), add).then_inc(sem("inv_start"), 1)
                ve.wait_ge(sem("inv_start"), n + 1)
                for k in range(1, LEVELS):
                    for q in range(2):
                        for key, dst in ((("x", n, k, q), inv), (("xt", n, k, q), invT)):
                            ps = full(ve, ("xt", n, k, q))
                            ps = full(ve, key)
                            d = dst[:, 4 * q:4 * q + 4, :]
                            empty(TT(d, d, four(ps), add), key)
                        emptied(ve, ("x", n, k, q), ("xt", n, k, q))
                    if n == 0 and k < 5:
                        rope_piece(k - 1)
                if n == 0:
                    ps = full(ve, ("st",))
                    empty(TT(s0[:, :, :], four(ps), bc(const("blk").unsqueeze(1), P, 4, P), mul), ("st",))
                    emptied(ve, ("st",))
                    ve.wait_ge(sem("f_done"), 1)
                    for p in range(4):
                        ins = TS(s0[:, p, :], s0[:, p, :], fcol[:, p:p + 1], None, mul)
                        ins.then_inc(sem("s0c"), 1)
                    ve.wait_ge(sem("s0c"), 4)
                    ve.nop().then_inc(sem("state_ready"), 1)

            pumps = []

            def pump():
                if pumps:
                    split_to(pumps.pop(0), 2)

            def centre(rows_, n, w, eps, sqbuf, count):
                x = rows_[:, :, 0:n * w].rearrange("p i (a b) -> p i a b", a=n)
                sq = sqbuf[:, :, 0:n * w].rearrange("p i (a b) -> p i a b", a=n)
                for i in range(2):
                    ins = ve.tensor_reduce(mean[:, i, 0:n], x[:, i, :, :], AX.X, add)
                link(ins)
                link(TS(mean[:, :, 0:n], mean[:, :, 0:n], 1.0 / w, None, mul))
                pump()
                for i in range(2):
                    link(TT(x[:, i, :, :], x[:, i, :, :], bc(mean[:, i, 0:n].unsqueeze(2), P, n, w), sub))
                pump()
                for i in range(2):
                    link(TT(sq[:, i, :, :], x[:, i, :, :], x[:, i, :, :], mul))
                pump()
                for i in range(2):
                    link(ve.tensor_reduce(var[:, i, 0:n], sq[:, i, :, :], AX.X, add))
                TS(var[:, :, 0:n], var[:, :, 0:n], 1.0 / w, eps, mul, add).then_inc(sem("gn_var"), 1)
                ve.wait_ge(sem("gn_root"), count)
                link(ve.reciprocal(rs8[:, :, 0:n], rs8[:, :, 0:n]))
                return x

            emptied(ve, ("y", 0), ("y", 1))
            pumps += ["rg0.0", "rg0.1"]
            x = centre(yrow, 8, 64, 64e-5, ar(6672, 2, 512), 1)
            for i in range(2):
                ins = TT(x[:, i, :, :], x[:, i, :, :], bc(rs8[:, i, 0:8].unsqueeze(2), P, 8, 64), mul)
                ins.then_inc(sem("yn"), 1)
            ve.wait_ge(sem("yn"), 2)
            ve.nop().then_inc(sem("y_rows"), 1)
            for i in range(2):
                ps = full(ve, ("yT", i))
                if i == 0:
                    split_to("rg1.0", 2)
                for p in range(4):
                    ins = TS(yrw[:, p, P * i:P * i + P], ps[:, P * p:P * p + P], pc("rw_lnx_w", p), pc("rw_lnx_b", p),
                             mul, add)
                empty(ins, ("yT", i))
            emptied(ve, ("yT", 0), ("yT", 1))
            link(TT(yrw[:, :, :], yrw[:, :, :], v_, add))
            TT(yrw[:, :, :], yrw[:, :, :], gT[:, :, :], mul).then_inc(sem("yrw_ready"), 1)
            split_to("rg1.1", 2)

            def rope(x, n, tab, t1_, t2_, dst):
                for i in range(2):
                    c = bc(cosd[:, tab + i, :].unsqueeze(1), P, n, 64)
                    s1 = bc(sind[:, tab + i, 0:32].unsqueeze(1), P, n, 32)
                    s2 = bc(sind[:, tab + i, 32:64].unsqueeze(1), P, n, 32)
                    TT(t1_[:, i, :, :], x[:, i, :, :], c, mul)
                    TT(t2_[:, i, :, 0:32], x[:, i, :, 32:64], s1, mul)
                    link(TT(t2_[:, i, :, 32:64], x[:, i, :, 0:32], s2, mul))
                for i in range(2):
                    link(TT(dst[:, i, :, :], t1_[:, i, :, :], t2_[:, i, :, :], add))

            for g in range(2):
                ps = full(ve, ("R", g))
                empty(TT(rst[:, 2 * g:2 * g + 2, :], four(ps, 2), bc(const("blkret").unsqueeze(1), P, 2, 256), mul),
                      ("R", g))
            for n in range(2):
                if n:
                    split_to("rs1.0", 2)
                for o in range(2):
                    ps = full(ve, ("s", n, o))
                    if n:
                        full(ve, ("o", 0, 0))
                        full(ve, ("o", 0, 1))
                    for p in range(4):
                        hd = 2 * p + o
                        ins = STT(out=sT[:, hd, :], in0=ps[:, P * p:P * p + P], scalar=float(GAMMA[hd] ** -128.0),
                                  in1=incl, op0=mul, op1=mul)
                    empty(ins, ("s", n, o))
                split_to("rs0.1" if n == 0 else "rs1.1", 2)
                for g in range(2):
                    ps = full(ve, ("o", n, g))
                    empty(ve.tensor_copy(orow[:, n, 512 * g:512 * g + 512], ps[:, :]), ("o", n, g))
            emptied(ve, ("o", 1, 0), ("o", 1, 1), ("o", 0, 0), ("o", 0, 1))
            split_to("rs2.0", 2)
            pumps += ["rs2.1"]
            x = centre(orow, 8, P, 1e-5, ar(2048, 2, D), 2)
            for i in range(2):
                link(TT(x[:, i, :, :], x[:, i, :, :], bc(rs8[:, i, 0:8].unsqueeze(2), P, 8, P), mul))
            for f in range(2):
                for i in range(2):
                    emptied(ve, ("rg", f, i))
            TT(orow[:, :, :], orow[:, :, :], gr[:, :, :], mul).then_inc(sem("o_rows"), 1)
            for f in range(4):
                for i in range(2):
                    emptied(ve, ("rs", f, i))
            ve.wait_ge(sem("yrwT_upper"), 1)
            TT(yrwT[1][:, :, :], yrw[:, :, :], yrwT[0][:, :, :].bitcast(F32), sub).then_inc(sem("yrwT_ready"), 1)
            for i in range(2):
                for q in range(2):
                    lower_of(oT, ("oT", i, q), 4 * q, i)
            split_to("bret3", 2)
            for i in range(2):
                for f in range(2):
                    c = slice(512 * f, 512 * f + 512)
                    ps = full(ve, ("brw", i, f))
                    empty(TT(mrow[:, i, c], ps[:, :], sg[:, i, 0, c], mul), ("brw", i, f))
            emptied(ve, *[("brw", i, f) for i in range(2) for f in range(2)])
            for i in range(2):
                for f in range(2):
                    c = slice(512 * f, 512 * f + 512)
                    ps = full(ve, ("bret", i, f))
                    empty(TT(mtmp, ps[:, :], sg[:, i, 1, c], mul), ("bret", i, f))
                    emptied(ve, ("bret", i, f))
                    link(TT(mrow[:, i, c], mrow[:, i, c], mtmp, add))
            ve.nop().then_inc(sem("merged"), 1)
            for i in range(2):
                for q in range(2):
                    lower_of(mT, ("mT", i, q), 4 * q, i)
            split_to("wo3", 2)
            post_norm("wo", 1)
            norm(1, "norm_ffn_pre")
            def act_lower(j):
                for c in range(2):
                    ve.wait_ge(sem("actT_upper"), 2 * j + c + 1)
                    TT(actT[1][:, 2 * j + c, :], acc[:, j % 2, c, :], actT[0][:, 2 * j + c, :].bitcast(F32), sub) \
                        .then_inc(sem("act_ready"), 1)

            for j in range(11):
                b = j % 2
                for c in range(4):
                    if c % 2 == 1:
                        split_to(f"up{j}" + "gv"[c // 2], 2)
                    if c == 3 and j:
                        act_lower(j - 1)
                    ch = 2 * j + c % 2 + 22 * (c // 2)
                    ps = full(ve, ("up", j, c))
                    ve.wait_ge(sem("tap0"), 4 * j + c + 1)
                    for tap in (1, 0):
                        sft = 2 - tap
                        a = acc[:, b, c, sft:T]
                        ins = STT(out=a, in0=ps[:, 0:T - sft], scalar=fcw(tap, ch), in1=a, op0=mul, op1=add)
                        if tap:
                            link(ins)
                    empty(ins, ("up", j, c))
                for c in range(2):
                    ve.wait_ge(sem("gelu"), 2 * j + c + 1)
                    emptied(ve, ("up", j, c + 2))
                    TT(acc[:, b, c, :], acc[:, b, c, :], acc[:, b, 2 + c, :], mul).then_inc(sem("act_product"), 1)
            act_lower(10)
            split_to("dn10", 2)
            post_norm("dn", 2)
            norm(2, "ssm_norm_w_2")
            for c in range(24):
                if c % 2 == 1:
                    split_to(f"xbc{c // 2}", 2)
                ps = full(ve, ("xbc", c))
                ve.wait_ge(sem("stap0"), c + 1)
                for sft in (1, 2, 3):
                    a = cacc[:, c % 4, sft:T]
                    ins = STT(out=a, in0=ps[:, 0:T - sft], scalar=scw(3 - sft, c), in1=a, op0=mul, op1=add)
                    if sft < 3:
                        link(ins)
                empty(ins, ("xbc", c))
            split_to("dt", 2)
            ps = full(ve, ("dt",))
            ve.wait_ge(sem("rowp_landed"), 96)
            d2 = ps[:, 0:64].rearrange("p (a b) -> p a b", a=2)
            empty(TT(dtv[:, :, :], d2, bc(dtb.unsqueeze(1), P, 2, 32), add), ("dt",))
            emptied(ve, ("dt",))
            link(TS(acs[:, :, :], dtv[:, :, :], -1.0, None, mul))
            TT(adt[:, :, :], dtv[:, :, :], acs[:, :, :], ALU.min).then_inc(sem("dt_in"), 1)
            link(TS(dtv[:, :, :], dtv[:, :, :], 0.0, None, mx_))
            ve.wait_ge(sem("dt_log"), 1)
            link(TT(dtv[:, :, :], dtv[:, :, :], adt[:, :, :], add))
            link(TS(arow, arow, -1.0, None, mul))
            TT(adt[:, :, :], dtv[:, :, :], bc(arow.unsqueeze(1), P, 2, 32), mul).then_inc(sem("adt_ready"), 1)
            split_to("z0.1", 2)
            ps = full(ve, ("ac",))
            link(ve.tensor_copy(acs[:, :, :], ps[:, 0:64].rearrange("p (a b) -> p a b", a=2)))
            empty(TT(tot, ps[:, 64:96], acs[:, 0, :], sub), ("ac",))
            emptied(ve, ("ac",))
            ve.nop().then_inc(sem("dte_in"), 1)
            hv = lambda a: a.rearrange("p (a b) -> p a b", a=32)
            for i in range(2):
                emptied(ve, *[("xsT", i, q) for q in range(4)])
                TT(hv(xd[:, i, :]), hv(xs[:, i, :]), bc(dtv[:, i, :].unsqueeze(2), P, 32, 64), mul) \
                    .then_inc(sem("xd_ready"), 1)
                if i == 0:
                    ve.wait_ge(sem("dte_done"), 2)
                    ve.wait_ge(sem("xd_ready"), 1)
                    TT(hv(xdd[:]), hv(xd[:, 0, :]), bc(dte.unsqueeze(2), P, 32, 64), mul).then_inc(sem("xd_ready"), 1)
            for i in range(2):
                link(TT(hv(xs[:, i, :]), hv(xs[:, i, :]), bc(dsk_.unsqueeze(2), P, 32, 64), mul))
            split_to("z1.1", 2)
            for n in range(2):
                ps = full(ve, ("cb", n))
                empty(TT(cbm[:, n, :].rearrange("p (a b) -> p a b", a=4), four(ps), bc(incl.unsqueeze(1), P, 4, P), mul),
                      ("cb", n))
            emptied(ve, ("cb", 0), ("cb", 1))

            def segs(z):
                n, u = divmod(z, 8)
                ps = full(ve, ("bc", n, u))
                if z >= 2:
                    ve.wait_ge(sem("wT_ready"), z - 1)
                for e in range(4):
                    hd = 4 * u + e
                    ins = TS(eT2[:, z % 2, P * e:P * e + P], ps[:, P * e:P * e + P], acs[:, n, hd:hd + 1], 0.0, sub, ALU.min)
                empty(ins, ("bc", n, u))
                emptied(ve, ("bc", n, u))
                ve.nop().then_inc(sem("seg_ready"), 1)

            def weigh(z):
                n, u = divmod(z, 8)
                g = u // 2
                ve.wait_ge(sem("seg_exp"), z + 1)
                if z >= 4:
                    zz = (z // 2) - 2
                    full(ve, ("yd", zz // 4, zz % 4))
                TT(wT[:, g % 2, 4 * (u % 2):4 * (u % 2) + 4, :], eT2[:, z % 2, :].rearrange("p (a b) -> p a b", a=4),
                   bc(cbm[:, n, P * g:P * g + P].unsqueeze(1), P, 4, P), mul).then_inc(sem("wT_ready"), 1)

            def join(z):
                n, g = divmod(z, 4)
                c = slice(512 * g, 512 * g + 512)
                ps = full(ve, ("yd", n, g))
                empty(TT(xs[:, n, c], xs[:, n, c], ps[:, :], add), ("yd", n, g))
                if n:
                    ps = full(ve, ("yo", g))
                    e8 = lambda a: a.rearrange("p (a b) -> p a b", a=8)
                    empty(TT(e8(xdd[:, c]), e8(ps[:, :]), bc(eac[:, 8 * g:8 * g + 8].unsqueeze(2), P, 8, 64), mul),
                          ("yo", g))
                    emptied(ve, ("yo", g), ("yd", n, g))
                    link(TT(xs[:, n, c], xs[:, n, c], xdd[:, c], add))

            for g in range(4):
                full(ve, ("sst", g))
            segs(0)
            for z in range(16):
                if z + 1 < 16:
                    segs(z + 1)
                weigh(z)
                if z % 4 == 3:
                    m = z // 4
                    split_to(f"z{2 + m // 2}.{m % 2}", 2)
                if z % 2 == 1 and z >= 3:
                    join(z // 2 - 1)
            join(7)
            emptied(ve, *[("yd", n, g) for n in range(2) for g in range(4)])
            for i in range(2):
                ve.wait_ge(sem("z_silu"), i + 1)
                TT(xs[:, i, :], xs[:, i, :], zrow[:, i, :], mul).then_inc(sem("yz_ready"), 1)
            ve.wait_ge(sem("yg_root"), 1)
            link(ve.reciprocal(var[:, :, 0:4], var[:, :, 0:4]))
            for i in range(2):
                v = xs[:, i, :].rearrange("p (a b) -> p a b", a=4)
                TT(v, v, bc(var[:, i, 0:4].unsqueeze(2), P, 4, 512), mul).then_inc(sem("yg_rows"), 1)
            for i in range(2):
                for q in range(4):
                    ps = full(ve, ("gT", i, q))
                    a = colat[("ssm_gnorm_w_2", 0)] + 4 * q
                    empty(TT(four(yg[:, i, q, :]), four(ps), bc(cols[:, a:a + 4].unsqueeze(2), P, 4, P), mul), ("gT", i, q))
                    emptied(ve, ("gT", i, q))
                    ve.nop().then_inc(sem("yg_scaled"), 1)
            for i in range(2):
                for q in range(4):
                    ve.wait_ge(sem("yg_upper"), 4 * i + q + 1)
                    c = (slice(None), slice(4 * q, 4 * q + 4), slice(P * i, P * i + P))
                    TT(ygT[1][c], four(yg[:, i, q, :]), ygT[0][c].bitcast(F32), sub).then_inc(sem("ygT_ready"), 1)
            split_to("so7", 2)

            def plain_join(key):
                for i in range(2):
                    for f in range(2):
                        c = slice(512 * f, 512 * f + 512)
                        ps = full(ve, (key, i, f))
                        empty(TT(h[:, i, c], h[:, i, c], ps[:, :], add), (key, i, f))
                emptied(ve, *[(key, i, f) for i in range(2) for f in range(2)])
                ve.nop().then_inc(sem("h_ready"), 2)

            def embed(m):
                n = 3 if m == 0 else 5
                norm(n, "ple_norm_w_2", 8 * m)
                lowered[0] += 1
                ve.wait_ge(sem("operand_uppers"), lowered[0])
                ps = full(ve, ("pT", m))
                empty(TT(pT[1][:, :, :], four(ps, 2), pT[0][:, :, :].bitcast(F32), sub), ("pT", m))
                split_to(f"pp{m}", 2)
                for f in range(2):
                    split_to(f"pg{m}{f}.1", 2)
                    for i in range(2):
                        z = 2 * f + i
                        c = slice(512 * f, 512 * f + 512)
                        emptied(ve, ("pg", m, f, i))
                        ps = full(ve, ("pp", m, f, i))
                        empty(TT(tmph[:, i, c], psg[:, z % 2, :], ps[:, :], mul), ("pp", m, f, i))
                        emptied(ve, ("pp", m, f, i))
                        ve.nop().then_inc(sem("ple_used"), 1)
                        TT(h[:, i, c], h[:, i, c], tmph[:, i, c], add).then_inc(sem("out_ready") if m else sem("ple_joined"), 1)
                if m == 0:
                    ve.wait_ge(sem("ple_joined"), 4)
                    ve.nop().then_inc(sem("h_ready"), 2)

            plain_join("so")
            embed(0)
            norm(4, "attn_norm_w_2")

            def head_norm(x, n, w, t_, count):
                for i in range(2):
                    link(TT(t_[:, i, :, :], x[:, i, :, :], x[:, i, :, :], mul))
                for i in range(2):
                    link(ve.tensor_reduce(var[:, i, 0:n], t_[:, i, :, :], AX.X, add))
                TS(var[:, :, 0:n], var[:, :, 0:n], 1.0 / 64, 1e-6, mul, add).then_inc(sem("hn_in"), 1)
                ve.wait_ge(sem("hn_root"), count)
                link(ve.reciprocal(rs8[:, :, 0:n], rs8[:, :, 0:n]))
                for i in range(2):
                    link(TT(x[:, i, :, :], x[:, i, :, :], bc(rs8[:, i, 0:n].unsqueeze(2), P, n, 64), mul))
                for i in range(2):
                    link(TT(x[:, i, :, :], x[:, i, :, :], bc(w.unsqueeze(1), P, n, 64), mul))

            split_to("kv.1", 2)
            for j in range(4):
                split_to(f"ain{j}.1", 2)
            emptied(ve, ("kv", 0), ("kv", 1))
            kx = kvr[:, :, 0:256].rearrange("p i (a b) -> p i a b", a=4)
            cut = lambda a, n: a[:, :, 0:64 * n].rearrange("p i (a b) -> p i a b", a=n)
            head_norm(kx, 4, kn_, cut(at1, 4), 1)
            rope(kx, 4, 2, cut(at1, 4), cut(at2, 4), cut(akr, 4))
            ve.nop().then_inc(sem("ak_rows"), 1)
            emptied(ve, *[("ain", j, i) for j in range(2) for i in range(2)])
            head_norm(h8(aq, 16), 16, qn, h8(at1, 16), 2)
            rope(h8(aq, 16), 16, 2, h8(at1, 16), h8(at2, 16), h8(aq, 16))
            for i in range(2):
                for u in range(2):
                    for o in range(2):
                        src = aq[:, i, 512 * u + 256 * o:512 * u + 256 * o + 256].rearrange("p (g d) -> p g d", g=4)
                        dst = aqr[:, i, 512 * u:512 * u + 512].rearrange("p (g o d) -> p g o d", g=4, o=2)[:, :, o, :]
                        ins = ve.tensor_copy(dst, src)
            ins.then_inc(sem("aq_rows"), 1)

            def softmax_in(z):
                n, u, o, gh = UNITS[z]
                nh, w = (4, P) if n == 0 else (2, 2 * P)
                hd = 8 * u + 4 * o + 2 * gh
                ps = full(ve, ("as", z))
                if z >= 2:
                    full(ve, ("eT", z - 2))
                s = asb[:, z % 2, :].rearrange("p (a b) -> p a b", a=nh)
                link(TS(asb[:, z % 2, :], ps[:, :], 0.125, None, mul))
                empty(TT(s, s, bc(const(f"att{n}").unsqueeze(1), P, nh, w), add), ("as", z))
                emptied(ve, ("as", z))
                m = mx[:, z % 2, 0:nh]
                link(ve.tensor_reduce(m, s, AX.X, mx_))
                link(TT(m, m, sinks[:, hd:hd + nh], mx_))
                link(TT(dsk[:, z % 2, 0:nh], sinks[:, hd:hd + nh], m, sub))
                TT(s, s, bc(m.unsqueeze(2), P, nh, w), sub).then_inc(sem("sub_ready"), 1)

            def softmax_out(z):
                n, u, o, gh = UNITS[z]
                nh, w = (4, P) if n == 0 else (2, 2 * P)
                hd = 8 * u + 4 * o + 2 * gh
                s = asb[:, z % 2, :].rearrange("p (a b) -> p a b", a=nh)
                ve.wait_ge(sem("exps"), z + 1)
                ve.wait_ge(sem("sink_exp"), z + 1)
                link(ve.tensor_reduce(den[:, z, 0:nh], s, AX.X, add))
                link(TT(den[:, z, 0:nh], den[:, z, 0:nh], dsk[:, z % 2, 0:nh], add))
                link(ve.reciprocal(den[:, z, 0:nh], den[:, z, 0:nh]))
                ps = full(ve, ("ao", z))
                dst = ao[:, n, 64 * hd:64 * hd + 64 * nh].rearrange("p (a b) -> p a b", a=nh)
                empty(TT(dst, ps[:, 0:64 * nh].rearrange("p (a b) -> p a b", a=nh),
                         bc(den[:, z, 0:nh].unsqueeze(2), P, nh, 64), mul), ("ao", z))

            softmax_in(0)
            for z in range(len(UNITS)):
                if z + 1 < len(UNITS):
                    softmax_in(z + 1)
                softmax_out(z)
            emptied(ve, *[("ao", z) for z in range(len(UNITS))])
            emptied(ve, *[("ain", 2 + j, i) for j in range(2) for i in range(2)])
            TT(ao[:, :, :], ao[:, :, :], ag[:, :, :], mul).then_inc(sem("ao_rows"), 1)
            for i in range(2):
                for q in range(2):
                    lower_of(aoT, ("aoT", i, q), 4 * q, i)
            split_to("ao3", 2)
            plain_join("fo")
            embed(1)


def kernel(**inputs):
    import concourse.bacc as bacc
    from concourse.bass_utils import run_bass_kernel_spmd as run

    nc = bacc.Bacc("TRN2", target_bir_lowering=False, num_devices=1)
    where, table = constants()
    arrays, io = {}, {}
    for name, a in list(inputs.items()) + [("table", table)]:
        a = np.ascontiguousarray(a)
        arrays[f"in_{name}"] = a
        io[name] = nc.dram_tensor(f"in_{name}", a.shape, mybir.dt.from_np(a.dtype), kind="ExternalInput").ap()
    out = nc.dram_tensor("out", (1, T, D), F32, kind="ExternalOutput").ap()
    build(nc, io, out, where, table.shape[1])
    r = run(nc, [arrays], core_ids=[0])
    return r.results[0]["out"]
```

```python
from contextlib import ExitStack

import numpy as np
import concourse.bass as bass
from concourse import mybir

F32 = mybir.dt.float32
F32R = mybir.dt.float32r
I32 = mybir.dt.int32
ALU = mybir.AluOpType
ACT = mybir.ActivationFunctionType
AX = mybir.AxisListType

P = 128
D = 1024
KT = D // P
T = 256
NEG = -1.0e30
GAMMA = [1.0 - 2.0 ** (-5 - h) for h in range(8)]
LEVELS = 7


def constants():
    r = np.arange(P)
    row, col = r[:, None], r[None, :]
    parts = {}
    parts["ident"] = (row == col)
    parts["incl"] = (row <= col)
    parts["strict"] = (row < col)
    parts["ones"] = np.ones((P, P))
    parts["blk"] = (row // 64 == col // 64)
    parts["blkret"] = np.repeat(parts["blk"][:, ::64], P, axis=1)
    for k in range(LEVELS):
        same = (row >> (k + 1)) == (col >> (k + 1))
        parts[f"off{k}"] = same & (((col >> k) & 1) == 1) & (((row >> k) & 1) == 0)
    parts["off0L"] = parts["off0"].T
    causal = np.where(col <= row, 0.0, NEG)
    before = np.where(col > row, 0.0, NEG)
    parts["att0"] = causal
    parts["att1"] = np.concatenate([before, causal], axis=1)
    lg = np.log1p(-np.exp2(-5.0 - np.arange(8)))
    parts["gq"] = np.exp((r[:, None] + 1.0) * lg[None])
    parts["gk"] = np.exp((127.0 - r[:, None]) * lg[None]) * 0.125
    inv = (10000.0 ** (-np.arange(32) / 32)).astype(np.float32)
    parts["inv"] = np.broadcast_to(inv[None], (P, 32))
    where, at = {}, 0
    for n, a in parts.items():
        where[n] = (at, a.shape[1])
        at += a.shape[1]
    return where, np.concatenate([np.asarray(a, np.float32) for a in parts.values()], axis=1)


def weight_units():
    out = []

    def turned(name, w, c0, cols):
        for j in range(cols // 256):
            out.append((f"{name}{j}", w, 0, KT, c0 + 256 * j, 256))

    def rows(name, w, c0):
        for half in range(2):
            out.append((f"{name}.{half}", w, 4 * half * P, 4, c0, 512))

    def deep(name, w, n):
        for t in range(0, n, 2):
            out.append((f"{name}{t // 2}", w, t * P, 2, 0, D))

    turned("rw", "w_in", 0, 1792)
    for n, name in enumerate(["q", "k", "v0", "v1", "g0", "g1", "s0", "s1", "s2", "s3"]):
        rows("r" + name, "w_in", 1792 + 512 * n)
    deep("brw", "w_branch_rw", 4)
    deep("bret", "w_branch_ret", 8)
    deep("wo", "w_out", 8)
    for j in range(11):
        for part, c0 in (("g", 0), ("v", 2816)):
            out.append((f"up{j}{part}", "ffn_w_up", 0, KT, c0 + 256 * j, 256))
    deep("dn", "ffn_w_down", 22)
    turned("xbc", "ssm_in_w_2", 2048, 3072)
    out.append(("dt", "ssm_in_w_2", 0, KT, 5120, 32))
    for j in range(4):
        rows(f"z{j}", "ssm_in_w_2", 512 * j)
    deep("so", "ssm_out_w_2", 16)

    def embed(m):
        out.append((f"pp{m}", f"ple_proj_w_2:{m}", 0, 2, 0, D))
        rows(f"pg{m}0", f"ple_gate_w_2:{m}", 0)
        rows(f"pg{m}1", f"ple_gate_w_2:{m}", 512)

    embed(0)
    rows("kv", "kv_w_2", 0)
    for j in range(4):
        rows(f"ain{j}", "attn_in_w_2", 512 * j)
    deep("ao", "attn_out_w_2", 8)
    embed(1)
    return out


LOADS = 3
PARTS = 2
SLOT = 2048
ARENA = 26128

STAGES = [
    [("norm_mix_pre", 0, 8), ("norm_ffn_pre", 0, 8), ("ssm_norm_w_2", 0, 8), ("ple_norm_w_2", 0, 8),
     ("kv_norm_w_2", 0, 8), ("attn_norm_w_2", 0, 8), ("ple_norm_w_2", 8, 8), ("rw_mu", 0, 14), ("rw_w0", 0, 4),
     ("rw_a0", 0, 4), ("rw_k_k", 0, 4), ("rw_k_a", 0, 4), ("rw_r_k", 0, 4), ("rw_lnx_w", 0, 4),
     ("rw_lnx_b", 0, 4), ("ssm_gnorm_w_2", 0, 16)],
    [("ffn_conv_w", 0, 88)],
    [("ffn_conv_w", 88, 44), ("ffn_conv_b", 0, 44)],
    [("ssm_conv_w_2", 0, 96), ("ssm_conv_b_2", 0, 24)],
]


def build(nc, io, out, where, ncols):
    ctx = ExitStack()
    with ctx:
        def sb(name, shape, dt=F32):
            return ctx.enter_context(nc.sbuf_tensor(name, shape, dt))

        sems = {}

        def sem(name):
            if name not in sems:
                sems[name] = ctx.enter_context(nc.semaphore(name))
            return sems[name]

        consts = sb("consts", [P, ncols])
        loaded = sb("loaded", [P, LOADS * SLOT])
        upper = sb("upper", [P, PARTS * SLOT], F32R)
        lower = sb("lower", [P, PARTS * SLOT], F32R)
        cols = sb("cols", [P, 512])
        lora = sb("lora", [P, 2, 512])
        postw = sb("postw", [P, D])
        rowp = sb("rowp", [P, 64 + 64 + 16 + 32 * 3])
        h = sb("h", [P, 2, D])
        xT = (sb("xT_upper", [P, KT, T], F32R), sb("xT_lower", [P, KT, T], F32R))
        small = sb("small", [P, 1408])
        posi = sb("posi", [P, 4], I32)
        arena_at = (nc.sbuf_base + 31) // 32 * 32
        arena = sb("arena", [P, ARENA])
        split_arena = nc.alloc_sbuf_tensor_at("split_arena", [P, ARENA], F32R, offset=arena_at)
        PS = [ctx.enter_context(nc.psum_tensor(f"bank{b}", [P, 512], F32)) for b in range(8)]

        def const(name):
            a, n = where[name]
            return consts[:, a:a + n]

        ident = const("ident")

        def ar(at, *shape, of=arena):
            n = int(np.prod(shape))
            v = of[:, at:at + n]
            if len(shape) == 2:
                v = v.rearrange("p (a b) -> p a b", a=shape[0])
            if len(shape) == 3:
                v = v.rearrange("p (a b c) -> p a b c", a=shape[0], b=shape[1])
            if len(shape) == 4:
                v = v.rearrange("p (a b c d) -> p a b c d", a=shape[0], b=shape[1], c=shape[2])
            return v

        def sm(at, *shape):
            n = int(np.prod(shape))
            v = small[:, at:at + n]
            if len(shape) == 2:
                v = v.rearrange("p (a b) -> p a b", a=shape[0])
            if len(shape) == 3:
                v = v.rearrange("p (a b c) -> p a b c", a=shape[0], b=shape[1])
            return v

        def two(at, at2, *shape):
            return ar(at, *shape, of=split_arena), ar(at2, *shape, of=split_arena)

        hs = ar(0, 2, D)
        tmph = hs
        pr = ar(2048, 14, 257)
        dif = ar(5648, 14, 256)
        ld, av, kn = ar(5648, 4, 256), ar(6672, 4, 256), ar(7696, 4, 256)
        qr, kr = ar(9232, 2, 512), ar(10256, 2, 512)
        cc, gT = ar(11280, 4, 256), ar(12304, 4, 256)
        zr = ar(13328, 4, 2, 256)
        bt, kt = ar(15376, 4, 2, P), ar(16400, 4, 2, P)
        vrow, yrow = ar(17424, 2, 512), ar(5648, 2, 512)
        krow, brow, sa, rhs = ar(0, 512), ar(512, 512), ar(1024, 512), ar(1536, 512)
        s0 = ar(18448, 4, P)
        stage = ar(18448, 4, P)
        mats = ar(18960, 8, 4, P)
        ex, ex2, ex3 = ar(18960, 4, 256), ar(19984, 4, 256), ar(21008, 4, 256)
        lor = ar(22032, 2, 256)
        inv, invT, t1, lk = ar(23056, 8, P), ar(24080, 8, P), ar(25104, 8, P), ar(11280, 8, P)
        mid = ar(25616, 8)
        yrw = ar(16400, 4, T)
        yrwT = two(15376, 12304, 4, T)
        vr, gr = h, ar(19472, 2, D)
        sg = ar(21520, 2, 2, D)
        qT, kTr = ar(5648, 4, T), ar(6672, 4, T)
        sT = ar(7696, 8, P)
        rst = ar(11280, 4, T)
        orow = ar(13328, 2, D)
        oT = two(2048, 4096, KT, T)
        ro = lora
        mrow, mT = ar(13328, 2, D), two(9232, 11280, KT, T)
        mtmp = ar(17424, 512)
        actT = two(2048, 7680, 22, T)
        acc = ar(13312, 2, 4, T)
        zrow = ar(2048, 2, 2048)
        xbc = ar(6144, 24, T)
        cbm = ar(6144, 2, 512)
        xs = ar(12288, 2, 2048)
        cacc = ar(16384, 4, T)
        xd = ar(16384, 2, 2048)
        xdd = ar(20480, 2048)
        wT = ar(22528, 2, 8, P)
        eT2 = ar(24576, 2, 512)
        bR = ar(25600, 512)
        ss0 = ar(0, 4, 512)
        yg = ar(2048, 2, 4, 512)
        ygT = two(16384, 20480, 16, T)
        prow, pT = ar(2048, 2, T), two(2560, 3072, 2, T)
        psg = ar(3584, 2, 512)
        xT2 = two(20480, 22528, KT, T)
        kvr = ar(4096, 2, 512)
        aq, ag = ar(5120, 2, D), ar(7168, 2, D)
        at1, at2 = ar(9216, 2, D), ar(11264, 2, D)
        aqr = ar(13312, 2, D)
        aqT = ar(15360, 2, 4, T)
        akT = ar(17408, 2, T)
        akr = ar(17920, 2, T)
        asb = ar(18432, 2, 512)
        aeT = ar(20480, 2, 512)
        ao = ar(21504, 2, D)
        aoT = two(9216, 11264, KT, T)
        ssq, rstd = sm(0, 4), sm(4, 4)
        mean, var, rs8 = sm(8, 2, 32), sm(72, 2, 32), sm(136, 2, 32)
        dtv, adt, acs = sm(200, 2, 32), sm(264, 2, 32), sm(328, 2, 32)
        tot, dte, eac = sm(392, 32), sm(424, 32), sm(456, 32)
        arow = sm(488, 32)
        ang, cosd, sind = sm(520, 4, 32), sm(648, 4, 64), sm(904, 4, 64)
        angn = sm(1160, 4, 32)
        posf = sm(1288, 4)
        fcol = sm(1292, 4)
        om = sm(1296, 4)
        den, dsk = sm(1308, 12, 4), sm(1356, 2, 4)
        eps6 = sm(1364, 1)
        mx = sm(1366, 4, 4)
        nsinks = sm(1384, 16)
        qn, kn_, sinks, dtb, alog, dsk_ = (rowp[:, 0:64], rowp[:, 64:128], rowp[:, 128:144], rowp[:, 144:176],
                                           rowp[:, 176:208], rowp[:, 208:240])

        colat, at = {}, 0
        for g, parts in enumerate(STAGES):
            at = [0, 114, 202, 290][g]
            for name, r0, n in parts:
                colat[(name, r0)] = at
                at += n

        def pc(name, j, r0=0):
            a = colat[(name, r0)] + j
            return cols[:, a:a + 1]

        def pcs(name, n, r0=0):
            a = colat[(name, r0)]
            return cols[:, a:a + n]

        def fcw(tap, c):
            return cols[:, 114 + 44 * tap + c:115 + 44 * tap + c]

        def fcb(c):
            return cols[:, 202 + 44 + c:203 + 44 + c]

        def scw(tap, c):
            return cols[:, 290 + 24 * tap + c:291 + 24 * tap + c]

        def scb(c):
            return cols[:, 290 + 96 + c:291 + 96 + c]

        units = weight_units()
        index = {u[0]: n for n, u in enumerate(units)}
        unit_landed = [sem(f"unit_landed{s}") for s in range(LOADS)]
        uppers, lowers = sem("unit_uppers"), sem("unit_lowers")
        units_used, used_count = sem("units_used"), [0]
        unit_done = {}

        def part(of, slots, n):
            nk, width = units[n][3], units[n][5]
            at = (n % slots) * SLOT
            return of[:, at:at + nk * width]

        def tiles(ap, n):
            return ap.rearrange("p (k c) -> p k c", k=units[n][3])

        def part_free(eng, n):
            if n >= PARTS:
                eng.wait_ge(*unit_done[n - PARTS])

        psum_full = [sem(f"psum_full{b}") for b in range(8)]
        psum_emptied = [sem(f"psum_emptied{b}") for b in range(8)]
        uses, use_of = [0] * 8, {}

        def take(pe, key, bank):
            if uses[bank]:
                pe.wait_ge(psum_emptied[bank], uses[bank])
            uses[bank] += 1
            use_of[key] = (bank, uses[bank])
            return PS[bank]

        def fill(ins, key):
            ins.then_inc(psum_full[use_of[key][0]], 1)

        def full(eng, key):
            bank, n = use_of[key]
            eng.wait_ge(psum_full[bank], n)
            return PS[bank]

        def empty(ins, key):
            ins.then_inc(psum_emptied[use_of[key][0]], 1)

        def emptied(eng, *keys):
            for key in keys:
                bank, n = use_of[key]
                eng.wait_ge(psum_emptied[bank], n)

        NORMS = ["norm_mix_pre", "norm_ffn_pre", "ssm_norm_w_2", "ple_norm_w_2", "attn_norm_w_2", "ple_norm_w_2"]
        norm_keys = lambda n: [("nT", n, i, q) for i in range(2) for q in range(2)]
        UNITS = [(n, u, o, gh) for u in range(2) for n in range(2) for o in range(2) for gh in range(n + 1)]
        HEADS = [4 if n == 0 else 2 for n, _, _, _ in UNITS]
        block = ctx.enter_context(nc.Block())

        @block.tensor
        def _(pe):
            mm = pe.matmul

            def turns(key, bank, ins):
                ps = take(pe, key, bank)
                for j, a in enumerate(ins):
                    m, n = a.shape
                    last = pe.transpose(ps[0:n, j * P:j * P + m], a, ident[0:m, 0:m])
                fill(last, key)

            def norm_turns(n):
                for i in range(2):
                    pe.wait_ge(sem("rows_scaled"), 2 * n + i + 1)
                    for q in range(2):
                        turns(("nT", n, i, q), (0 if n in (3, 5) else 4) + 2 * i + q, [hs[:, i, P * (4 * q + j):P * (4 * q + j + 1)]
                                                               for j in range(4)])

            def mm3(out, a, b, start, stop):
                mm(out, a[0], b[0], start=start, stop=False)
                mm(out, a[0], b[1], start=False, stop=False)
                return mm(out, a[1], b[0], start=False, stop=stop)

            def unit(name):
                n = index[name]
                pe.wait_ge(lowers, n + 1)
                return tiles(part(upper, PARTS, n), n), tiles(part(lower, PARTS, n), n)

            def both(x, *at):
                return x[0][at], x[1][at]

            def used(name, last=None, key=None):
                if key is None:
                    used_count[0] += 1
                    last.then_inc(units_used, 1)
                    unit_done[index[name]] = (units_used, used_count[0])
                else:
                    unit_done[index[name]] = (psum_full[use_of[key][0]], use_of[key][1])

            every = slice(None)

            def turned(name, keys, banks, norm=None):
                w = unit(name)
                for c in range(2):
                    ps = take(pe, keys[c], banks[c])
                    for k in range(KT):
                        if norm is not None and c == 0 and k % 4 == 0:
                            xT_ready(norm, 2 + k // 2)
                        last = mm3(ps[:, 0:T], both(w, every, k, slice(c * P, c * P + P)), both(xT, every, k, every),
                                   k == 0, k == KT - 1)
                    fill(last, keys[c])
                used(name, key=keys[1])

            def deep_product(name, n, xt, key, banks, before={}):
                ps = {(i, f): take(pe, (key, i, f), banks + 2 * i + f) for i in range(2) for f in range(2)}
                for t in range(n):
                    if t in before:
                        before[t]()
                    if t % 2 == 0:
                        w = unit(f"{name}{t // 2}")
                    for i in range(2):
                        for f in range(2):
                            last = mm3(ps[i, f][:, :], both(xt, every, t, slice(i * P, i * P + P)),
                                       both(w, every, t % 2, slice(512 * f, 512 * f + 512)), t == 0, t == n - 1)
                            if t == n - 1:
                                fill(last, (key, i, f))
                    if t == n - 1:
                        used(f"{name}{t // 2}", key=(key, 1, 1))
                    elif t % 2:
                        used(f"{name}{t // 2}", last)

            def rows_half(name, half, ps, keys, x, ready=None):
                w = unit(f"{name}.{half}")
                for i in range(2):
                    if ready:
                        ready(2 * half + i + 1)
                    for k in range(4):
                        last = mm3(ps[i][:, :], both(x, every, 4 * half + k, slice(i * P, i * P + P)),
                                   both(w, every, k, every), half + k == 0, half == 1 and k == 3)
                    if half:
                        fill(last, keys[i])
                used(f"{name}.{half}", *((last,) if half == 0 else (None, keys[1])))

            def rows(name, keys, banks, x, ready=None):
                ps = [take(pe, keys[i], banks[i]) for i in range(2)]
                for half in range(2):
                    rows_half(name, half, ps, keys, x, ready)

            def xT_ready(n, pieces):
                pe.wait_ge(sem("xT_lower_ready"), 4 * n + pieces)

            pe.wait_ge(sem("consts_landed"), 16)
            norm_turns(0)
            pe.wait_ge(sem("stage_landed"), 16 * sum(len(s) for s in STAGES))
            for g, parts in enumerate(STAGES):
                n = sum(p[2] for p in parts)
                turns(("cols", g), g, [stage[0:n, g, :]])
            for j in range(7):
                turned(f"rw{j}", [("rw", 2 * j), ("rw", 2 * j + 1)], (2 * (j % 2), 2 * (j % 2) + 1),
                       0 if j == 0 else None)
            rows("rq", [("rq", i) for i in range(2)], (4, 5), xT)
            pe.wait_ge(sem("lora_in"), 2)
            pe.wait_ge(sem("shifted"), 14)
            pe.wait_ge(sem("lora_landed"), 48)
            for p in range(4):
                ps = take(pe, ("w", p), p % 2)
                fill(mm(ps[:, 0:T], lora[0:64, 0, P * p:P * p + P], lor[0:64, 0, :], start=True, stop=True), ("w", p))
                ps = take(pe, ("a", p), 2 + p % 2)
                fill(mm(ps[:, 0:T], lora[64:128, 0, P * p:P * p + P], pr[64:128, 12, 1:257],
                        start=True, stop=True), ("a", p))
                ps = take(pe, ("g", p), 4 + p % 2)
                fill(mm(ps[:, 0:T], lora[:, 1, P * p:P * p + P], lor[:, 1, :], start=True, stop=True), ("g", p))
            rows("rk", [("rk", i) for i in range(2)], (6, 7), xT)
            pe.wait_ge(sem("kk_squared"), 1)
            for p in range(4):
                ps = take(pe, ("ss", p), p)
                fill(mm(ps[:, 0:T], const("blk"), ex[:, p, :], start=True, stop=True), ("ss", p))
            for i in range(2):
                turns(("vT", i), 6 + i, [pr[:, 8 + p, 1 + P * i:1 + P * i + P] for p in range(4)])
            rows("rv0", [("rv", 0, i) for i in range(2)], (4, 5), xT)
            pe.wait_ge(sem("rk_ready"), 1)
            for p in range(4):
                ps = take(pe, ("bs", p), p)
                fill(mm(ps[:, 0:T], const("blk"), ex2[:, p, :], start=True, stop=True), ("bs", p))
            rows("rv1", [("rv", 1, i) for i in range(2)], (6, 7), xT)
            pe.wait_ge(sem("decayed"), 1)
            for n in range(2):
                if n == 0:
                    turns(("kbT", 0), 6, [kt[:, p, 0, :] for p in range(4)])
                    turns(("kbT", 1), 7, [bt[:, p, 0, :] for p in range(4)])
                for hd in range(8):
                    p, o = hd // 2, hd % 2
                    r = slice(64 * o, 64 * o + 64)
                    ps = take(pe, ("m", n, hd), hd % 4)
                    mm(ps[:, 0:256], bt[r, p, n, :], zr[r, p, n, :], start=True, stop=True)
                    fill(mm(ps[:, 256:512], kt[r, p, n, :], zr[r, p, n, :], start=True, stop=True), ("m", n, hd))
                for o in range(2):
                    r = slice(64 * o, 64 * o + 64)
                    ps = take(pe, ("L", n, o), 4 + o)
                    for p in range(4):
                        last = mm(ps[:, P * p:P * p + P], zr[r, p, n, 0:P], bt[r, p, n, :], start=True, stop=True)
                    fill(last, ("L", n, o))
                pe.wait_ge(sem("inv_start"), n + 1)
                for k in range(1, LEVELS):
                    for q in range(2):
                        pe.wait_ge(sem("lk_ready"), 12 * n + 2 * (k - 1) + q + 1)
                        if k > 1:
                            emptied(pe, ("x", n, k - 1, q), ("xt", n, k - 1, q))
                        ps = take(pe, ("t1", n, k, q), 4 + q)
                        for e in range(4):
                            last = mm(ps[:, P * e:P * e + P], lk[:, 4 * q + e, :], inv[:, 4 * q + e, :],
                                      start=True, stop=True)
                        fill(last, ("t1", n, k, q))
                    for q in range(2):
                        emptied(pe, ("t1", n, k, q))
                        for key, a, b, bank in ((("x", n, k, q), invT, t1, 2 * q), (("xt", n, k, q), t1, invT, 2 * q + 1)):
                            ps = take(pe, key, bank)
                            for e in range(4):
                                hd = 4 * q + e
                                last = mm(ps[:, P * e:P * e + P], a[:, hd, :], b[:, hd, :], start=True, stop=True)
                            fill(last, key)
                emptied(pe, ("vT", 0), ("vT", 1))
                if n:
                    pe.wait_ge(sem("state_ready"), 1)
                ps = take(pe, ("rhs", n), 6)
                for p in range(4):
                    if n:
                        mm(ps[:, P * p:P * p + P], zr[:, p, n, 0:P], s0[:, p, :], start=True, stop=False)
                    for o in range(2):
                        hd = 2 * p + o
                        last = mm(ps[:, 64 * hd:64 * hd + 64], mats[:, hd, 2, :], vrow[:, n, 64 * hd:64 * hd + 64],
                                  start=(n == 0), stop=(n == 0 or o == 1))
                fill(last, ("rhs", n))
                emptied(pe, ("rhs", n), ("x", n, LEVELS - 1, 0), ("x", n, LEVELS - 1, 1),
                        ("xt", n, LEVELS - 1, 0), ("xt", n, LEVELS - 1, 1))
                ps = take(pe, ("sa", n), 7)
                for hd in range(8):
                    last = mm(ps[:, 64 * hd:64 * hd + 64], invT[:, hd, :], rhs[:, 64 * hd:64 * hd + 64],
                              start=True, stop=True)
                fill(last, ("sa", n))
                emptied(pe, ("sa", n))
                ps = take(pe, ("y", n), 6)
                for p in range(4):
                    if n:
                        mm(ps[:, P * p:P * p + P], zr[:, p, n, P:2 * P], s0[:, p, :], start=True, stop=False)
                    for o in range(2):
                        hd = 2 * p + o
                        c = slice(64 * hd, 64 * hd + 64)
                        mm(ps[:, c], mats[:, hd, 3, :], vrow[:, n, c], start=(n == 0), stop=False)
                        last = mm(ps[:, c], mats[:, hd, 1, :], sa[:, c], start=False, stop=(n == 0 or o == 1))
                fill(last, ("y", n))
                if n == 0:
                    emptied(pe, ("kbT", 0), ("kbT", 1))
                    ps = take(pe, ("st",), 7)
                    for p in range(4):
                        c = slice(P * p, P * p + P)
                        mm(ps[:, c], krow[:, c], vrow[:, 0, c], start=True, stop=False)
                        last = mm(ps[:, c], brow[:, c], sa[:, c], start=False, stop=True)
                    fill(last, ("st",))
            def gate(f):
                name, key = (f"rg{f}", "rg") if f < 2 else (f"rs{f - 2}", "rs")
                rows(name, [(key, f % 2 if f < 2 else f - 2, i) for i in range(2)], (0, 1) if f % 2 == 0 else (2, 3), xT)

            def scores_of(n):
                for o in range(2):
                    r = slice(64 * o, 64 * o + 64)
                    ps = take(pe, ("s", n, o), 6 + o)
                    for p in range(4):
                        last = mm(ps[:, P * p:P * p + P], kTr[r, p, P * n:P * n + P], qT[r, p, P * n:P * n + P],
                                  start=True, stop=True)
                    fill(last, ("s", n, o))

            def outputs_of(n):
                emptied(pe, ("s", n, 0), ("s", n, 1))
                if n:
                    emptied(pe, ("R", 0), ("R", 1))
                for g in range(2):
                    ps = take(pe, ("o", n, g), 4 + g)
                    for e in range(2):
                        p = 2 * g + e
                        if n:
                            mm(ps[:, 256 * e:256 * e + 256], qT[:, p, P:2 * P], rst[:, p, :], start=True, stop=False)
                        for o in range(2):
                            hd = 2 * p + o
                            last = mm(ps[:, 256 * e + P * o:256 * e + P * o + P], sT[:, hd, :],
                                      vr[:, n, P * hd:P * hd + P], start=(n == 0), stop=(n == 0 or o == 1))
                    fill(last, ("o", n, g))

            gate(0)
            pe.wait_ge(sem("y_rows"), 1)
            for i in range(2):
                turns(("yT", i), 4 + i, [yrow[:, i, P * p:P * p + P] for p in range(4)])
            pe.wait_ge(sem("qk_rope"), 2)
            for i in range(2):
                turns(("qT", i), 6, [qr[:, i, P * p:P * p + P] for p in range(4)])
                turns(("kTr", i), 7, [kr[:, i, P * p:P * p + P] for p in range(4)])
            gate(1)
            emptied(pe, ("rv", 0, 0), ("rv", 1, 0), ("rv", 0, 1), ("rv", 1, 1))
            for g in range(2):
                ps = take(pe, ("R", g), 4 + g)
                for e in range(2):
                    p = 2 * g + e
                    last = mm(ps[:, 256 * e:256 * e + 256], kr[:, 0, P * p:P * p + P], vr[:, 0, 256 * p:256 * p + 256],
                              start=True, stop=True)
                fill(last, ("R", g))
            emptied(pe, ("qT", 0), ("qT", 1), ("kTr", 0), ("kTr", 1))
            scores_of(0)
            gate(2)
            outputs_of(0)
            scores_of(1)
            gate(3)
            outputs_of(1)
            gate(4)
            gate(5)
            pe.wait_ge(sem("o_rows"), 1)
            for i in range(2):
                for q in range(2):
                    turns(("oT", i, q), 4 + 2 * i + q, [orow[:, i, P * (4 * q + j):P * (4 * q + j) + P] for j in range(4)])
            pe.wait_ge(sem("yrwT_ready"), 1)
            deep_product("brw", 4, yrwT, "brw", 0)
            emptied(pe, *[("oT", i, q) for i in range(2) for q in range(2)])
            deep_product("bret", 8, oT, "bret", 4)
            pe.wait_ge(sem("merged"), 1)
            for i in range(2):
                for q in range(2):
                    turns(("mT", i, q), 4 + 2 * i + q, [mrow[:, i, P * (4 * q + j):P * (4 * q + j) + P] for j in range(4)])
            emptied(pe, *[("mT", i, q) for i in range(2) for q in range(2)])
            deep_product("wo", 8, mT, "wo", 0)
            norm_turns(1)
            for j in range(11):
                for v, name in enumerate("gv"):
                    b = 4 * (j % 2) + 2 * v
                    turned(f"up{j}{name}", [("up", j, 2 * v), ("up", j, 2 * v + 1)], (b, b + 1),
                           1 if j == v == 0 else None)
            pe.wait_ge(sem("act_ready"), 22)
            deep_product("dn", 22, actT, "dn", 0)
            norm_turns(2)
            for j in range(12):
                turned(f"xbc{j}", [("xbc", 2 * j), ("xbc", 2 * j + 1)], (2 * (j % 2), 2 * (j % 2) + 1),
                       2 if j == 0 else None)
            ps = take(pe, ("dt",), 4)
            w = unit("dt")
            for i in range(2):
                for k in range(KT):
                    last = mm3(ps[:, 32 * i:32 * i + 32], both(xT, every, k, slice(i * P, i * P + P)),
                               both(w, every, k, every), k == 0, k == KT - 1)
            fill(last, ("dt",))
            used("dt", key=("dt",))
            z_keys = lambda j: [("z", j, i) for i in range(2)]
            rows("z0", z_keys(0), (0, 1), xT)
            pe.wait_ge(sem("adt_ready"), 1)
            ps = take(pe, ("ac",), 5)
            for n in range(2):
                mm(ps[:, 32 * n:32 * n + 32], const("incl"), adt[:, n, :], start=True, stop=True)
            fill(mm(ps[:, 64:96], const("ones"), adt[:, 0, :], start=True, stop=True), ("ac",))
            pe.wait_ge(sem("xbc_ready"), 24)
            for i in range(2):
                for q in range(4):
                    turns(("xsT", i, q), 6 + q % 2, [xbc[:, 4 * q + j, P * i:P * i + P] for j in range(4)])
            turns(("bR",), 6, [xbc[:, 16 + g, 0:P] for g in range(4)])
            rows("z1", z_keys(1), (2, 3), xT)
            for n in range(2):
                ps = take(pe, ("cb", n), 7)
                for g in range(4):
                    last = mm(ps[:, P * g:P * g + P], xbc[:, 16 + g, P * n:P * n + P], xbc[:, 20 + g, P * n:P * n + P],
                              start=True, stop=True)
                fill(last, ("cb", n))
            pe.wait_ge(sem("xd_ready"), 3)
            emptied(pe, ("bR",))
            for g in range(4):
                ps = take(pe, ("sst", g), 4 + g % 2)
                fill(mm(ps[:, :], bR[:, P * g:P * g + P], xdd[:, 512 * g:512 * g + 512], start=True, stop=True), ("sst", g))

            def spread(n, u):
                ps = take(pe, ("bc", n, u), u % 2)
                for e in range(4):
                    hd = 4 * u + e
                    last = mm(ps[:, P * e:P * e + P], adt[:, n, hd:hd + 1].to_broadcast([P, P]), const("incl"),
                              start=True, stop=True)
                fill(last, ("bc", n, u))

            spread(0, 0)
            spread(0, 1)
            for n in range(2):
                for g in range(4):
                    if 4 * n + g < 7:
                        nn, ng = divmod(4 * n + g + 1, 4)
                        spread(nn, 2 * ng)
                        spread(nn, 2 * ng + 1)
                    pe.wait_ge(sem("wT_ready"), 2 * (4 * n + g) + 2)
                    ps = take(pe, ("yd", n, g), 2 + g % 2)
                    for e in range(8):
                        hd = 8 * g + e
                        last = mm(ps[:, 64 * e:64 * e + 64], wT[:, g % 2, e, :], xd[:, n, 64 * hd:64 * hd + 64],
                                  start=True, stop=True)
                    fill(last, ("yd", n, g))
                    if n:
                        emptied(pe, ("sst", g))
                        ps = take(pe, ("yo", g), 4 + g % 2)
                        fill(mm(ps[:, :], xbc[:, 20 + g, P:2 * P], ss0[:, g, :], start=True, stop=True), ("yo", g))
                    if g % 2 == 0:
                        m = 2 * n + g // 2
                        if m % 2 == 0:
                            zps = [take(pe, key, 6 + i) for i, key in enumerate(z_keys(2 + m // 2))]
                        rows_half(f"z{2 + m // 2}", m % 2, zps, z_keys(2 + m // 2), xT)
            pe.wait_ge(sem("yg_rows"), 2)
            for i in range(2):
                for q in range(4):
                    turns(("gT", i, q), 6 + q % 2, [xs[:, i, P * (4 * q + j):P * (4 * q + j) + P] for j in range(4)])
            pe.wait_ge(sem("ygT_ready"), 8)
            def embedding_turns(m):
                pe.wait_ge(sem("p_landed"), 16 * (m + 1))
                turns(("pT", m), 7, [prow[:, i, P * k:P * k + P] for k in range(2) for i in range(2)])

            deep_product("so", 16, ygT, "so", 0, {13: lambda: embedding_turns(0)})

            def embed(m):
                n = 3 if m == 0 else 5
                emptied(pe, ("pT", m))
                w = unit(f"pp{m}")
                for f in range(2):
                    for i in range(2):
                        ps = take(pe, ("pp", m, f, i), 4 + 2 * f + i)
                        for k in range(2):
                            last = mm3(ps[:, :], both(pT, every, k, slice(i * P, i * P + P)),
                                       both(w, every, k, slice(512 * f, 512 * f + 512)), k == 0, k == 1)
                        fill(last, ("pp", m, f, i))
                used(f"pp{m}", key=("pp", m, 1, 1))
                norm_turns(n)
                for f in range(2):
                    rows(f"pg{m}{f}", [("pg", m, f, i) for i in range(2)], (2 * f, 2 * f + 1), xT,
                         None if f else lambda pieces: xT_ready(n, pieces))

            embed(0)
            norm_turns(4)
            rows("kv", [("kv", i) for i in range(2)], (0, 1), xT2, lambda pieces: pe.wait_ge(sem("xT2_lower_ready"), pieces))
            AIN = ((2, 3), (0, 1), (2, 3), (2, 3))
            for j in range(2):
                rows(f"ain{j}", [("ain", j, i) for i in range(2)], AIN[j], xT,
                     None if j else lambda pieces: xT_ready(4, pieces))

            def ain_half(j, half, ps={}):
                if half == 0:
                    ps[j] = [take(pe, ("ain", j, i), AIN[j][i]) for i in range(2)]
                rows_half(f"ain{j}", half, ps[j], [("ain", j, i) for i in range(2)], xT)

            def query_turns(u):
                pe.wait_ge(sem("aq_rows"), u + 1)
                for i in range(2):
                    turns(("aqT", i, u), 4 + i, [aqr[:, i, 512 * u + P * g:512 * u + P * g + P] for g in range(4)])

            def out_turns(i, q, units, bank):
                pe.wait_ge(sem("ao_rows"), units)
                turns(("aoT", i, q), bank, [ao[:, i, P * (4 * q + j):P * (4 * q + j) + P] for j in range(4)])

            ain_half(2, 0)
            pe.wait_ge(sem("ak_rows"), 1)
            turns(("akT",), 6, [akr[:, i, P * u:P * u + P] for u in range(2) for i in range(2)])
            ain_half(2, 1)
            query_turns(0)
            emptied(pe, ("akT",), *[("aqT", i, 0) for i in range(2)])

            OUT_TURNS = {3: (0, 0, 2, 2), 7: (1, 0, 6, 3), 9: (0, 1, 8, 2)}

            def scores(z):
                n, u, o, gh = UNITS[z]
                r = slice(64 * o, 64 * o + 64)
                ps = take(pe, ("as", z), z % 2)
                nh, w = (4, P) if n == 0 else (2, 2 * P)
                for e in range(nh):
                    last = mm(ps[:, w * e:w * e + w], aqT[r, u, nh * gh * n + e, P * n:P * n + P], akT[r, u, 0:w],
                              start=True, stop=True)
                fill(last, ("as", z))

            def values(z):
                n, u, o, gh = UNITS[z]
                pe.wait_ge(sem("exps"), sum(HEADS[:z + 1]))
                turns(("eT", z), 4 + z % 2, [asb[:, z % 2, P * j:P * j + P] for j in range(4)])
                emptied(pe, ("eT", z))
                ps = take(pe, ("ao", z), 6 + z % 2)
                nh, kt_ = (4, 1) if n == 0 else (2, 2)
                for e in range(nh):
                    for s in range(kt_):
                        last = mm(ps[:, 64 * e:64 * e + 64], aeT[:, z % 2, P * (kt_ * e + s):P * (kt_ * e + s) + P],
                                  kvr[:, s, 256 + 64 * (2 * u + o):256 + 64 * (2 * u + o) + 64],
                                  start=(s == 0), stop=(s == kt_ - 1))
                fill(last, ("ao", z))

            scores(0)
            ain_half(3, 0)
            for z in range(len(UNITS)):
                if z + 1 < len(UNITS):
                    scores(z + 1)
                values(z)
                if z == 0:
                    ain_half(3, 1)
                if z == 2:
                    query_turns(1)
                    emptied(pe, *[("aqT", i, 1) for i in range(2)])
                if z in OUT_TURNS:
                    out_turns(*OUT_TURNS[z])
            out_turns(1, 1, 12, 4)
            deep_product("ao", 8, aoT, "fo", 0, {0: lambda: emptied(pe, ("aoT", 0, 0), ("aoT", 1, 0)),
                                                 4: lambda: emptied(pe, ("aoT", 0, 1), ("aoT", 1, 1)),
                                                 5: lambda: embedding_turns(1)})
            embed(1)

        @block.sync
        def _(sp):
            sp.dma_start(h[:, :, :], io["x"].rearrange("o (i p) d -> p (o i) d", p=P)).then_inc(sem("x_landed"), 16)
            sp.dma_start(consts[:, :], io["table"]).then_inc(sem("consts_landed"), 16)

            for n, (name, w, r0, nk, c0, width) in enumerate(units):
                w, _, layer = w.partition(":")
                src = io[w][int(layer or 0)] if len(io[w].shape) == 3 else io[w]
                if n >= LOADS:
                    sp.wait_ge(lowers, n - LOADS + 1)
                sp.dma_start(tiles(part(loaded, LOADS, n), n),
                             src[r0:r0 + nk * P, c0:c0 + width].rearrange("(k p) c -> p k c", p=P)) \
                    .then_inc(unit_landed[n % LOADS], 16)
            sp.wait_ge(sem("out_ready"), 4)
            sp.dma_start(out.rearrange("o (i p) d -> p (o i) d", p=P), h[:, :, :]).then_inc(sem("out_written"), 16)
            sp.wait_ge(sem("out_written"), 16)

        @block.gpsimd
        def _(pool):
            for g, parts in enumerate(STAGES):
                at = 0
                for name, r0, n in parts:
                    src = io[name]
                    if len(src.shape) == 3:
                        src = src[0].rearrange("t (r c) -> (t r) c", c=P)
                    elif len(src.shape) == 2 and name == "ple_norm_w_2":
                        src = src.rearrange("l (r c) -> (l r) c", c=P)
                    elif len(src.shape) == 2:
                        src = src[0].rearrange("(r c) -> r c", c=P)
                    else:
                        src = src.rearrange("(r c) -> r c", c=P)
                    pool.dma_start(stage[at:at + n, g, :], src[r0:r0 + n, :]).then_inc(sem("stage_landed"), 16)
                    at += n
            pool.dma_start(lora[0:64, 0, :], io["rw_w2"][0]).then_inc(sem("lora_landed"), 16)
            pool.dma_start(lora[64:128, 0, :], io["rw_a2"][0]).then_inc(sem("lora_landed"), 16)
            pool.dma_start(lora[:, 1, :], io["rw_g2"][0]).then_inc(sem("lora_landed"), 16)

            def spread_row(dst, src, s):
                pool.dma_start(dst, src.partition_broadcast(P)).then_inc(sem(s), 16)

            spread_row(postw[:, :], io["norm_mix_post"][0], "postw_landed")
            for dst, src in ((qn, io["q_norm_w_2"][0]), (kn_, io["k_norm_w_2"]), (sinks, io["attn_sinks_2"][0]),
                             (dtb, io["ssm_dt_bias_2"][0]), (alog, io["ssm_a_log_2"][0]), (dsk_, io["ssm_d_2"][0])):
                spread_row(dst, src, "rowp_landed")
            for m, name in enumerate(["positions", "positions_2"]):
                pool.dma_start(posi[:, 2 * m:2 * m + 2], io[name].rearrange("o (i p) -> p (o i)", p=P),
                               allow_slow_non_contiguous=True).then_inc(sem("pos_landed"), 16)
            for n in range(2):
                for k in range(1, LEVELS):
                    if k == 1:
                        pool.wait_ge(sem("mats_ready"), 8 * (n + 1))
                    for q in range(2):
                        if k > 1:
                            full(pool, ("t1", n, k - 1, q))
                        elif n:
                            full(pool, ("t1", 0, LEVELS - 1, q))
                        pool.tensor_tensor(lk[:, 4 * q:4 * q + 4, :], mats[:, 4 * q:4 * q + 4, 0, :],
                                           const(f"off{k}").unsqueeze(1).broadcast_to([P, 4, P]), ALU.mult) \
                            .then_inc(sem("lk_ready"), 1)
            full(pool, ("o", 1, 0))
            full(pool, ("o", 1, 1))
            pool.dma_start(h[:, :, :], io["x"].rearrange("o (i p) d -> p (o i) d", p=P)).then_inc(sem("x_again"), 16)
            pool.wait_ge(sem("h_ready"), 2)
            spread_row(postw[:, :], io["norm_ffn_post"][0], "postw_landed")
            for m in range(2):
                pool.wait_ge(sem("h_ready" if m else "ygT_ready"), 8)
                pool.dma_start(prow[:, :, :], io["p_2"][m].rearrange("o (i p) c -> p (o i) c", p=P)) \
                    .then_inc(sem("p_landed"), 16)

        @block.scalar
        def _(act):
            chain = [0]

            def link(ins):
                chain[0] += 1
                ins.then_inc(sem("act_chain"), 1)
                act.wait_ge(sem("act_chain"), chain[0])

            A = act.activation

            split_at = [0]

            def split_to(name, more=0):
                while split_at[0] <= min(index[name] + more, len(units) - 1):
                    n = split_at[0]
                    act.wait_ge(unit_landed[n % LOADS], 16 * (n // LOADS + 1))
                    part_free(act, n)
                    A(part(upper, PARTS, n), part(loaded, LOADS, n), ACT.Copy).then_inc(uppers, 1)
                    split_at[0] += 1

            def upper_of(dst, key, k0, i, n=4):
                ps = full(act, key)
                A(dst[0][:, k0:k0 + n, P * i:P * i + P], ps[:, :].rearrange("p (a b) -> p a b", a=n), ACT.Copy) \
                    .then_inc(sem("operand_uppers"), 1)

            def norm_upper(n):
                for x in ((xT2, xT) if n == 4 else (xT,)):
                    for q in range(2):
                        for i in range(2):
                            xs_count[0] += 1
                            act.wait_ge(sem("xT_scaled"), xs_count[0])
                            A(x[0][:, 4 * q:4 * q + 4, P * i:P * i + P],
                              hs[:, i, 512 * q:512 * q + 512].rearrange("p (a b) -> p a b", a=4), ACT.Copy) \
                                .then_inc(sem("xT_upper_ready"), 1)

            xs_count = [0]

            def norm(n):
                if n == 0:
                    act.wait_ge(sem("x_landed"), 16)
                for i in range(2):
                    if n:
                        act.wait_ge(sem("h_ready"), 2 * n + i - 1)
                    A(hs[:, i, :], h[:, i, :], ACT.Square, accum_out=ssq[:, i:i + 1]).then_inc(sem("sq_done"), 1)
                    act.wait_ge(sem("sq_done"), 2 * n + i + 1)
                    act.wait_ge(sem("eps_set"), 1)
                    A(rstd[:, i:i + 1], ssq[:, i:i + 1], ACT.Sqrt, scale=1.0 / D, bias=eps6).then_inc(sem("root"), 1)

            def post_norm(key, count):
                for i in range(2):
                    for f in range(2):
                        ps = full(act, (key, i, f))
                        A(hs[:, i, 512 * f:512 * f + 512], ps[:, :], ACT.Square,
                          accum_out=ssq[:, 2 * i + f:2 * i + f + 1]).then_inc(sem("post_sq"), 1)
                act.wait_ge(sem("post_sum"), count)
                A(rstd[:, 0:2], ssq[:, 0:2], ACT.Sqrt, scale=1.0 / D, bias=eps6).then_inc(sem("root2"), 1)

            def copy(dst, key, w=512, func=ACT.Copy):
                ps = full(act, key)
                empty(A(dst, ps[:, 0:w], func), key)

            norm(0)
            split_to("rw1")
            norm_upper(0)
            for c in range(14):
                if c % 2 == 1:
                    split_to(f"rw{c // 2}", 2)
                copy(pr[:, c, 1:257], ("rw", c), T)
            act.wait_ge(sem("angles"), 1)
            A(cosd[:, :, 0:32], angn[:, :, :], ACT.Sin).then_inc(sem("trig"), 1)
            A(sind[:, :, 32:64], ang[:, :, :], ACT.Sin).then_inc(sem("trig"), 1)
            split_to("rq.1")
            act.wait_ge(sem("shifted"), 2)
            A(lor[0:64, 0, :], pr[0:64, 12, 1:257], ACT.Tanh).then_inc(sem("lora_in"), 1)
            A(lor[:, 1, :], pr[:, 13, 1:257], ACT.Sigmoid).then_inc(sem("lora_in"), 1)
            split_to("rq.1", 2)
            for i in range(2):
                copy(qr[:, i, :], ("rq", i))
            for p in range(4):
                ps = full(act, ("w", p))
                empty(A(ld[:, p, :], ps[:, 0:T], ACT.Sigmoid, bias=pc("rw_w0", p)), ("w", p))
                ps = full(act, ("a", p))
                empty(A(av[:, p, :], ps[:, 0:T], ACT.Sigmoid, bias=pc("rw_a0", p)), ("a", p))
                copy(gT[:, p, :], ("g", p), T)
            split_to("rk.1", 2)
            for i in range(2):
                copy(kr[:, i, :], ("rk", i))
            act.wait_ge(sem("knorm_in"), 1)
            A(ex[:, :, :], ex3[:, :, :], ACT.Sqrt).then_inc(sem("knorm_root"), 1)
            for i in range(2):
                copy(vrow[:, i, :], ("vT", i))
            split_to("rv0.1", 2)
            for i in range(2):
                copy(vr[:, i, 0:512], ("rv", 0, i))
            act.wait_ge(sem("cum_ready"), 1)
            A(ex3[:, :, :], cc[:, :, :], ACT.Exp).then_inc(sem("e_done"), 1)
            act.wait_ge(sem("prev_ready"), 1)
            A(ex[:, :, :], ld[:, :, :], ACT.Exp).then_inc(sem("e_done"), 1)
            act.wait_ge(sem("rk_ready"), 1)
            for p in range(4):
                full(act, ("bs", p))
            A(ex2[:, :, :], cc[:, :, :], ACT.Exp, scale=-1.0).then_inc(sem("e_done"), 1)
            act.wait_ge(sem("fcol_in"), 1)
            A(fcol[:, :], fcol[:, :], ACT.Exp).then_inc(sem("f_done"), 1)
            split_to("rv1.1", 2)
            for i in range(2):
                copy(vr[:, i, 512:1024], ("rv", 1, i))
            copy(krow[:], ("kbT", 0))
            copy(brow[:], ("kbT", 1))
            for n in range(2):
                for k in range(1, LEVELS):
                    for q in range(2):
                        copy(t1[:, 4 * q:4 * q + 4, :], ("t1", n, k, q))
                copy(rhs[:], ("rhs", n))
                copy(sa[:], ("sa", n))
                copy(yrow[:, n, :], ("y", n))
            split_to("rg0.1", 2)
            act.wait_ge(sem("gn_var"), 1)
            A(rs8[:, :, 0:8], var[:, :, 0:8], ACT.Sqrt).then_inc(sem("gn_root"), 1)
            for i in range(2):
                copy(gr[:, i, 0:512], ("rg", 0, i), func=ACT.Silu)
            for i in range(2):
                ps = full(act, ("qT", i))
                empty(A(qT[:, :, P * i:P * i + P], ps[:, :].rearrange("p (a b) -> p a b", a=4), ACT.Copy), ("qT", i))
                ps = full(act, ("kTr", i))
                empty(A(kTr[:, :, P * i:P * i + P], ps[:, :].rearrange("p (a b) -> p a b", a=4), ACT.Copy), ("kTr", i))
            split_to("rg1.1", 2)
            for i in range(2):
                copy(gr[:, i, 512:1024], ("rg", 1, i), func=ACT.Silu)
            for f in range(4):
                split_to(f"rs{f}.1", 2)
                for i in range(2):
                    copy(sg[:, i, f // 2, 512 * (f % 2):512 * (f % 2) + 512], ("rs", f, i), func=ACT.Sigmoid)
                if f == 2:
                    act.wait_ge(sem("gn_var"), 2)
                    A(rs8[:, :, 0:8], var[:, :, 0:8], ACT.Sqrt).then_inc(sem("gn_root"), 1)
            act.wait_ge(sem("yrw_ready"), 1)
            A(yrwT[0][:, :, :], yrw[:, :, :], ACT.Copy).then_inc(sem("yrwT_upper"), 1)
            for i in range(2):
                for q in range(2):
                    upper_of(oT, ("oT", i, q), 4 * q, i)
            split_to("bret3", 2)
            for i in range(2):
                for q in range(2):
                    upper_of(mT, ("mT", i, q), 4 * q, i)
            split_to("wo3", 1)
            post_norm("wo", 1)
            split_to("wo3", 2)
            norm(1)
            norm_upper(1)
            def act_upper(j):
                for c in range(2):
                    act.wait_ge(sem("act_product"), 2 * j + c + 1)
                    A(actT[0][:, 2 * j + c, :], acc[:, j % 2, c, :], ACT.Copy).then_inc(sem("actT_upper"), 1)

            for j in range(11):
                for c in range(4):
                    if c % 2 == 1:
                        split_to(f"up{j}" + "gv"[c // 2], 2)
                    if c == 2 and j:
                        act_upper(j - 1)
                    ch = 2 * j + c % 2 + 22 * (c // 2)
                    ps = full(act, ("up", j, c))
                    if j >= 2:
                        act.wait_ge(sem("act_ready"), 2 * (j - 1))
                    A(acc[:, j % 2, c, :], ps[:, 0:T], ACT.Identity, bias=fcb(ch), scale=fcw(2, ch)) \
                        .then_inc(sem("tap0"), 1)
                for c in range(2):
                    emptied(act, ("up", j, c))
                    A(acc[:, j % 2, c, :], acc[:, j % 2, c, :], ACT.Gelu_apprx_tanh).then_inc(sem("gelu"), 1)
            act_upper(10)
            split_to("dn10", 1)
            post_norm("dn", 2)
            split_to("dn10", 2)
            norm(2)
            norm_upper(2)
            def z_copy(j):
                for i in range(2):
                    copy(zrow[:, i, 512 * j:512 * j + 512], ("z", j, i))

            for c in range(24):
                if c % 2 == 1:
                    split_to(f"xbc{c // 2}", 2)
                ps = full(act, ("xbc", c))
                if c >= 4:
                    act.wait_ge(sem("xbc_ready"), c - 3)
                A(cacc[:, c % 4, :], ps[:, 0:T], ACT.Identity, bias=scb(c), scale=scw(3, c)).then_inc(sem("stap0"), 1)
                if c >= 1:
                    emptied(act, ("xbc", c - 1))
                    A(xbc[:, c - 1, :], cacc[:, (c - 1) % 4, :], ACT.Silu).then_inc(sem("xbc_ready"), 1)
            emptied(act, ("xbc", 23))
            A(xbc[:, 23, :], cacc[:, 3, :], ACT.Silu).then_inc(sem("xbc_ready"), 1)
            split_to("dt", 2)
            act.wait_ge(sem("dt_in"), 1)
            link(A(adt[:, :, :], adt[:, :, :], ACT.Exp))
            link(A(adt[:, :, :], adt[:, :, :], ACT.Ln, bias=1.0))
            act.wait_ge(sem("rowp_landed"), 96)
            A(arow[:, :], alog, ACT.Exp).then_inc(sem("dt_log"), 1)
            split_to("z0.1", 2)
            z_copy(0)
            for i in range(2):
                for q in range(4):
                    copy(xs[:, i, 512 * q:512 * q + 512], ("xsT", i, q))
            copy(bR[:], ("bR",))
            act.wait_ge(sem("dte_in"), 1)
            A(dte[:, :], tot[:, :], ACT.Exp).then_inc(sem("dte_done"), 1)
            A(eac[:, :], acs[:, 1, :], ACT.Exp).then_inc(sem("dte_done"), 1)
            split_to("z1.1", 2)
            z_copy(1)
            for g in range(4):
                copy(ss0[:, g, :], ("sst", g))
            for u in range(16):
                act.wait_ge(sem("seg_ready"), u + 1)
                A(eT2[:, u % 2, :], eT2[:, u % 2, :], ACT.Exp).then_inc(sem("seg_exp"), 1)
                if u % 4 == 3:
                    m = u // 4
                    split_to(f"z{2 + m // 2}.{m % 2}", 2)
                    if m % 2:
                        z_copy(2 + m // 2)
            for j in range(4):
                emptied(act, ("z", j, 0), ("z", j, 1))
            for i in range(2):
                A(zrow[:, i, :], zrow[:, i, :], ACT.Silu).then_inc(sem("z_silu"), 1)
            for i in range(2):
                for g in range(4):
                    act.wait_ge(sem("yz_ready"), i + 1)
                    A(xd[:, i, 512 * g:512 * g + 512], xs[:, i, 512 * g:512 * g + 512], ACT.Square,
                      accum_out=mean[:, i, g:g + 1]).then_inc(sem("yg_sq"), 1)
            act.wait_ge(sem("yg_sq"), 8)
            A(var[:, :, 0:4], mean[:, :, 0:4], ACT.Sqrt, scale=1.0 / 512, bias=eps6).then_inc(sem("yg_root"), 1)

            for i in range(2):
                for q in range(4):
                    act.wait_ge(sem("yg_scaled"), 4 * i + q + 1)
                    A(ygT[0][:, 4 * q:4 * q + 4, P * i:P * i + P],
                      yg[:, i, q, :].rearrange("p (a b) -> p a b", a=4), ACT.Copy).then_inc(sem("yg_upper"), 1)
            def embedding_upper(m):
                ps = full(act, ("pT", m))
                A(pT[0][:, :, :], ps[:, :].rearrange("p (a b) -> p a b", a=2), ACT.Copy).then_inc(sem("operand_uppers"), 1)

            split_to("so6")
            embedding_upper(0)
            split_to("so7", 2)

            def embed(m):
                n = 3 if m == 0 else 5
                norm(n)
                norm_upper(n)
                for f in range(2):
                    split_to(f"pg{m}{f}.1", 2 - f)
                    for i in range(2):
                        z = 2 * f + i
                        ps = full(act, ("pg", m, f, i))
                        if z >= 2 or m:
                            act.wait_ge(sem("ple_used"), 4 * m + z - 1)
                        empty(A(psg[:, z % 2, :], ps[:, :], ACT.Sigmoid), ("pg", m, f, i))

            embed(0)
            split_to("kv.1")
            norm(4)
            norm_upper(4)
            def head_rows(dst, sq, key, cols_):
                ps = full(act, key)
                A(sq, ps[:, 0:cols_], ACT.Square).then_inc(sem("hn_sq"), 1)
                empty(A(dst, ps[:, :], ACT.Copy), key)

            def head_root(count, m):
                act.wait_ge(sem("hn_in"), count)
                A(rs8[:, :, 0:m], var[:, :, 0:m], ACT.Sqrt).then_inc(sem("hn_root"), 1)

            split_to("kv.1", 1)
            split_to("ain0.1")
            for i in range(2):
                head_rows(kvr[:, i, :], at1[:, i, 512:768], ("kv", i), 256)
            head_root(1, 4)
            split_to("ain1.0")
            split_to("ain1.1")
            for i in range(2):
                head_rows(aq[:, i, 0:512], at1[:, i, 0:512], ("ain", 0, i), 512)
            head_root(2, 8)
            split_to("ain2.0")
            split_to("ain2.1")
            act.wait_ge(sem("ak_rows"), 1)
            for i in range(2):
                head_rows(aq[:, i, 512:1024], at1[:, i, 512:1024], ("ain", 1, i), 512)
            ps = full(act, ("akT",))
            empty(A(akT[:, :, :], ps[:, :].rearrange("p (a b) -> p a b", a=2), ACT.Copy), ("akT",))
            for i in range(2):
                copy(ag[:, i, 0:512], ("ain", 2, i), func=ACT.Silu)
            head_root(3, 8)
            split_to("ain3.0")

            def queries(u):
                for i in range(2):
                    ps = full(act, ("aqT", i, u))
                    empty(A(aqT[:, u, :, P * i:P * i + P], ps[:, :].rearrange("p (a b) -> p a b", a=4), ACT.Copy),
                          ("aqT", i, u))

            queries(0)
            for z in range(len(UNITS)):
                act.wait_ge(sem("sub_ready"), z + 1)
                w = 512 // HEADS[z]
                for e in range(HEADS[z]):
                    s = asb[:, z % 2, w * e:w * e + w]
                    A(s, s, ACT.Exp, bias=mx[:, z % 2, e:e + 1], accum_out=den[:, z, e:e + 1]) \
                        .then_inc(sem("exps"), 1)
                A(dsk[:, z % 2, 0:HEADS[z]], dsk[:, z % 2, 0:HEADS[z]], ACT.Exp).then_inc(sem("sink_exp"), 1)
                if z == 0:
                    split_to("ain3.1")
                copy(aeT[:, z % 2, :], ("eT", z))
                if z == 2:
                    for i in range(2):
                        copy(ag[:, i, 512:1024], ("ain", 3, i), func=ACT.Silu)
                    queries(1)
                if z == 4:
                    upper_of(aoT, ("aoT", 0, 0), 0, 0)
                if z == 8:
                    upper_of(aoT, ("aoT", 1, 0), 0, 1)
                    split_to("ao1")
                if z == 10:
                    upper_of(aoT, ("aoT", 0, 1), 4, 0)
            upper_of(aoT, ("aoT", 1, 1), 4, 1)
            split_to("ao2")
            embedding_upper(1)
            split_to("ao3", 2)
            embed(1)

        @block.vector
        def _(ve):
            chain = [0]

            def link(ins):
                chain[0] += 1
                ins.then_inc(sem("ve_chain"), 1)
                ve.wait_ge(sem("ve_chain"), chain[0])

            TT, TS, STT = ve.tensor_tensor, ve.tensor_scalar, ve.scalar_tensor_tensor
            mul, add, sub, mx_ = ALU.mult, ALU.add, ALU.subtract, ALU.max

            def bc(a, *shape):
                return a.broadcast_to(list(shape))

            def four(ps, a=4):
                return ps[:, :].rearrange("p (a b) -> p a b", a=a)

            split_at, xl, lowered = [0], [0], [0]

            def split_to(name, more=0):
                while split_at[0] <= min(index[name] + more, len(units) - 1):
                    n = split_at[0]
                    ve.wait_ge(uppers, n + 1)
                    TT(part(lower, PARTS, n), part(loaded, LOADS, n), part(upper, PARTS, n).bitcast(F32), sub) \
                        .then_inc(lowers, 1)
                    split_at[0] += 1

            def lower_of(dst, key, k0, i, n=4):
                lowered[0] += 1
                ve.wait_ge(sem("operand_uppers"), lowered[0])
                ps = full(ve, key)
                c = (slice(None), slice(k0, k0 + n), slice(P * i, P * i + P))
                empty(TT(dst[1][c], four(ps, n), dst[0][c].bitcast(F32), sub), key)

            link(ve.memset(eps6, 1e-6))
            ve.memset(pr[:, :, 0:1], 0.0).then_inc(sem("eps_set"), 1)

            def norm(n, name, r0=0):
                for i in range(2):
                    ve.wait_ge(sem("root"), 2 * n + i + 1)
                    link(ve.reciprocal(rstd[:, i:i + 1], rstd[:, i:i + 1]))
                    TS(hs[:, i, :], h[:, i, :], rstd[:, i:i + 1], None, mul).then_inc(sem("rows_scaled"), 1)
                if n == 0:
                    for g, parts in enumerate(STAGES):
                        m = sum(p[2] for p in parts)
                        ps = full(ve, ("cols", g))
                        at = [0, 114, 202, 290][g]
                        empty(ve.tensor_copy(cols[:, at:at + m], ps[:, 0:m]), ("cols", g))
                    emptied(ve, *[("cols", g) for g in range(4)])
                    split_to("rw1")
                for x, w in (((xT2, "kv_norm_w_2"), (xT, name)) if n == 4 else ((xT, name),)):
                    def scale(p):
                        q, i = divmod(p, 2)
                        ps = full(ve, ("nT", n, i, q))
                        g = cols[:, colat[(w, r0)] + 4 * q:colat[(w, r0)] + 4 * q + 4]
                        if x is xT and n == 4:
                            ve.wait_ge(sem("xT2_lower_ready"), p + 1)
                        TT(four(hs[:, i, 512 * q:512 * q + 512]), four(ps), bc(g.unsqueeze(2), P, 4, P), mul) \
                            .then_inc(sem("xT_scaled"), 1)

                    def lower_piece(p):
                        q, i = divmod(p, 2)
                        xl[0] += 1
                        ve.wait_ge(sem("xT_upper_ready"), xl[0])
                        c = (slice(None), slice(4 * q, 4 * q + 4), slice(P * i, P * i + P))
                        TT(x[1][c], four(hs[:, i, 512 * q:512 * q + 512]), x[0][c].bitcast(F32), sub) \
                            .then_inc(sem("xT2_lower_ready" if x is xT2 else "xT_lower_ready"), 1)

                    scale(0)
                    scale(1)
                    for p in range(4):
                        lower_piece(p)
                        if p < 2:
                            scale(p + 2)
                for i in range(2):
                    for q in range(2):
                        empty(ve.nop(), ("nT", n, i, q))

            def post_norm(key, n):
                ve.wait_ge(sem("post_sq"), 4 * n)
                v = ssq[:, :].rearrange("p (a b) -> p a b", a=2)
                link(TT(rstd[:, 2:4], v[:, :, 0], v[:, :, 1], add))
                ve.tensor_copy(ssq[:, 0:2], rstd[:, 2:4]).then_inc(sem("post_sum"), 1)
                ve.wait_ge(sem("root2"), n)
                link(ve.reciprocal(rstd[:, 0:2], rstd[:, 0:2]))
                ve.wait_ge(sem("postw_landed"), 16 * n)
                ve.wait_ge(sem("x_again"), 16)
                for i in range(2):
                    for f in range(2):
                        c = slice(512 * f, 512 * f + 512)
                        ps = full(ve, (key, i, f))
                        empty(STT(out=tmph[:, i, c], in0=ps[:, :], scalar=rstd[:, i:i + 1], in1=postw[:, c],
                                  op0=mul, op1=mul), (key, i, f))
                    emptied(ve, (key, i, 0), (key, i, 1))
                    TT(h[:, i, :], h[:, i, :], tmph[:, i, :], add).then_inc(sem("h_ready"), 1)

            norm(0, "norm_mix_pre")
            for j in range(7):
                split_to(f"rw{j}", 2)
            ve.wait_ge(sem("pos_landed"), 32)
            link(ve.tensor_copy(posf[:, :], posi[:, :]))
            link(TT(ang[:, :, :], bc(posf[:, :].unsqueeze(2), P, 4, 32), bc(const("inv").unsqueeze(1), P, 4, 32), mul))
            magic = 1.5 * 2.0 ** 23
            link(TS(angn[:, :, :], ang[:, :, :], 1.0 / (2 * np.pi), magic, mul, add))
            link(TS(angn[:, :, :], angn[:, :, :], magic, None, sub))
            two_pi = 2 * np.pi
            c1 = float(np.float32(6.28125))
            c2 = float((two_pi - c1) // 2.0 ** -19 * 2.0 ** -19)
            for piece in (c1, c2, two_pi - c1 - c2):
                link(STT(out=ang[:, :, :], in0=angn[:, :, :], scalar=-piece, in1=ang[:, :, :], op0=mul, op1=add))
            link(TS(ang[:, :, :], ang[:, :, :], 3.1415925, -3.1415925, ALU.min, mx_))
            link(TS(angn[:, :, :], ang[:, :, :], float(np.pi / 2), None, add))
            link(TS(cosd[:, :, 32:64], angn[:, :, :], float(np.pi), -two_pi, ALU.is_gt, mul))
            link(TT(angn[:, :, :], angn[:, :, :], cosd[:, :, 32:64], add))
            TS(angn[:, :, :], angn[:, :, :], 3.1415925, -3.1415925, ALU.min, mx_).then_inc(sem("angles"), 1)
            ve.wait_ge(sem("trig"), 2)
            link(ve.tensor_copy(cosd[:, :, 32:64], cosd[:, :, 0:32]))
            link(TS(sind[:, :, 0:32], sind[:, :, 32:64], -1.0, None, mul))
            for c in range(14):
                emptied(ve, ("rw", c))
            link(TT(dif[:, :, :], pr[:, :, 0:256], pr[:, :, 1:257], sub))
            for c in (12, 13, *range(12)):
                STT(out=pr[:, c, 1:257], in0=dif[:, c, :], scalar=pc("rw_mu", c), in1=pr[:, c, 1:257],
                    op0=mul, op1=add).then_inc(sem("shifted"), 1)
            ve.wait_ge(sem("shifted"), 14)
            split_to("rq.1", 2)
            r_, k_, v_ = pr[:, 0:4, 1:257], pr[:, 4:8, 1:257], pr[:, 8:12, 1:257]
            for p in range(4):
                ins = TS(kn[:, p, :], k_[:, p, :], pc("rw_k_k", p), None, mul)
            link(ins)
            TT(ex[:, :, :], kn[:, :, :], kn[:, :, :], mul).then_inc(sem("kk_squared"), 1)
            split_to("rk.1", 2)
            for p in range(4):
                ps = full(ve, ("ss", p))
                empty(TS(ex3[:, p, :], ps[:, 0:T], 1e-24, None, mx_), ("ss", p))
            for p in range(4):
                emptied(ve, ("ss", p))
            ve.nop().then_inc(sem("knorm_in"), 1)
            split_to("rv0.0", 2)
            link(TS(om[:, :], pcs("rw_k_a", 4), -1.0, 1.0, mul, add))
            for p in range(4):
                emptied(ve, ("a", p), ("w", p))
            for p in range(4):
                TS(cc[:, p, :], av[:, p, :], pc("rw_k_a", p), om[:, p:p + 1], mul, add).then_inc(sem("ka"), 1)
            ve.wait_ge(sem("ka"), 4)
            link(TT(k_, k_, cc[:, :, :], mul))
            for p in range(4):
                ins = STT(out=ex2[:, p, :], in0=r_[:, p, :], scalar=pc("rw_r_k", p), in1=k_[:, p, :], op0=mul, op1=mul)
                ins.then_inc(sem("rk1"), 1)
            ve.wait_ge(sem("rk1"), 4)
            ve.nop().then_inc(sem("rk_ready"), 1)
            split_to("rv0.1", 2)
            ve.wait_ge(sem("knorm_root"), 1)
            link(ve.reciprocal(ex[:, :, :], ex[:, :, :]))
            link(TT(kn[:, :, :], kn[:, :, :], ex[:, :, :], mul))
            link(TS(ld[:, :, :], ld[:, :, :], -float(np.exp(-0.5)), None, mul))
            for p in range(4):
                for n in range(2):
                    c = slice(P * n, P * n + P)
                    ins = ve.tensor_tensor_scan(cc[:, p, c], bc(const("ones")[:, 0:1], P, P), ld[:, p, c], 0.0, mul, add)
                    ins.then_inc(sem("scan"), 1)
            ve.wait_ge(sem("scan"), 8)
            link(ve.tensor_copy(fcol[:, :], cc[:, :, 191]))
            c4 = cc[:, :, :].rearrange("p a (n t) -> p (a n) t", n=2)
            link(ve.tensor_copy(mid, c4[:, :, 63]))
            link(TT(c4, c4, bc(mid.unsqueeze(2), P, 8, P), sub))
            link(TT(ld[:, :, :], cc[:, :, :], ld[:, :, :], sub))
            ve.nop().then_inc(sem("cum_ready"), 1)
            ve.nop().then_inc(sem("prev_ready"), 1)
            TT(fcol[:, :], fcol[:, :], cc[:, :, 127], add).then_inc(sem("fcol_in"), 1)
            emptied(ve, ("vT", 0), ("vT", 1))
            for p in range(4):
                ps = full(ve, ("bs", p))
                empty(TT(v_[:, p, :], v_[:, p, :], ps[:, 0:T], mul), ("bs", p))
            split_to("rv1.0", 2)
            z_ = zr[:, :, :, 0:P]
            rr = zr[:, :, :, P:256]
            s4 = lambda a: a.rearrange("p a (n t) -> p a n t", n=2)
            ve.wait_ge(sem("e_done"), 3)
            link(TT(rr, s4(r_), s4(ex3[:, :, :]), mul))
            link(TT(ld[:, :, :], kn[:, :, :], ex[:, :, :], mul))
            link(TS(z_, s4(ld[:, :, :]), -1.0, None, mul))
            link(TT(kn[:, :, :], kn[:, :, :], av[:, :, :], mul))
            link(TT(bt[:, :, :, :], s4(kn[:, :, :]), s4(ex2[:, :, :]), mul))
            TT(kt[:, :, :, :], s4(k_), s4(ex2[:, :, :]), mul).then_inc(sem("decayed"), 1)
            split_to("rv1.1", 2)
            strict, incl = const("strict"), const("incl")
            h8 = lambda a, n=8: a[:, :, :].rearrange("p i (a b) -> p i a b", a=n)

            def rope_tile(x, n, tab, t1_, t2_, dst):
                c = bc(cosd[:, tab, :].unsqueeze(1), P, n, 64)
                s1 = bc(sind[:, tab, 0:32].unsqueeze(1), P, n, 32)
                s2 = bc(sind[:, tab, 32:64].unsqueeze(1), P, n, 32)
                TT(t1_, x, c, mul)
                TT(t2_[:, :, 0:32], x[:, :, 32:64], s1, mul)
                link(TT(t2_[:, :, 32:64], x[:, :, 0:32], s2, mul))
                link(TT(dst, t1_, t2_, add))

            def rope_piece(z):
                x, g = ((qr, "gq"), (kr, "gk"))[z // 2]
                i = z % 2
                emptied(ve, ("rq", i), ("rk", i))
                t = [ro[:, m, :].rearrange("p (a b) -> p a b", a=8) for m in range(2)]
                v = h8(x)[:, i, :, :]
                rope_tile(v, 8, i, t[0], t[1], v)
                ins = TT(v, v, bc(const(g).unsqueeze(2), P, 8, 64), mul)
                if z % 2:
                    ins.then_inc(sem("qk_rope"), 1)
                else:
                    link(ins)

            for n in range(2):
                if n == 0:
                    ve.wait_ge(sem("decayed"), 1)
                for hd in range(8):
                    ps = full(ve, ("m", n, hd))
                    if n:
                        if hd == 0:
                            full(ve, ("y", 0))
                    v = ps[:, :].rearrange("p (a b c) -> p a b c", a=2, b=2)
                    m = mats[:, hd, :, :].rearrange("p (a b) c -> p a b c", a=2)
                    link(TT(m[:, :, 0, :], v[:, :, 0, :], bc(strict.unsqueeze(1), P, 2, P), mul))
                    empty(TT(m[:, :, 1, :], v[:, :, 1, :], bc(incl.unsqueeze(1), P, 2, P), mul), ("m", n, hd))
                emptied(ve, *[("m", n, hd) for hd in range(8)])
                ve.nop().then_inc(sem("mats_ready"), 8)
                iv = inv.rearrange("p (a o) c -> p a o c", o=2)
                for o in range(2):
                    ps = full(ve, ("L", n, o))
                    empty(TT(iv[:, :, o, :], four(ps), bc(const("off0L").unsqueeze(1), P, 4, P), mul), ("L", n, o))
                emptied(ve, ("L", n, 0), ("L", n, 1))
                link(TT(inv[:, :, :], inv[:, :, :], bc(ident.unsqueeze(1), P, 8, P), add))
                link(TT(invT[:, :, :], mats[:, :, 0, :], bc(const("off0").unsqueeze(1), P, 8, P), mul))
                TT(invT[:, :, :], invT[:, :, :], bc(ident.unsqueeze(1), P, 8, P), add).then_inc(sem("inv_start"), 1)
                ve.wait_ge(sem("inv_start"), n + 1)
                for k in range(1, LEVELS):
                    for q in range(2):
                        for key, dst in ((("x", n, k, q), inv), (("xt", n, k, q), invT)):
                            ps = full(ve, ("xt", n, k, q))
                            ps = full(ve, key)
                            d = dst[:, 4 * q:4 * q + 4, :]
                            empty(TT(d, d, four(ps), add), key)
                        emptied(ve, ("x", n, k, q), ("xt", n, k, q))
                    if n == 0 and k < 5:
                        rope_piece(k - 1)
                if n == 0:
                    ps = full(ve, ("st",))
                    empty(TT(s0[:, :, :], four(ps), bc(const("blk").unsqueeze(1), P, 4, P), mul), ("st",))
                    emptied(ve, ("st",))
                    ve.wait_ge(sem("f_done"), 1)
                    for p in range(4):
                        ins = TS(s0[:, p, :], s0[:, p, :], fcol[:, p:p + 1], None, mul)
                        ins.then_inc(sem("s0c"), 1)
                    ve.wait_ge(sem("s0c"), 4)
                    ve.nop().then_inc(sem("state_ready"), 1)

            pumps = []

            def pump():
                if pumps:
                    split_to(pumps.pop(0), 2)

            def centre(rows_, n, w, eps, sqbuf, count):
                x = rows_[:, :, 0:n * w].rearrange("p i (a b) -> p i a b", a=n)
                sq = sqbuf[:, :, 0:n * w].rearrange("p i (a b) -> p i a b", a=n)
                for i in range(2):
                    ins = ve.tensor_reduce(mean[:, i, 0:n], x[:, i, :, :], AX.X, add)
                link(ins)
                link(TS(mean[:, :, 0:n], mean[:, :, 0:n], 1.0 / w, None, mul))
                pump()
                for i in range(2):
                    link(TT(x[:, i, :, :], x[:, i, :, :], bc(mean[:, i, 0:n].unsqueeze(2), P, n, w), sub))
                pump()
                for i in range(2):
                    link(TT(sq[:, i, :, :], x[:, i, :, :], x[:, i, :, :], mul))
                pump()
                for i in range(2):
                    link(ve.tensor_reduce(var[:, i, 0:n], sq[:, i, :, :], AX.X, add))
                TS(var[:, :, 0:n], var[:, :, 0:n], 1.0 / w, eps, mul, add).then_inc(sem("gn_var"), 1)
                ve.wait_ge(sem("gn_root"), count)
                link(ve.reciprocal(rs8[:, :, 0:n], rs8[:, :, 0:n]))
                return x

            emptied(ve, ("y", 0), ("y", 1))
            pumps += ["rg0.0", "rg0.1"]
            x = centre(yrow, 8, 64, 64e-5, ar(6672, 2, 512), 1)
            for i in range(2):
                ins = TT(x[:, i, :, :], x[:, i, :, :], bc(rs8[:, i, 0:8].unsqueeze(2), P, 8, 64), mul)
                ins.then_inc(sem("yn"), 1)
            ve.wait_ge(sem("yn"), 2)
            ve.nop().then_inc(sem("y_rows"), 1)
            for i in range(2):
                ps = full(ve, ("yT", i))
                if i == 0:
                    split_to("rg1.0", 2)
                for p in range(4):
                    ins = TS(yrw[:, p, P * i:P * i + P], ps[:, P * p:P * p + P], pc("rw_lnx_w", p), pc("rw_lnx_b", p),
                             mul, add)
                empty(ins, ("yT", i))
            emptied(ve, ("yT", 0), ("yT", 1))
            link(TT(yrw[:, :, :], yrw[:, :, :], v_, add))
            TT(yrw[:, :, :], yrw[:, :, :], gT[:, :, :], mul).then_inc(sem("yrw_ready"), 1)
            split_to("rg1.1", 2)

            def rope_products(x, n, tab, t1_, t2_):
                for i in range(2):
                    c = bc(cosd[:, tab + i, :].unsqueeze(1), P, n, 64)
                    s1 = bc(sind[:, tab + i, 0:32].unsqueeze(1), P, n, 32)
                    s2 = bc(sind[:, tab + i, 32:64].unsqueeze(1), P, n, 32)
                    TT(t1_[:, i, :, :], x[:, i, :, :], c, mul)
                    TT(t2_[:, i, :, 0:32], x[:, i, :, 32:64], s1, mul)
                    link(TT(t2_[:, i, :, 32:64], x[:, i, :, 0:32], s2, mul))

            def rope(x, n, tab, t1_, t2_, dst):
                rope_products(x, n, tab, t1_, t2_)
                for i in range(2):
                    link(TT(dst[:, i, :, :], t1_[:, i, :, :], t2_[:, i, :, :], add))

            for g in range(2):
                ps = full(ve, ("R", g))
                empty(TT(rst[:, 2 * g:2 * g + 2, :], four(ps, 2), bc(const("blkret").unsqueeze(1), P, 2, 256), mul),
                      ("R", g))
            for n in range(2):
                if n:
                    split_to("rs1.0", 2)
                for o in range(2):
                    ps = full(ve, ("s", n, o))
                    if n:
                        full(ve, ("o", 0, 0))
                        full(ve, ("o", 0, 1))
                    for p in range(4):
                        hd = 2 * p + o
                        ins = STT(out=sT[:, hd, :], in0=ps[:, P * p:P * p + P], scalar=float(GAMMA[hd] ** -128.0),
                                  in1=incl, op0=mul, op1=mul)
                    empty(ins, ("s", n, o))
                split_to("rs0.1" if n == 0 else "rs1.1", 2)
                for g in range(2):
                    ps = full(ve, ("o", n, g))
                    empty(ve.tensor_copy(orow[:, n, 512 * g:512 * g + 512], ps[:, :]), ("o", n, g))
            emptied(ve, ("o", 1, 0), ("o", 1, 1), ("o", 0, 0), ("o", 0, 1))
            split_to("rs2.0", 2)
            pumps += ["rs2.1"]
            x = centre(orow, 8, P, 1e-5, ar(2048, 2, D), 2)
            for i in range(2):
                link(TT(x[:, i, :, :], x[:, i, :, :], bc(rs8[:, i, 0:8].unsqueeze(2), P, 8, P), mul))
            for f in range(2):
                for i in range(2):
                    emptied(ve, ("rg", f, i))
            TT(orow[:, :, :], orow[:, :, :], gr[:, :, :], mul).then_inc(sem("o_rows"), 1)
            for f in range(4):
                for i in range(2):
                    emptied(ve, ("rs", f, i))
            ve.wait_ge(sem("yrwT_upper"), 1)
            TT(yrwT[1][:, :, :], yrw[:, :, :], yrwT[0][:, :, :].bitcast(F32), sub).then_inc(sem("yrwT_ready"), 1)
            for i in range(2):
                for q in range(2):
                    lower_of(oT, ("oT", i, q), 4 * q, i)
            split_to("bret3", 2)
            for i in range(2):
                for f in range(2):
                    c = slice(512 * f, 512 * f + 512)
                    ps = full(ve, ("brw", i, f))
                    empty(TT(mrow[:, i, c], ps[:, :], sg[:, i, 0, c], mul), ("brw", i, f))
            emptied(ve, *[("brw", i, f) for i in range(2) for f in range(2)])
            for i in range(2):
                for f in range(2):
                    c = slice(512 * f, 512 * f + 512)
                    ps = full(ve, ("bret", i, f))
                    empty(TT(mtmp, ps[:, :], sg[:, i, 1, c], mul), ("bret", i, f))
                    emptied(ve, ("bret", i, f))
                    link(TT(mrow[:, i, c], mrow[:, i, c], mtmp, add))
            ve.nop().then_inc(sem("merged"), 1)
            for i in range(2):
                for q in range(2):
                    lower_of(mT, ("mT", i, q), 4 * q, i)
            split_to("wo3", 1)
            post_norm("wo", 1)
            split_to("wo3", 2)
            norm(1, "norm_ffn_pre")
            def act_lower(j):
                for c in range(2):
                    ve.wait_ge(sem("actT_upper"), 2 * j + c + 1)
                    TT(actT[1][:, 2 * j + c, :], acc[:, j % 2, c, :], actT[0][:, 2 * j + c, :].bitcast(F32), sub) \
                        .then_inc(sem("act_ready"), 1)

            for j in range(11):
                b = j % 2
                for c in range(4):
                    if c % 2 == 1:
                        split_to(f"up{j}" + "gv"[c // 2], 2)
                    if c == 3 and j:
                        act_lower(j - 1)
                    ch = 2 * j + c % 2 + 22 * (c // 2)
                    ps = full(ve, ("up", j, c))
                    ve.wait_ge(sem("tap0"), 4 * j + c + 1)
                    for tap in (1, 0):
                        sft = 2 - tap
                        a = acc[:, b, c, sft:T]
                        ins = STT(out=a, in0=ps[:, 0:T - sft], scalar=fcw(tap, ch), in1=a, op0=mul, op1=add)
                        if tap:
                            link(ins)
                    empty(ins, ("up", j, c))
                for c in range(2):
                    ve.wait_ge(sem("gelu"), 2 * j + c + 1)
                    emptied(ve, ("up", j, c + 2))
                    TT(acc[:, b, c, :], acc[:, b, c, :], acc[:, b, 2 + c, :], mul).then_inc(sem("act_product"), 1)
            act_lower(10)
            split_to("dn10", 1)
            post_norm("dn", 2)
            split_to("dn10", 2)
            norm(2, "ssm_norm_w_2")
            for c in range(24):
                if c % 2 == 1:
                    split_to(f"xbc{c // 2}", 2)
                ps = full(ve, ("xbc", c))
                ve.wait_ge(sem("stap0"), c + 1)
                for sft in (1, 2, 3):
                    a = cacc[:, c % 4, sft:T]
                    ins = STT(out=a, in0=ps[:, 0:T - sft], scalar=scw(3 - sft, c), in1=a, op0=mul, op1=add)
                    if sft < 3:
                        link(ins)
                empty(ins, ("xbc", c))
            split_to("dt", 2)
            ps = full(ve, ("dt",))
            ve.wait_ge(sem("rowp_landed"), 96)
            d2 = ps[:, 0:64].rearrange("p (a b) -> p a b", a=2)
            empty(TT(dtv[:, :, :], d2, bc(dtb.unsqueeze(1), P, 2, 32), add), ("dt",))
            emptied(ve, ("dt",))
            link(TS(acs[:, :, :], dtv[:, :, :], -1.0, None, mul))
            TT(adt[:, :, :], dtv[:, :, :], acs[:, :, :], ALU.min).then_inc(sem("dt_in"), 1)
            link(TS(dtv[:, :, :], dtv[:, :, :], 0.0, None, mx_))
            ve.wait_ge(sem("dt_log"), 1)
            link(TT(dtv[:, :, :], dtv[:, :, :], adt[:, :, :], add))
            link(TS(arow, arow, -1.0, None, mul))
            TT(adt[:, :, :], dtv[:, :, :], bc(arow.unsqueeze(1), P, 2, 32), mul).then_inc(sem("adt_ready"), 1)
            split_to("z0.1", 2)
            ps = full(ve, ("ac",))
            link(ve.tensor_copy(acs[:, :, :], ps[:, 0:64].rearrange("p (a b) -> p a b", a=2)))
            empty(TT(tot, ps[:, 64:96], acs[:, 0, :], sub), ("ac",))
            emptied(ve, ("ac",))
            ve.nop().then_inc(sem("dte_in"), 1)
            hv = lambda a: a.rearrange("p (a b) -> p a b", a=32)
            for i in range(2):
                emptied(ve, *[("xsT", i, q) for q in range(4)])
                TT(hv(xd[:, i, :]), hv(xs[:, i, :]), bc(dtv[:, i, :].unsqueeze(2), P, 32, 64), mul) \
                    .then_inc(sem("xd_ready"), 1)
                if i == 0:
                    ve.wait_ge(sem("dte_done"), 2)
                    ve.wait_ge(sem("xd_ready"), 1)
                    TT(hv(xdd[:]), hv(xd[:, 0, :]), bc(dte.unsqueeze(2), P, 32, 64), mul).then_inc(sem("xd_ready"), 1)
            for i in range(2):
                link(TT(hv(xs[:, i, :]), hv(xs[:, i, :]), bc(dsk_.unsqueeze(2), P, 32, 64), mul))
            split_to("z1.1", 2)
            for n in range(2):
                ps = full(ve, ("cb", n))
                empty(TT(cbm[:, n, :].rearrange("p (a b) -> p a b", a=4), four(ps), bc(incl.unsqueeze(1), P, 4, P), mul),
                      ("cb", n))
            emptied(ve, ("cb", 0), ("cb", 1))

            def segs(z):
                n, u = divmod(z, 8)
                ps = full(ve, ("bc", n, u))
                if z >= 2:
                    ve.wait_ge(sem("wT_ready"), z - 1)
                for e in range(4):
                    hd = 4 * u + e
                    ins = TS(eT2[:, z % 2, P * e:P * e + P], ps[:, P * e:P * e + P], acs[:, n, hd:hd + 1], 0.0, sub, ALU.min)
                empty(ins, ("bc", n, u))
                emptied(ve, ("bc", n, u))
                ve.nop().then_inc(sem("seg_ready"), 1)

            def weigh(z):
                n, u = divmod(z, 8)
                g = u // 2
                ve.wait_ge(sem("seg_exp"), z + 1)
                if z >= 4:
                    zz = (z // 2) - 2
                    full(ve, ("yd", zz // 4, zz % 4))
                TT(wT[:, g % 2, 4 * (u % 2):4 * (u % 2) + 4, :], eT2[:, z % 2, :].rearrange("p (a b) -> p a b", a=4),
                   bc(cbm[:, n, P * g:P * g + P].unsqueeze(1), P, 4, P), mul).then_inc(sem("wT_ready"), 1)

            def join(z):
                n, g = divmod(z, 4)
                c = slice(512 * g, 512 * g + 512)
                ps = full(ve, ("yd", n, g))
                empty(TT(xs[:, n, c], xs[:, n, c], ps[:, :], add), ("yd", n, g))
                if n:
                    ps = full(ve, ("yo", g))
                    e8 = lambda a: a.rearrange("p (a b) -> p a b", a=8)
                    empty(TT(e8(xdd[:, c]), e8(ps[:, :]), bc(eac[:, 8 * g:8 * g + 8].unsqueeze(2), P, 8, 64), mul),
                          ("yo", g))
                    emptied(ve, ("yo", g), ("yd", n, g))
                    link(TT(xs[:, n, c], xs[:, n, c], xdd[:, c], add))

            for g in range(4):
                full(ve, ("sst", g))
            segs(0)
            for z in range(16):
                if z + 1 < 16:
                    segs(z + 1)
                weigh(z)
                if z % 4 == 3:
                    m = z // 4
                    split_to(f"z{2 + m // 2}.{m % 2}", 2)
                if z % 2 == 1 and z >= 3:
                    join(z // 2 - 1)
            join(7)
            emptied(ve, *[("yd", n, g) for n in range(2) for g in range(4)])
            for i in range(2):
                ve.wait_ge(sem("z_silu"), i + 1)
                TT(xs[:, i, :], xs[:, i, :], zrow[:, i, :], mul).then_inc(sem("yz_ready"), 1)
            ve.wait_ge(sem("yg_root"), 1)
            link(ve.reciprocal(var[:, :, 0:4], var[:, :, 0:4]))
            for i in range(2):
                v = xs[:, i, :].rearrange("p (a b) -> p a b", a=4)
                TT(v, v, bc(var[:, i, 0:4].unsqueeze(2), P, 4, 512), mul).then_inc(sem("yg_rows"), 1)
            for i in range(2):
                for q in range(4):
                    ps = full(ve, ("gT", i, q))
                    a = colat[("ssm_gnorm_w_2", 0)] + 4 * q
                    empty(TT(four(yg[:, i, q, :]), four(ps), bc(cols[:, a:a + 4].unsqueeze(2), P, 4, P), mul), ("gT", i, q))
                    emptied(ve, ("gT", i, q))
                    ve.nop().then_inc(sem("yg_scaled"), 1)
            for i in range(2):
                for q in range(4):
                    ve.wait_ge(sem("yg_upper"), 4 * i + q + 1)
                    c = (slice(None), slice(4 * q, 4 * q + 4), slice(P * i, P * i + P))
                    TT(ygT[1][c], four(yg[:, i, q, :]), ygT[0][c].bitcast(F32), sub).then_inc(sem("ygT_ready"), 1)
            def embedding_lower(m):
                lowered[0] += 1
                ve.wait_ge(sem("operand_uppers"), lowered[0])
                ps = full(ve, ("pT", m))
                empty(TT(pT[1][:, :, :], four(ps, 2), pT[0][:, :, :].bitcast(F32), sub), ("pT", m))

            split_to("so6")
            embedding_lower(0)
            split_to("so7", 1)

            def plain_join(key):
                for i in range(2):
                    for f in range(2):
                        c = slice(512 * f, 512 * f + 512)
                        ps = full(ve, (key, i, f))
                        empty(TT(h[:, i, c], h[:, i, c], ps[:, :], add), (key, i, f))
                    emptied(ve, (key, i, 0), (key, i, 1))
                    ve.nop().then_inc(sem("h_ready"), 1)

            def embed(m):
                n = 3 if m == 0 else 5
                split_to(f"pg{m}0.0")
                norm(n, "ple_norm_w_2", 8 * m)
                for f in range(2):
                    split_to(f"pg{m}{f}.1", 2 - f)
                    for i in range(2):
                        z = 2 * f + i
                        c = slice(512 * f, 512 * f + 512)
                        emptied(ve, ("pg", m, f, i))
                        ps = full(ve, ("pp", m, f, i))
                        empty(TT(tmph[:, i, c], psg[:, z % 2, :], ps[:, :], mul), ("pp", m, f, i))
                        emptied(ve, ("pp", m, f, i))
                        ve.nop().then_inc(sem("ple_used"), 1)
                        TT(h[:, i, c], h[:, i, c], tmph[:, i, c], add).then_inc(sem("out_ready") if m else sem("ple_joined"), 1)
                        if m == 0 and f:
                            ve.wait_ge(sem("ple_joined"), z + 1)
                            ve.nop().then_inc(sem("h_ready"), 1)

            plain_join("so")
            embed(0)
            split_to("kv.1")
            norm(4, "attn_norm_w_2")

            def norm_sums(n, sq, count, scale):
                ve.wait_ge(sem("hn_sq"), 2 * count)
                for i in range(2):
                    link(ve.tensor_reduce(var[:, i, 0:n], sq[:, i, :, :], AX.X, add))
                TS(var[:, :, 0:n], var[:, :, 0:n], scale / 64, scale * 1e-6, mul, add).then_inc(sem("hn_in"), 1)

            def norm_apply(x, n, w, count):
                ve.wait_ge(sem("hn_root"), count)
                link(ve.reciprocal(rs8[:, :, 0:n], rs8[:, :, 0:n]))
                for i in range(2):
                    link(TT(x[:, i, :, :], x[:, i, :, :], bc(rs8[:, i, 0:n].unsqueeze(2), P, n, 64), mul))
                for i in range(2):
                    link(TT(x[:, i, :, :], x[:, i, :, :], bc(w.unsqueeze(1), P, n, 64), mul))

            def heads(a, c0, n):
                return a[:, :, c0:c0 + 64 * n].rearrange("p i (a b) -> p i a b", a=n)

            def query_rope(u):
                x, t1_, t2_ = heads(aq, 512 * u, 8), heads(at1, 512 * u, 8), heads(at2, 512 * u, 8)
                rope_products(x, 8, 2, t1_, t2_)
                for i in range(2):
                    src = [a[:, i, 512 * u:512 * u + 512].rearrange("p (o g d) -> p o g d", o=2, g=4) for a in (at1, at2)]
                    dst = aqr[:, i, 512 * u:512 * u + 512].rearrange("p (g o d) -> p o g d", g=4, o=2)
                    for o in range(2):
                        ins = TT(dst[:, o, :, :], src[0][:, o, :, :], src[1][:, o, :, :], add)
                ins.then_inc(sem("aq_rows"), 1)

            split_to("kv.1", 1)
            split_to("ain0.1")
            link(TS(nsinks, sinks, -1.0, None, mul))
            kx = heads(kvr, 0, 4)
            norm_sums(4, heads(at1, 512, 4), 1, 1.0)
            split_to("ain1.0")
            emptied(ve, ("kv", 0), ("kv", 1))
            norm_apply(kx, 4, kn_, 1)
            rope(kx, 4, 2, heads(at1, 512, 4), heads(at2, 512, 4), heads(akr, 0, 4))
            ve.nop().then_inc(sem("ak_rows"), 1)
            split_to("ain1.1")
            norm_sums(8, heads(at1, 0, 8), 2, 64.0)
            split_to("ain2.0")
            emptied(ve, *[("ain", 0, i) for i in range(2)])
            norm_apply(heads(aq, 0, 8), 8, qn, 2)
            split_to("ain2.1")
            query_rope(0)
            norm_sums(8, heads(at1, 512, 8), 3, 64.0)
            split_to("ain3.0")

            def softmax_in(z):
                n, u, o, gh = UNITS[z]
                nh, w = (4, P) if n == 0 else (2, 2 * P)
                hd = 8 * u + 4 * o + 2 * gh
                ps = full(ve, ("as", z))
                if z >= 2:
                    full(ve, ("eT", z - 2))
                s = asb[:, z % 2, :].rearrange("p (a b) -> p a b", a=nh)
                empty(TT(s, ps[:, :].rearrange("p (a b) -> p a b", a=nh), bc(const(f"att{n}").unsqueeze(1), P, nh, w), add),
                      ("as", z))
                emptied(ve, ("as", z))
                m, m_ = mx[:, z % 2, 0:nh], mx[:, 2 + z % 2, 0:nh]
                link(ve.tensor_reduce(m_, s, AX.X, mx_))
                link(STT(out=m, in0=m_, scalar=-1.0, in1=nsinks[:, hd:hd + nh], op0=mul, op1=ALU.min))
                TT(dsk[:, z % 2, 0:nh], sinks[:, hd:hd + nh], m, add).then_inc(sem("sub_ready"), 1)

            def softmax_out(z):
                n, u, o, gh = UNITS[z]
                nh, w = (4, P) if n == 0 else (2, 2 * P)
                hd = 8 * u + 4 * o + 2 * gh
                ve.wait_ge(sem("sink_exp"), z + 1)
                ve.wait_ge(sem("exps"), sum(HEADS[:z + 1]))
                link(TT(den[:, z, 0:nh], den[:, z, 0:nh], dsk[:, z % 2, 0:nh], add))
                link(ve.reciprocal(den[:, z, 0:nh], den[:, z, 0:nh]))
                ps = full(ve, ("ao", z))
                rows_ = ao[:, n, 64 * hd:64 * hd + 64 * nh]
                dst = rows_.rearrange("p (a b) -> p a b", a=nh)
                empty(TT(dst, ps[:, 0:64 * nh].rearrange("p (a b) -> p a b", a=nh),
                         bc(den[:, z, 0:nh].unsqueeze(2), P, nh, 64), mul), ("ao", z))
                emptied(ve, ("ao", z), *[("ain", 2 + u, i) for i in range(2)])
                TT(rows_, rows_, ag[:, n, 64 * hd:64 * hd + 64 * nh], mul).then_inc(sem("ao_rows"), 1)

            softmax_in(0)
            emptied(ve, *[("ain", 1, i) for i in range(2)])
            norm_apply(heads(aq, 512, 8), 8, qn, 3)
            for z in range(len(UNITS)):
                if z + 1 < len(UNITS):
                    softmax_in(z + 1)
                softmax_out(z)
                if z == 0:
                    split_to("ain3.1")
                    query_rope(1)
                if z == 4:
                    lower_of(aoT, ("aoT", 0, 0), 0, 0)
                if z == 8:
                    lower_of(aoT, ("aoT", 1, 0), 0, 1)
                    split_to("ao1")
                if z == 10:
                    lower_of(aoT, ("aoT", 0, 1), 4, 0)
            lower_of(aoT, ("aoT", 1, 1), 4, 1)
            split_to("ao2")
            embedding_lower(1)
            split_to("ao3", 1)
            plain_join("fo")
            embed(1)


def kernel(**inputs):
    import concourse.bacc as bacc
    from concourse.bass_utils import run_bass_kernel_spmd as run

    nc = bacc.Bacc("TRN2", target_bir_lowering=False, num_devices=1)
    where, table = constants()
    arrays, io = {}, {}
    for name, a in list(inputs.items()) + [("table", table)]:
        a = np.ascontiguousarray(a)
        arrays[f"in_{name}"] = a
        io[name] = nc.dram_tensor(f"in_{name}", a.shape, mybir.dt.from_np(a.dtype), kind="ExternalInput").ap()
    out = nc.dram_tensor("out", (1, T, D), F32, kind="ExternalOutput").ap()
    build(nc, io, out, where, table.shape[1])
    r = run(nc, [arrays], core_ids=[0])
    return r.results[0]["out"]
```
